# Optimizing a Trainium2 kernel written in Bass

```python
import math
import jax, jax.numpy as jnp
from jax import lax
import numpy as np

D_MODEL = 1024
BATCH = 1
SEQ = 1024
DEPTH = 2

HEAD_DIM = 64
A_HEADS = 4
A_QK = 2 * HEAD_DIM
A_V = 2 * HEAD_DIM
A_WIDTH = A_HEADS * A_V
B_HEADS = 8
B_DIM = HEAD_DIM
B_WIDTH = B_HEADS * B_DIM
DILATED_BRANCHES = ((128, 1), (512, 4), (2048, 16))
ATTN_BLOCK = 128
EVEN_IN = 2 * A_HEADS * A_QK + A_WIDTH + 3 * B_WIDTH
C_HEADS = 4
C_DK = D_MODEL // 2 // C_HEADS
C_DV = D_MODEL // C_HEADS
C_GATE_RANK = 16
C_TAU = 16.0
C_CHUNK = 64
ODD_IN = 2 * C_HEADS * C_DK + 2 * C_HEADS * C_DV + C_GATE_RANK
FFN_HIDDEN = -(-8 * D_MODEL // (3 * 256)) * 256
N_EVEN = (DEPTH + 1) // 2
N_ODD = DEPTH // 2
EPS = 1e-6

kernel_name = "hybrid_diffattn_dilated_gla_block"

f32 = jnp.float32

def rmsnorm(x, g):
    x32 = x.astype(f32)
    y = x32 * lax.rsqrt(jnp.mean(x32 * x32, axis=-1, keepdims=True) + EPS) * g.astype(f32)
    return y.astype(x.dtype)

def alibi_slopes(n):
    return 2.0 ** (-8.0 * jnp.arange(1, n + 1, dtype=f32) / n)

def diff_attention(q, k, v, lam, lam_init, subln_g):
    Bn, S = q.shape[0], q.shape[1]
    nb = S // ATTN_BLOCK
    qf = (q.astype(f32) * HEAD_DIM ** -0.5).reshape(Bn, nb, ATTN_BLOCK, A_HEADS, 2, HEAD_DIM)
    qf = qf.transpose(1, 0, 3, 4, 2, 5)
    kf = k.astype(f32).transpose(0, 2, 3, 1, 4)
    vf = v.astype(f32).transpose(0, 2, 1, 3)
    slopes = alibi_slopes(A_HEADS)
    kpos = jnp.arange(S)

    def block(args):
        qb, n = args
        qpos = n * ATTN_BLOCK + jnp.arange(ATTN_BLOCK)
        dist = qpos[:, None] - kpos[None, :]
        causal = dist >= 0
        s = jnp.einsum('bhcqd,bhckd->bhcqk', qb, kf)
        s = jnp.where(causal, s - (slopes[:, None, None] * dist.astype(f32))[None, :, None], -jnp.inf)
        p = jax.nn.softmax(s, axis=-1)
        w = p[:, :, 0] - lam * p[:, :, 1]
        return jnp.einsum('bhqk,bhkv->bhqv', w, vf)

    o = lax.map(block, (qf, jnp.arange(nb)))
    o = rmsnorm(o, subln_g) * (1.0 - lam_init)
    return o.transpose(1, 0, 3, 2, 4).reshape(Bn, S, A_WIDTH)

def dilated_branch(q, k, v, window, dilation, slopes):
    Bn, S, H, dh = q.shape
    L = S // dilation
    steps = window // dilation
    nb = -(-L // ATTN_BLOCK)
    Lp = nb * ATTN_BLOCK

    def streams(t):
        t = t.reshape(Bn, L, dilation, H, dh).transpose(0, 2, 1, 3, 4)
        return jnp.pad(t, ((0, 0), (0, 0), (0, Lp - L), (0, 0), (0, 0)))

    def banded(t):
        tb = jnp.pad(t, ((0, 0), (0, 0), (ATTN_BLOCK, 0), (0, 0), (0, 0)))
        tb = tb.reshape(Bn, dilation, nb + 1, ATTN_BLOCK, H, dh)
        return jnp.concatenate([tb[:, :, :-1], tb[:, :, 1:]], axis=3)

    qb = streams(q).reshape(Bn, dilation, nb, ATTN_BLOCK, H, dh)
    kb = banded(streams(k))
    vb = banded(streams(v))
    a = jnp.arange(ATTN_BLOCK)
    bi = jnp.arange(2 * ATTN_BLOCK)
    rel = ATTN_BLOCK + a[:, None] - bi[None, :]
    kidx = (jnp.arange(nb) * ATTN_BLOCK)[:, None] - ATTN_BLOCK + bi[None, :]
    valid = ((rel >= 0) & (rel <= steps))[None] & (kidx >= 0)[:, None, :]
    dist = (rel * dilation).astype(f32)
    s = jnp.einsum('brnqhd,brnkhd->brnhqk', qb, kb)
    s = jnp.where(valid[None, None, :, None], s - slopes[:, None, None] * dist, -jnp.inf)
    lse = jax.nn.logsumexp(s, axis=-1)
    p = jnp.exp(s - lse[..., None])
    o = jnp.einsum('brnhqk,brnkhd->brnqhd', p, vb)
    o = o.reshape(Bn, dilation, Lp, H, dh)[:, :, :L].transpose(0, 2, 1, 3, 4).reshape(Bn, S, H, dh)
    lse = lse.transpose(0, 1, 2, 4, 3).reshape(Bn, dilation, Lp, H)[:, :, :L]
    lse = lse.transpose(0, 2, 1, 3).reshape(Bn, S, H)
    return o, lse

def dilated_attention(q, k, v):
    qf = q.astype(f32) * B_DIM ** -0.5
    kf = k.astype(f32)
    vf = v.astype(f32)
    slopes = alibi_slopes(B_HEADS)
    outs, lses = [], []
    for window, dilation in DILATED_BRANCHES:
        o, l = dilated_branch(qf, kf, vf, window, dilation, slopes)
        outs.append(o)
        lses.append(l)
    wts = jax.nn.softmax(jnp.stack(lses, 0), axis=0)
    o = jnp.einsum('nbsh,nbshd->bshd', wts, jnp.stack(outs, 0))
    return o.reshape(q.shape[0], q.shape[1], B_WIDTH)

def even_mixer(h, w_in, lam_p, subln_g, w_out, layer_idx):
    Bn, S, _ = h.shape
    proj = h @ w_in
    o1 = A_HEADS * A_QK
    o2 = 2 * o1
    o3 = o2 + A_WIDTH
    qa = proj[..., :o1].reshape(Bn, S, A_HEADS, 2, HEAD_DIM)
    ka = proj[..., o1:o2].reshape(Bn, S, A_HEADS, 2, HEAD_DIM)
    va = proj[..., o2:o3].reshape(Bn, S, A_HEADS, A_V)
    qb = proj[..., o3:o3 + B_WIDTH].reshape(Bn, S, B_HEADS, B_DIM)
    kb = proj[..., o3 + B_WIDTH:o3 + 2 * B_WIDTH].reshape(Bn, S, B_HEADS, B_DIM)
    vb = proj[..., o3 + 2 * B_WIDTH:].reshape(Bn, S, B_HEADS, B_DIM)
    lam_init = 0.8 - 0.6 * math.exp(-0.3 * layer_idx)
    lp = lam_p.astype(f32)
    lam = jnp.exp(jnp.sum(lp[0] * lp[1])) - jnp.exp(jnp.sum(lp[2] * lp[3])) + lam_init
    ya = diff_attention(qa, ka, va, lam, lam_init, subln_g)
    yb = dilated_attention(qb, kb, vb)
    y = jnp.concatenate([ya, yb], axis=-1).astype(h.dtype)
    return y @ w_out

def gla(q, k, v, log_a):
    Bn, S, H, dk = q.shape
    dv = v.shape[-1]
    N = S // C_CHUNK

    def chunks(t):
        return t.reshape(Bn, N, C_CHUNK, H, t.shape[-1]).transpose(1, 0, 3, 2, 4)

    causal = jnp.tril(jnp.ones((C_CHUNK, C_CHUNK), bool))[:, :, None]

    def step(state, inp):
        qc, kc, vc, gc = inp
        b = jnp.cumsum(gc, axis=-2)
        diff = b[:, :, :, None, :] - b[:, :, None, :, :]
        decay = jnp.where(causal, jnp.exp(jnp.where(causal, diff, 0.0)), 0.0)
        attn = jnp.einsum('bhijk,bhjk->bhij', qc[:, :, :, None, :] * decay, kc)
        o = jnp.einsum('bhij,bhjv->bhiv', attn, vc) + jnp.einsum('bhik,bhkv->bhiv', qc * jnp.exp(b), state)
        b_last = b[:, :, -1:, :]
        state = jnp.exp(b_last[:, :, 0, :, None]) * state + jnp.einsum('bhjk,bhjv->bhkv', kc * jnp.exp(b_last - b), vc)
        return state, o

    s0 = jnp.zeros((Bn, H, dk, dv), f32)
    _, o = lax.scan(step, s0, (chunks(q), chunks(k), chunks(v), chunks(log_a)))
    return o.transpose(1, 0, 3, 2, 4).reshape(Bn, S, H, dv)

def odd_mixer(h, w_in, w_g2, b_g2, head_g, w_out):
    Bn, S, _ = h.shape
    proj = (h @ w_in).astype(f32)
    nk = C_HEADS * C_DK
    nv = C_HEADS * C_DV
    q = proj[..., :nk].reshape(Bn, S, C_HEADS, C_DK) * C_DK ** -0.5
    k = proj[..., nk:2 * nk].reshape(Bn, S, C_HEADS, C_DK)
    v = proj[..., 2 * nk:2 * nk + nv].reshape(Bn, S, C_HEADS, C_DV)
    r = proj[..., 2 * nk + nv:2 * nk + 2 * nv]
    glr = proj[..., 2 * nk + 2 * nv:]
    log_a = jax.nn.log_sigmoid(glr @ w_g2.astype(f32) + b_g2.astype(f32)) / C_TAU
    log_a = log_a.reshape(Bn, S, C_HEADS, C_DK)
    o = gla(q, k, v, log_a)
    o = rmsnorm(o, head_g).reshape(Bn, S, nv) * jax.nn.silu(r)
    return o.astype(h.dtype) @ w_out

def swiglu(h, w_gate, w_up, w_down):
    return (jax.nn.silu(h @ w_gate) * (h @ w_up)) @ w_down

def setup_inputs(seed: int = 0) -> dict:
    key = jax.random.key(seed)
    ks = jax.random.split(key, 20)

    def w(k, shape, fan_in, gain=1.0):
        return jax.random.normal(k, shape, f32) * (gain * fan_in ** -0.5)

    return {
        "x": jax.random.normal(ks[0], (BATCH, SEQ, D_MODEL), f32),
        "c": jax.random.normal(ks[1], (BATCH, D_MODEL), f32),
        "ada_w": w(ks[2], (DEPTH, D_MODEL, 6 * D_MODEL), D_MODEL, 0.5),
        "ada_b": 0.01 * jax.random.normal(ks[3], (DEPTH, 6 * D_MODEL), f32),
        "norm_g": 1.0 + 0.02 * jax.random.normal(ks[4], (DEPTH, 4, D_MODEL), f32),
        "ev_w_in": w(ks[5], (N_EVEN, D_MODEL, EVEN_IN), D_MODEL),
        "ev_lambda": 0.1 * jax.random.normal(ks[6], (N_EVEN, 4, HEAD_DIM), f32),
        "ev_subln_g": 1.0 + 0.02 * jax.random.normal(ks[7], (N_EVEN, A_V), f32),
        "ev_w_out": w(ks[8], (N_EVEN, A_WIDTH + B_WIDTH, D_MODEL), A_WIDTH + B_WIDTH),
        "od_w_in": w(ks[9], (N_ODD, D_MODEL, ODD_IN), D_MODEL),
        "od_w_g2": w(ks[10], (N_ODD, C_GATE_RANK, C_HEADS * C_DK), C_GATE_RANK),
        "od_b_g2": 0.1 * jax.random.normal(ks[11], (N_ODD, C_HEADS * C_DK), f32),
        "od_head_g": 1.0 + 0.02 * jax.random.normal(ks[12], (N_ODD, C_DV), f32),
        "od_w_out": w(ks[13], (N_ODD, C_HEADS * C_DV, D_MODEL), C_HEADS * C_DV),
        "ffn_w_gate": w(ks[14], (DEPTH, D_MODEL, FFN_HIDDEN), D_MODEL),
        "ffn_w_up": w(ks[15], (DEPTH, D_MODEL, FFN_HIDDEN), D_MODEL),
        "ffn_w_down": w(ks[16], (DEPTH, FFN_HIDDEN, D_MODEL), FFN_HIDDEN),
    }

def reference(x, c, ada_w, ada_b, norm_g, ev_w_in, ev_lambda, ev_subln_g, ev_w_out,
              od_w_in, od_w_g2, od_b_g2, od_head_g, od_w_out, ffn_w_gate, ffn_w_up, ffn_w_down):
    for l in range(DEPTH):
        mod = (jax.nn.silu(c) @ ada_w[l] + ada_b[l])[:, None, :]
        sh1, sc1, g1, sh2, sc2, g2 = jnp.split(mod, 6, axis=-1)
        h = rmsnorm(x, norm_g[l, 0]) * (1 + sc1) + sh1
        if l % 2 == 0:
            e = l // 2
            y = even_mixer(h, ev_w_in[e], ev_lambda[e], ev_subln_g[e], ev_w_out[e], l)
        else:
            o = l // 2
            y = odd_mixer(h, od_w_in[o], od_w_g2[o], od_b_g2[o], od_head_g[o], od_w_out[o])
        x = x + (1 + g1) * rmsnorm(y, norm_g[l, 1])
        h = rmsnorm(x, norm_g[l, 2]) * (1 + sc2) + sh2
        y = swiglu(h, ffn_w_gate[l], ffn_w_up[l], ffn_w_down[l])
        x = x + (1 + g2) * rmsnorm(y, norm_g[l, 3])
    return x


_drawn_inputs = setup_inputs


def setup_inputs(seed=0):
    import zlib

    import numpy as np

    out = dict(_drawn_inputs(seed))
    spreads = {}
    factors = {}
    for name, (base, spread) in spreads.items():
        noise = np.random.default_rng([zlib.crc32(name.encode()), seed]).standard_normal(out[name].shape)
        drawn = base * np.exp(spread * noise) if base else spread * noise
        out[name] = __import__('jax').numpy.asarray(drawn.astype(out[name].dtype))
    for name, factor in factors.items():
        out[name] = (out[name] * factor).astype(out[name].dtype)
    return out
```

```python
from contextlib import ExitStack
import math

import numpy as np

import concourse.bass as bass
from concourse import mybir

D = 1024
S = 1024
P = 128
KB = D // P
HALF = S // 2
A_HEADS, B_HEADS, HEAD_DIM = 4, 8, 64
C_HEADS, C_DK, C_DV, C_RANK, C_TAU = 4, 128, 256, 16, 16.0
FFN = 2816
FB = FFN // P
NIN = [24, 25]
EPS = 1e-6
SCORE_SCALE = HEAD_DIM ** -0.5
LAM_INIT = 0.8 - 0.6 * math.exp(-0.3 * 0)
LEVELS = 7
MASKED = -1e30

FFN_UNITS = 3 * FB
PACK_IN = [0, NIN[0] + KB + FFN_UNITS]
PACK_OUT = [PACK_IN[0] + NIN[0], PACK_IN[1] + NIN[1]]
PACK_FFN = [PACK_OUT[0] + KB, PACK_OUT[1] + KB]
PACK_UNITS = PACK_FFN[1] + FFN_UNITS
USE_IN, USE_OUT, USE_FFN = [0, 0], [0, 0], [0, 0]
USE_OUT[0] = 2 * NIN[0]
USE_FFN[0] = USE_OUT[0] + 2 * KB
USE_IN[1] = USE_FFN[0] + 2 * FFN_UNITS
USE_OUT[1] = USE_IN[1] + 2 * NIN[1]
USE_FFN[1] = USE_OUT[1] + 2 * KB
PAIRS_IN, PAIRS_OUT = 12, KB // 2
T_IN = [0, 2 * PAIRS_IN + 2 * PAIRS_OUT + 2 * FB]
T_OUT = [T_IN[0] + 2 * PAIRS_IN, T_IN[1] + 2 * PAIRS_IN]
T_FFN = [T_OUT[0] + 2 * PAIRS_OUT, T_OUT[1] + 2 * PAIRS_OUT]


def trunk_kernel(nc, xT, cT, weights, ada_w, ada_bT, norm_gT, lam_p, subln_g, w_g2, b_g2, head_g,
                 identity, distance, causal_bias, dilated_bias, level_masks, outT):
    f32, f32r, u8 = mybir.dt.float32, mybir.dt.float32r, mybir.dt.uint8
    ALU, ACT, AX = mybir.AluOpType, mybir.ActivationFunctionType, mybir.AxisListType

    ctx = ExitStack()
    with ctx:
        def sb(name, shape, dt=f32):
            return ctx.enter_context(nc.sbuf_tensor(name, shape, dt))

        def sem(name):
            return ctx.enter_context(nc.semaphore(name))

        proj = nc.dram_tensor("proj", [24, P, S], f32, kind="Internal").ap()
        x = sb("x", [P, KB, S])
        h_hi = sb("h_hi", [P, KB, HALF], f32r)
        h_lo = sb("h_lo", [P, KB, HALF], f32r)
        w_raw = sb("w_raw", [P, 2, 1024])
        w_hi = sb("w_hi", [P, 2, 1024], f32r)
        w_lo = sb("w_lo", [P, 2, 1024], f32r)
        a_hi = sb("a_hi", [P, 2, HALF], f32r)
        a_lo = sb("a_lo", [P, 2, HALF], f32r)
        ybuf = sb("ybuf", [P, 8 * HALF])
        arena = sb("arena", [P, 20736])
        glr = sb("glr", [P, S])
        rinv = sb("rinv", [P, 3, HALF])
        ident = sb("ident", [P, P])
        mean_w = sb("mean_w", [P, P])
        ones = sb("ones", [P, P])
        masks = sb("masks", [P, 8, P], u8)
        wg2 = sb("wg2", [P, P])
        bg2 = sb("bg2", [P, 1])
        cs = sb("cs", [P, KB])
        ada_b = sb("ada_b", [P, 96])
        mod = sb("mod", [P, 96])
        ng = sb("ng", [P, 64])
        gain = sb("gain", [P, 64])
        small = sb("small", [P, 128])
        ps = ctx.enter_context(nc.psum_tensor("ps", [P, 4096], f32))

        def bank(b, n=512):
            return ps[:, b * 512:b * 512 + n]

        lamv = ybuf[:, 0:256]
        y3 = ybuf[:, :].rearrange("p (k t) -> p k t", k=KB)
        yT = arena[:, 0:8192].rearrange("p (k t) -> p k t", k=KB)
        act = arena[:, 0:FB * HALF].rearrange("p (k t) -> p k t", k=FB)
        silu_g = arena[:, FB * HALF:FB * HALF + HALF]
        sq = arena[:, 11776:15872].rearrange("p (k t) -> p k t", k=KB)
        stage = arena[:, 0:1024].rearrange("p (s t) -> p s t", s=2)
        ada_raw = arena[:, 1024:3072].rearrange("p (s n) -> p s n", s=2)
        ada_acc = arena[:, 3072:6144].rearrange("p (g n) -> p g n", g=3)
        q_dup = arena[:, 8192:10240].rearrange("p (c t) -> p c t", c=2)
        k_dup = arena[:, 10240:12288].rearrange("p (c t) -> p c t", c=2)
        hf, lf = (t[:, :, :].rearrange("p k t -> p (k t)") for t in (h_hi, h_lo))
        wf, wg = (t[:, :, :].rearrange("p k t -> p (k t)") for t in (w_hi, w_lo))
        two = lambda t: t.rearrange("p (c t) -> p c t", c=2)
        q_split = [two(hf[:, 0:2048]), two(lf[:, 2048:4096])]
        k_high = [two(hf[:, 2048:4096]), two(wf)]
        k_low = [two(lf[:, 0:2048]), two(wg)]
        v_sb = arena[:, 12288:13312]
        v_tok = arena[:, 13312:14336].rearrange("p (n d) -> p n d", d=P)
        wT = arena[:, 14336:16384].rearrange("p (c k q) -> p c k q", c=2, q=P)
        dist = arena[:, 16384:17408]
        mask_bias = arena[:, 17408:18432]
        bias = arena[:, 18432:20480].rearrange("p (c k) -> p c k", c=2)
        sc = ybuf[:, 0:2048].rearrange("p (c k) -> p c k", c=2)
        pr = ybuf[:, 2048:4096].rearrange("p (c k) -> p c k", c=2)
        o_sb = glr[:, :].rearrange("p (n d) -> p n d", d=P)
        gq = arena[:, 8192:9216]
        gk = arena[:, 9216:10240]
        gvr = arena[:, 10240:12288].rearrange("p (b t) -> p b t", b=2)
        gb = arena[:, 12288:13312]
        gd = arena[:, 13312:14336]
        gx = arena[:, 14336:16384].rearrange("p (s t) -> p s t", s=2)
        attnT = arena[:, 16384:17408].rearrange("p (n i) -> p n i", i=P)
        qe = arena[:, 17408:18432]
        ke = arena[:, 18432:19456]
        ke_tok = arena[:, 19456:20480].rearrange("p (n d) -> p n d", d=P)
        state = arena[:, 20480:20736]
        gv_tok = ybuf[:, 0:2048].rearrange("p (n d) -> p n d", d=C_DV)
        go = ybuf[:, 2048:4096].rearrange("p (n d) -> p n d", d=C_DV)
        mx, nmx, rs = small[:, 0:16], small[:, 16:32], small[:, 32:48]
        r0, ms = small[:, 48:64], small[:, 64:72]
        coef, neglam = small[:, 72:73], small[:, 73:74]
        slope = small[:, 74:76]
        lam2 = small[:, 76:78]
        eps_c = small[:, 78:79]
        sub_g = small[:, 79:80]
        hg = small[:, 80:82]
        eblast = small[:, 82:90]
        r1 = small[:, 90:92]

        s_const, s_x = sem("consts_loaded"), sem("x_loaded")
        raw_full = [sem("raw_full0"), sem("raw_full1")]
        hi_done, lo_done = sem("w_hi_done"), sem("w_lo_done")
        unit_used = sem("unit_used")
        free0, free1 = sem("bank0_free"), sem("bank1_free")
        exp_g = sem("exp_gate_done")
        st_done = sem("proj_stored")
        ah_done, al_done = sem("a_hi_done"), sem("a_lo_done")
        dn_done, dn_ev0, dn_ev1 = sem("down_done"), sem("down_read_act"), sem("down_read_dve")
        xn_done, hh_done, hl_done = sem("xn_done"), sem("h_hi_done"), sem("h_lo_done")
        sq_done, ssum_done, mean_done = sem("square_done"), sem("square_summed"), sem("mean_done")
        root_done, rinv_done, x_upd = sem("root_done"), sem("rinv_done"), sem("x_updated")
        ada_full = [sem("ada_full0"), sem("ada_full1")]
        ada_used, acc_done, ada_mm, mod_done = sem("ada_used"), sem("ada_summed"), sem("ada_mm"), sem("mod_done")
        cs_done, setup_done, lam_dot, lam_exp = sem("silu_c_done"), sem("setup_done"), sem("lam_dot"), sem("lam_exp")
        glr_mm, glr_done = sem("gate_rank_mm"), sem("gate_rank_done")
        outs = sem("out_stored")
        tab_full = sem("bias_tables")
        qk_full, qk_hi, qk_lo = sem("qk_full"), sem("qk_high"), sem("qk_low")
        v_full, v_read = sem("v_full"), sem("v_read")
        s_done = [sem("scores0"), sem("scores1")]
        s_read = [sem("scores_read0"), sem("scores_read1")]
        nm_done, exp_done, w_done = sem("neg_max"), sem("exp_done"), sem("weights_done")
        ta_done, ta_free = sem("turned_a"), sem("turned_a_read")
        td_done, td_free = sem("turned_d"), sem("turned_d_read")
        pv_done, o_done = sem("pv_done"), sem("o_read")
        sub_root, o_ready, blk_done = sem("sub_root"), sem("o_ready"), sem("block_done")
        g_qk, g_v, g_r, g_w = sem("g_qk"), sem("g_v"), sem("g_r"), sem("g_w")
        g_z, g_zread, g_sp, g_b = sem("g_z"), sem("g_zread"), sem("g_softplus"), sem("g_cumsum")
        g_eb, g_ekd, g_ek, g_qk_done = sem("g_exp_b"), sem("g_last_minus_b"), sem("g_exp_k"), sem("g_qe_ke")
        g_d, g_f, g_x, g_s, g_pred = sem("g_diff"), sem("g_factor"), sem("g_level"), sem("g_scores"), sem("g_masked")
        g_vt, g_vtr, g_kt, g_ktr = sem("g_v_turned"), sem("g_v_copied"), sem("g_k_turned"), sem("g_k_copied")
        g_o, g_or, g_u, g_st = sem("g_out"), sem("g_out_read"), sem("g_update"), sem("g_state")
        g_root, g_on, g_silu, g_ot, g_yt = sem("g_root"), sem("g_normed"), sem("g_silu_r"), sem("g_out_turned"), sem("g_y")

        waited = sem("wait_carried")

        block = ctx.enter_context(nc.Block())

        def h_job(layer, kind, half):
            return 6 * layer + 2 * kind + half

        def stat_job(layer, kind, half):
            order = {(0, 0): 0, (0, 1): 1, (1, 0): 2, (2, 0): 3, (1, 1): 4, (2, 1): 5,
                     (3, 0): 6, (4, 0): 7, (3, 1): 8}
            if (layer, kind, half) == (1, 0, 0):
                return 7
            if layer == 0:
                return order[(kind, half)]
            return 9 + {(0, 1): 0, (1, 0): 1, (2, 0): 2, (1, 1): 3, (2, 1): 4, (3, 0): 5, (3, 1): 6}[(kind, half)]

        def rinv_slot(kind, half):
            return half if kind in (0, 2) else 2

        def upd(layer, kind, half):
            return 4 * layer + (0 if kind == 1 else 2) + half + 1

        def in_base(layer, half):
            return USE_IN[layer] + half * NIN[layer]

        def ffn_base(layer, half):
            return USE_FFN[layer] + half * FFN_UNITS

        def dn_idx(layer, half):
            return 2 * layer + half

        LANE = [8, 14]

        def lanes(kind, n):
            if kind == 0:
                if n < 4:
                    return [(0, n % 2, 0, n + 1)]
                return [(0, 0, 0, 4), (0, 1, 4, n - 3)]
            out = []
            for c in (0, 1):
                for k0 in range(0, n + 1, 4):
                    out.append((c, c, k0, min(4, n + 1 - k0)))
            return out

        def lane_count(kind, n, lane):
            return 1 + sum(g[1] == lane for m in range(n) for g in lanes(kind, m))

        @block.sync
        def _(sp):
            sp.sem_inc(st_done, 16)
            sp.dma_start(cs[:, :], cT).then_inc(s_const, 16)
            sp.dma_start(ada_b[:, :], ada_bT).then_inc(s_const, 16)
            sp.dma_start(ng[:, :], norm_gT).then_inc(s_const, 16)
            sp.dma_start(ident[:, :], identity).then_inc(s_const, 16)
            sp.dma_start(lamv, lam_p).then_inc(s_const, 16)
            sp.dma_start(sub_g, subln_g).then_inc(s_const, 16)
            sp.dma_start(hg, head_g).then_inc(s_const, 16)
            sp.dma_start(ybuf[:, 1024:2048], level_masks.rearrange("p l i -> p (l i)")).then_inc(s_const, 16)
            for half in range(2):
                sp.dma_start(x[:, :, half * HALF:(half + 1) * HALF],
                             xT.rearrange("(k p) t -> p k t", p=P)[:, :, half * HALF:(half + 1) * HALF]).then_inc(s_x, 16)

            def ada_pair(pair):
                sp.wait_ge(ada_used, 2 * pair + 1)
                for s in range(2):
                    sp.dma_start(ada_raw[:, s, :], ada_w[bass.ds(2 * pair + s, 1)] .rearrange("u p n -> (u p) n")
                                 if not isinstance(pair, int) else ada_w[2 * pair + s]).then_inc(ada_full[s], 16)

            def unit(pack, use, s):
                sp.wait_ge(lo_done, use + 1)
                src = weights[pack] if isinstance(pack, int) else weights[bass.ds(pack, 1)].rearrange("u p n -> (u p) n")
                sp.dma_start(w_raw[:, s, :], src).then_inc(raw_full[s], 16)

            def stream(pack, use, pairs):
                with sp.Fori(0, pairs) as i:
                    for s in range(2):
                        unit(pack + 2 * i + s, use + 2 * i + s, (use + s) % 2)

            def project(layer, half):
                use, n_ada = in_base(layer, half), [[12, 12], [12, 4]][layer][half]
                ada0 = [[8, 20], [32, 44]][layer][half]
                done = PAIRS_IN * (2 * layer + half)

                def store(i):
                    sp.wait_ge(free0, T_IN[layer] + PAIRS_IN * half + i + 2)
                    sp.wait_ge(free1, T_IN[layer] + PAIRS_IN * half + i + 2)
                    dst = proj[2 * i:2 * i + 2] if isinstance(i, int) else proj[bass.ds(2 * i, 2)]
                    sp.dma_start(dst.rearrange("b p t -> p b t")[:, :, half * HALF:(half + 1) * HALF],
                                 stage[:, :, :]).then_inc(st_done, 16)

                def body(i, ada):
                    for s in range(2):
                        unit(PACK_IN[layer] + 2 * i + s, use + 2 * i + s, (use + s) % 2)
                    if ada:
                        ada_pair(ada0 + i)

                body(0, True)
                with sp.Fori(1, n_ada) as i:
                    body(i, True)
                    store(i - 1)
                if n_ada < PAIRS_IN:
                    with sp.Fori(n_ada, PAIRS_IN) as i:
                        body(i, False)
                        store(i - 1)
                if layer == 1:
                    unit(PACK_IN[1] + 24, use + 24, (use + 24) % 2)
                store(PAIRS_IN - 1)

            def attention():
                sp.wait_ge(st_done, 16 * 2 * PAIRS_IN + 16)
                sp.wait_ge(hl_done, 16)
                sp.wait_ge(mod_done, 3)
                sp.dma_start(dist, distance).then_inc(tab_full, 16)
                sp.dma_start(mask_bias, causal_bias).then_inc(tab_full, 16)

                def load(b, slot, kind, j):
                    rows = (0, 4, 8) if kind == 0 else (12, 16, 20)

                    def row(r):
                        i = rows[r] + j
                        return proj[i] if isinstance(i, int) else proj[bass.ds(i, 1)].rearrange("u p n -> (u p) n")
                    sp.wait_ge(qk_lo, 4 * b + 1)
                    for c in range(2):
                        for top in (0, 64):
                            sp.dma_start(q_dup[top:top + 64, c, :], row(0)[64 * c:64 * c + 64, :]).then_inc(qk_full, 16)
                            sp.dma_start(k_dup[top:top + 64, c, :], row(1)[64 * c:64 * c + 64, :]).then_inc(qk_full, 16)
                    sp.wait_ge(v_read, b + 1)
                    sp.dma_start(v_sb, row(2)).then_inc(v_full, 16)

                with sp.Fori(0, 2) as i:
                    for s in range(2):
                        load(2 * i + s, s, 0, 2 * i + s)
                load(4, 0, 1, 0)
                sp.dma_start(mask_bias, dilated_bias).then_inc(tab_full, 16)
                load(5, 1, 1, 1)
                load(6, 0, 1, 2)
                load(7, 1, 1, 3)

            def gated():
                sp.wait_ge(st_done, 16 * 4 * PAIRS_IN + 16)
                sp.wait_ge(hl_done, 8 * (h_job(1, 0, 1) + 1))
                sp.wait_ge(mod_done, 5)
                with sp.Fori(0, C_HEADS) as h:
                    def row(i, n=1):
                        return proj[bass.ds(i, n)].rearrange("u p n -> p u n")
                    sp.wait_ge(g_yt, 4 * h + 1)
                    sp.dma_start(wg2[0:C_RANK, :], w_g2[bass.ds(h, 1)].rearrange("u p n -> (u p) n")).then_inc(g_w, 16)
                    sp.dma_start(bg2[:, :], b_g2[bass.ds(h, 1)].rearrange("u p n -> (u p) n")).then_inc(g_w, 16)
                    sp.dma_start(gq, proj[bass.ds(h, 1)].rearrange("u p n -> (u p) n")).then_inc(g_qk, 16)
                    sp.dma_start(gk, proj[bass.ds(4 + h, 1)].rearrange("u p n -> (u p) n")).then_inc(g_qk, 16)
                    sp.dma_start(gvr[:, :, :], row(8 + 2 * h, 2)).then_inc(g_v, 16)
                    sp.wait_ge(g_vt, 4 * h + 4)
                    sp.dma_start(gvr[:, :, :], row(16 + 2 * h, 2)).then_inc(g_r, 16)

            with sp.Fori(0, 8) as pair:
                ada_pair(pair)
            for layer in range(2):
                for half in range(2):
                    project(layer, half)
                if layer == 0:
                    attention()
                else:
                    gated()
                for half in range(2):
                    stream(PACK_OUT[layer], USE_OUT[layer] + KB * half, KB // 2)
                for half in range(2):
                    use = ffn_base(layer, half)
                    stream(PACK_FFN[layer], use, FFN_UNITS // 2)
            for half in range(2):
                sp.wait_ge(x_upd, upd(1, 3, half))
                sp.dma_start(outT.rearrange("(k p) t -> p k t", p=P)[:, :, half * HALF:(half + 1) * HALF],
                             x[:, :, half * HALF:(half + 1) * HALF]).then_inc(outs, 16)
            sp.wait_ge(outs, 32)

        @block.gpsimd
        def _(pool):
            pool.sem_inc(lo_done, 2)

            def lo(use, s):
                pool.wait_ge(hi_done, use + 1)
                pool.tensor_tensor(w_lo[:, s, :], w_raw[:, s, :], w_hi[:, s, :].bitcast(f32),
                                   ALU.subtract).then_inc(lo_done, 1)

            def split_qk(b, s):
                for c in range(2):
                    pool.drain()
                    pool.wait_ge(qk_hi, 4 * b + 2 * c + 1)
                    pool.tensor_tensor(q_split[s][64:128, c, :], q_dup[64:128, c, :],
                                       q_split[s][64:128, c, :].bitcast(f32), ALU.subtract).then_inc(qk_lo, 1)
                    pool.drain()
                    pool.wait_ge(qk_hi, 4 * b + 2 * c + 2)
                    pool.tensor_tensor(k_low[s][:, c, :], k_dup[:, c, :],
                                       k_high[s][:, c, :].bitcast(f32), ALU.subtract).then_inc(qk_lo, 1)

            pool.sem_inc(qk_lo, 1)
            with pool.Fori(0, USE_OUT[0] // 2) as i:
                for s in range(2):
                    lo(2 * i + s, s)
            with pool.Fori(0, 4) as i:
                for s in range(2):
                    split_qk(2 * i + s, s)
            with pool.Fori(USE_OUT[0] // 2, (USE_FFN[1] + 2 * FFN_UNITS) // 2) as i:
                for s in range(2):
                    lo(2 * i + s, s)

        @block.tensor
        def _(pe):
            pe.sem_inc(unit_used, 2)
            pe.sem_inc(pv_done, 1)

            def passes(out, wsl, mh, ml, first, last):
                s, a, b = wsl
                pe.matmul(out, w_hi[:, s, a:b], mh, start=first, stop=False)
                pe.matmul(out, w_hi[:, s, a:b], ml, start=False, stop=False)
                return pe.matmul(out, w_lo[:, s, a:b], mh, start=False, stop=last)

            def unit(use, s, b):
                pe.wait_ge(lo_done, use + 3)
                for k in range(KB):
                    mm = passes(bank(b), (s, k * P, (k + 1) * P), h_hi[:, k, :], h_lo[:, k, :], k == 0, k == KB - 1)
                mm.then_inc(unit_used, 1)

            def pairs(use, tiles, n):
                with pe.Fori(0, n) as i:
                    for s in range(2):
                        pe.wait_ge((free0, free1)[s], tiles + i + 1)
                        unit(use + 2 * i + s, (use + s) % 2, s)

            def mean(layer, kind, half):
                n = stat_job(layer, kind, half)
                pe.wait_ge(ssum_done, n + 1)
                if n:
                    pe.wait_ge(root_done, n)
                pe.matmul(bank(7), mean_w[:, :], rinv[:, rinv_slot(kind, half), :], start=True, stop=True)\
                    .then_inc(mean_done, 1)

            def ada_turn(n, groups):
                pe.wait_ge(acc_done, n + 1)
                if n:
                    pe.wait_ge(mod_done, n)
                for g in range(groups):
                    for m in range(KB):
                        mm = pe.matmul(bank(6)[:, g * 8 + m:g * 8 + m + 1], ada_acc[:, g, m * P:(m + 1) * P],
                                       ones[:, 0:1], start=True, stop=True)
                mm.then_inc(ada_mm, 1)

            def attention_block(kind, b, slot):
                before = (lambda t: LANE[0] * b + t) if kind == 0 else (lambda t: LANE[0] * 4 + LANE[1] * (b - 4) + t)

                def turn_v():
                    pe.wait_ge(v_full, 16 * b + 16)
                    for lane in range(2):
                        pe.wait_ge((ta_free, td_free)[lane], before(0) + 1)
                        for n in range(4):
                            m = 4 * lane + n
                            mm = pe.transpose(bank(4 + lane)[:, n * P:(n + 1) * P], v_sb[:, m * P:(m + 1) * P], ident[:, :])
                        mm.then_inc((ta_done, td_done)[lane], 1)

                def scores(n):
                    for c in range(2):
                        pe.wait_ge(s_read[c], 8 * b + n + 1)
                        if n == 0:
                            pe.wait_ge(qk_lo, 4 * b + 2 * c + 3)
                        W = 256 * ((n + 2) // 2)
                        for k0 in range(0, W, 512):
                            w = min(512, W - k0)
                            for part in (k_high, k_low):
                                mm = pe.matmul(ps[:, c * 1024 + k0:c * 1024 + k0 + w],
                                               q_split[slot][:, c, n * P:(n + 1) * P], part[slot][:, c, k0:k0 + w],
                                               start=part is k_high, stop=part is k_low)
                        mm.then_inc(s_done[c], 1)

                def weigh(n):
                    count = [lane_count(kind, n, 0), lane_count(kind, n, 1)]
                    done = [(0, 0)] * 2
                    if kind == 0:
                        pe.wait_ge(w_done, 8 * b + n + 1 + 1)
                    for c, lane, k0, m in lanes(kind, n):
                        if kind == 1:
                            pe.wait_ge(exp_done, 16 * b + 2 * n + c + 1 + 1)
                        pe.wait_ge((ta_free, td_free)[lane], before(count[lane]) + 1)
                        for i in range(m):
                            mm = pe.transpose(bank(4 + lane)[:, i * P:(i + 1) * P],
                                              pr[:, c, (k0 + i) * P:(k0 + i + 1) * P], ident[:, :])
                        mm.then_inc((ta_done, td_done)[lane], 1)
                        count[lane] += 1
                    pe.wait_ge(ta_free, before(count[0]) + 1)
                    pe.wait_ge(td_free, before(count[1]) + 1)
                    pe.wait_ge(o_done, 8 * b + n + 1)
                    for c in range(1 if kind == 0 else 2):
                        for kb in range(n + 1):
                            mm = pe.matmul(bank(6)[:, c * P:(c + 1) * P], wT[:, c, kb, :], v_tok[:, kb, :],
                                           start=kb == 0, stop=kb == n)
                    mm.then_inc(pv_done, 1)

                def turn_out():
                    pe.wait_ge(o_ready, b + 1)
                    for lane in range(2):
                        pe.wait_ge((ta_free, td_free)[lane], before(LANE[kind] - 1) + 1)
                        for n in range(4):
                            mm = pe.transpose(bank(4 + lane)[:, n * P:(n + 1) * P], o_sb[:, 4 * lane + n, :], ident[:, :])
                        mm.then_inc((ta_done, td_done)[lane], 1)

                turn_v()
                scores(0)
                for n in range(8):
                    if n < 7:
                        scores(n + 1)
                    weigh(n)
                turn_out()

            def attention():
                pe.wait_ge(free0, T_OUT[0] + 1)
                pe.wait_ge(free1, T_OUT[0] + 1)
                for kind in range(2):
                    with pe.Fori(0, 2) as i:
                        for s in range(2):
                            attention_block(kind, 4 * kind + 2 * i + s, s)
                pe.wait_ge(ta_free, 4 * sum(LANE) + 1)
                pe.wait_ge(td_free, 4 * sum(LANE) + 1)

            def gated():
                pe.wait_ge(free0, T_OUT[1] + 1)
                pe.wait_ge(free1, T_OUT[1] + 1)
                pe.wait_ge(glr_done, 2)
                with pe.Fori(0, C_HEADS) as h:
                    pe.wait_ge(g_w, 32 * h + 32)
                    pe.wait_ge(g_yt, 4 * h + 1)
                    for n in range(2):
                        mm = pe.matmul(bank(n), wg2[:, :], glr[:, n * 512:(n + 1) * 512], start=True, stop=True)
                    mm.then_inc(g_z, 1)
                    pe.wait_ge(g_v, 16 * h + 16)
                    pe.wait_ge(g_or, 8 * h + 1)
                    pe.wait_ge(g_st, 8 * h + 1)
                    for n in range(4):
                        for i in range(2):
                            for b in range(2):
                                m = 2 * n + i
                                mm = pe.transpose(bank(4 + n)[:, i * 256 + b * P:i * 256 + (b + 1) * P],
                                                  gvr[:, b, m * P:(m + 1) * P], ident[:, :])
                        mm.then_inc(g_vt, 1)
                    pe.wait_ge(g_zread, 2 * h + 2)
                    for lv in range(LEVELS + 1):
                        pe.wait_ge(g_x, 8 * h + lv + 1)
                        pe.wait_ge(g_pred, 16 * h + 2 * max(0, lv - 1) + 1)
                        for n in range(8):
                            t = slice(n * P, (n + 1) * P)
                            a, b = (gx[:, lv % 2, t], gx[:, lv % 2, t]) if lv < LEVELS else (gk[:, t], gq[:, t])
                            mm = pe.matmul(bank(2 * (lv % 2) + n // 4)[:, (n % 4) * P:(n % 4 + 1) * P], a, b,
                                           start=True, stop=True)
                        mm.then_inc(g_s, 1)
                        if lv == 0:
                            pe.wait_ge(g_qk_done, 2 * h + 2)
                            for n in range(2):
                                pe.wait_ge(g_vtr, 4 * h + 4)
                                for i in range(4):
                                    m = 4 * n + i
                                    mm = pe.transpose(bank(4 + n)[:, i * P:(i + 1) * P], ke[:, m * P:(m + 1) * P], ident[:, :])
                                mm.then_inc(g_kt, 1)
                    pe.wait_ge(g_pred, 16 * h + 16 + 1)
                    pe.wait_ge(g_ktr, 2 * h + 2)
                    for n in range(8):
                        t = slice(n * P, (n + 1) * P)
                        if n < 7:
                            if n >= 2:
                                pe.wait_ge(g_st, 8 * h + n - 1 + 1)
                            pe.matmul(bank(6 + n % 2)[:, 0:C_DV], ke_tok[:, n, :], gv_tok[:, n, :], start=True, stop=True)\
                                .then_inc(g_u, 1)
                        if n >= 2:
                            pe.wait_ge(g_or, 8 * h + n - 1 + 1)
                        mm = pe.matmul(bank(4 + n % 2)[:, 0:C_DV], attnT[:, n, :], gv_tok[:, n, :], start=True, stop=n == 0)
                        if n:
                            pe.wait_ge(g_st, 8 * h + n + 1)
                            mm = pe.matmul(bank(4 + n % 2)[:, 0:C_DV], qe[:, t], state, start=False, stop=True)
                        mm.then_inc(g_o, 1)
                    pe.wait_ge(g_on, h + 1)
                    for b in range(2):
                        for n in range(2):
                            for i in range(4):
                                mm = pe.transpose(bank(2 * b + n)[:, i * P:(i + 1) * P],
                                                  go[:, 4 * n + i, b * P:(b + 1) * P], ident[:, :])
                            mm.then_inc(g_ot, 1)
                pe.wait_ge(g_yt, 4 * C_HEADS + 1)

            def down(layer, half):
                use, d = ffn_base(layer, half) + 2 * FB, dn_idx(layer, half)
                tiles = T_FFN[layer] + FB * (half + 1)
                pe.wait_ge(free0, tiles + 1)
                pe.wait_ge(free1, tiles + 1)
                pe.wait_ge(root_done, [[6, 8], [14, 15]][layer][half])

                def row(i, s, first, last):
                    pe.wait_ge(lo_done, use + 2 * i + s + 3)
                    pe.wait_ge(al_done, FB * d + 2 * i + s + 1)
                    slot = (use + s) % 2
                    for m in range(KB):
                        mm = passes(bank(m), (slot, m * P, (m + 1) * P), a_hi[:, s, :], a_lo[:, s, :], first, last)
                    mm.then_inc(unit_used, 1)

                row(0, 0, True, False)
                row(0, 1, False, False)
                with pe.Fori(1, FB // 2 - 1) as i:
                    for s in range(2):
                        row(i, s, False, False)
                row(FB // 2 - 1, 0, False, False)
                row(FB // 2 - 1, 1, False, True)
                pe.wait_ge(dn_ev0, 4 * (d + 1))
                pe.wait_ge(dn_ev1, 4 * (d + 1))

            pe.wait_ge(s_const, 128)
            pe.wait_ge(setup_done, 1)
            mean(0, 0, 0)
            mean(0, 0, 1)
            ada_turn(0, 2)
            for layer in range(2):
                if layer == 1:
                    mean(1, 0, 1)
                for half in range(2):
                    pe.wait_ge(hl_done, 8 * (h_job(layer, 0, half) + 1))
                    use = in_base(layer, half)
                    pairs(use, T_IN[layer] + PAIRS_IN * half, PAIRS_IN)
                    if layer == 1:
                        unit(use + 24, (use + 24) % 2, 2)
                        pe.matmul(bank(3)[:, 0:1], ident[:, :], ones[:, 0:1], start=True, stop=True).then_inc(glr_mm, 1)
                        pe.wait_ge(glr_done, half + 1)
                    ada_turn(1 + 2 * layer + half, [[3, 3], [3, 1]][layer][half])
                if layer == 0:
                    attention()
                else:
                    gated()
                for half in range(2):
                    pe.wait_ge(hl_done, 8 * (h_job(layer, 1, half) + 1))
                    pairs(USE_OUT[layer] + KB * half, T_OUT[layer] + PAIRS_OUT * half, PAIRS_OUT)
                    mean(layer, 1, half)
                    mean(layer, 2, half)
                for half in range(2):
                    pe.wait_ge(hl_done, 8 * (h_job(layer, 2, half) + 1))
                    pairs(ffn_base(layer, half), T_FFN[layer] + FB * half, FB)
                    down(layer, half)
                    mean(layer, 3, half)
                    if layer == 0 and half == 0:
                        mean(1, 0, 0)

        @block.scalar
        def _(a):
            for count in (free0, exp_done, ta_free, g_or):
                a.sem_inc(count, 1)

            def hi_at(base, i, s):
                slot = (base + s) % 2
                a.wait_ge(raw_full[slot], 16 * ((base + s) // 2 + i) + 16)
                a.wait_ge(unit_used, base + 2 * i + s + 1)
                a.activation(w_hi[:, slot, :], w_raw[:, slot, :], ACT.Copy).then_inc(hi_done, 1)

            def square(layer, kind, half):
                n = stat_job(layer, kind, half)
                if kind in (0, 2):
                    if layer == 0 and kind == 0:
                        a.wait_ge(s_x, 32)
                    else:
                        a.wait_ge(x_upd, upd(layer - (kind == 0), 3 if kind == 0 else 1, half))
                    src = x[:, :, half * HALF:(half + 1) * HALF]
                else:
                    src = y3
                    if kind == 3:
                        a.wait_ge(dn_ev1, 4 * (dn_idx(layer, half) + 1))
                    else:
                        a.wait_ge(free1, T_OUT[layer] + PAIRS_OUT * (half + 1) + 1)
                    a.drain()
                if n:
                    a.wait_ge(ssum_done, n)
                a.activation(sq[:, :, :], src, ACT.Square).then_inc(sq_done, 1)
                a.wait_ge(mean_done, n + 1)
                r = rinv[:, rinv_slot(kind, half), :]
                a.activation(r, bank(7), ACT.Sqrt, bias=eps_c).then_inc(root_done, 1)

            def modulate(layer, kind, half, k, first_unit):
                j = h_job(layer, kind, half)
                g = 8 * (4 * layer + (0 if kind == 0 else 2)) + k
                sh = 48 * layer + (0 if kind == 0 else 24) + k
                aj = 2 * (2 * layer + (kind == 2)) + half
                a.wait_ge(xn_done, 8 * aj + k + 1)
                if k == 0:
                    a.wait_ge(unit_used, first_unit + 2)
                a.activation(y3[:, k, :], y3[:, k, :], ACT.Identity, bias=mod[:, sh:sh + 1], scale=gain[:, g:g + 1])
                a.drain()
                a.activation(h_hi[:, k, :], y3[:, k, :], ACT.Copy).then_inc(hh_done, 1)

            def project(layer, half):
                base = in_base(layer, half)
                st = PAIRS_IN * (2 * layer + half)
                with a.Fori(0, PAIRS_IN) as i:
                    for s in range(2):
                        hi_at(base, i, s)
                    a.wait_ge(unit_used, base + 2 * i + 3)
                    a.wait_ge(st_done, 16 * (st + i) + 16)
                    a.activation(stage[:, 0, :], bank(0), ACT.Copy).then_inc(free0, 1)
                if layer == 1:
                    hi_at(base + 24, 0, 0)
                    a.wait_ge(glr_mm, half + 1)
                    a.activation(glr[:, half * HALF:(half + 1) * HALF], bank(2), ACT.Copy)\
                        .then_inc(glr_done, 1)

            def attention():
                a.wait_ge(lam_dot, 2)

                def split(b, slot, n, last=False):
                    if last:
                        return
                    a.wait_ge(qk_full, 128 * b + 128)
                    c = n // 2
                    dst, src = ((q_split, q_dup), (k_high, k_dup))[n % 2]
                    a.activation(dst[slot][:, c, :], src[:, c, :], ACT.Copy).then_inc(qk_hi, 1)

                def block_(kind, b, slot, last):
                    before = (lambda t: LANE[0] * b + t) if kind == 0 else (lambda t: LANE[0] * 4 + LANE[1] * (b - 4) + t)
                    count = 0

                    def copy_a(dst, m):
                        nonlocal count
                        count += 1
                        a.wait_ge(ta_done, before(count))
                        a.activation(dst, bank(4)[:, 0:m * P].rearrange("p (m q) -> p m q", q=P), ACT.Copy).then_inc(ta_free, 1)

                    def exps(n):
                        for c in range(2):
                            a.wait_ge(nm_done, 16 * b + 2 * n + c + 1)
                            if kind == 0:
                                a.wait_ge(w_done, 8 * b + n + 1)
                            K = P * (n + 1)
                            a.activation(pr[:, c, 0:K], sc[:, c, 0:K], ACT.Exp, bias=nmx[:, 2 * n + c:2 * n + c + 1],
                                         accum_out=rs[:, 2 * n + c:2 * n + c + 1]).then_inc(exp_done, 1)

                    a.wait_ge(pv_done, 8 * b + 1)
                    copy_a(v_tok[:, 0:4, :], 4)
                    exps(0)
                    for n in range(8):
                        for c, lane, k0, m in lanes(kind, n):
                            if lane == 0:
                                a.wait_ge(pv_done, 8 * b + n + 1)
                                copy_a(wT[:, c, k0:k0 + m, :], m)
                        a.wait_ge(td_done, before(lane_count(kind, n + 1, 1)))
                        if n < 7:
                            exps(n + 1)
                        if n < 4:
                            split(b + 1, 1 - slot, n, last)
                    if kind == 0:
                        a.wait_ge(o_done, 8 * b + 8 + 1)
                        a.activation(ms, ms, ACT.Sqrt, bias=eps_c, scale=1.0 / P).then_inc(sub_root, 1)
                    count += 1
                    a.wait_ge(ta_done, before(count))
                    dst = yT[:, b, 0:512] if isinstance(b, int) else yT[:, bass.ds(b, 1), 0:512].rearrange("p u t -> p (u t)")
                    a.activation(dst, bank(4), ACT.Copy if kind else ACT.Identity,
                                 **({} if kind else {"scale": sub_g})).then_inc(ta_free, 1)

                a.wait_ge(unit_used, USE_OUT[0] + 2)
                for n in range(4):
                    split(0, 0, n)
                with a.Fori(0, 2) as i:
                    for s in range(2):
                        block_(0, 2 * i + s, s, False)
                with a.Fori(0, 1) as i:
                    for s in range(2):
                        block_(1, 4 + 2 * i + s, s, False)
                block_(1, 6, 0, False)
                block_(1, 7, 1, True)

            def gated():
                with a.Fori(0, C_HEADS) as h:
                    a.wait_ge(g_z, h + 1)
                    a.activation(gd, ps[:, 0:1024], ACT.Abs, bias=bg2[:, :]).then_inc(g_zread, 1)
                    a.drain()
                    a.activation(gd, gd, ACT.Exp, scale=-1.0)
                    a.drain()
                    a.activation(gd, gd, ACT.Ln, bias=1.0).then_inc(g_sp, 1)
                    for n in range(4):
                        a.wait_ge(g_vt, 4 * h + n + 1)
                        a.activation(gv_tok[:, 2 * n:2 * n + 2, :], bank(4 + n).rearrange("p (i d) -> p i d", i=2), ACT.Copy)\
                            .then_inc(g_vtr, 1)
                    a.wait_ge(g_b, h + 1)
                    a.activation(qe, gb, ACT.Exp, scale=1.0 / C_TAU).then_inc(g_eb, 1)
                    a.activation(eblast, gb.rearrange("p (n t) -> p n t", t=P)[:, :, P - 1], ACT.Exp, scale=1.0 / C_TAU)\
                        .then_inc(g_eb, 1)
                    a.wait_ge(g_ekd, h + 1)
                    a.activation(ke, ke, ACT.Exp, scale=1.0 / C_TAU).then_inc(g_ek, 1)
                    for lv in range(LEVELS):
                        m = 64 >> lv
                        v = gd.rearrange("p (n u t) -> p n u t", u=2, t=m)
                        a.wait_ge(g_d, 7 * h + lv + 1)
                        a.activation(v[:, :, 0, :], v[:, :, 0, :], ACT.Exp, scale=-1.0 / C_TAU)
                        a.activation(v[:, :, 1, :], v[:, :, 1, :], ACT.Exp, scale=1.0 / C_TAU)
                        a.drain().then_inc(g_f, 1)
                        if lv == 0:
                            for n in range(2):
                                a.wait_ge(g_kt, 2 * h + n + 1)
                                a.activation(ke_tok[:, 4 * n:4 * n + 4, :], bank(4 + n).rearrange("p (i d) -> p i d", i=4), ACT.Copy)\
                                    .then_inc(g_ktr, 1)
                    for n in range(8):
                        a.wait_ge(g_o, 8 * h + n + 1)
                        a.activation(gd[:, 0:C_DV], bank(4 + n % 2)[:, 0:C_DV], ACT.Square, accum_out=ms[:, n:n + 1])
                        a.activation(go[:, n, :], bank(4 + n % 2)[:, 0:C_DV], ACT.Copy).then_inc(g_or, 1)
                        a.drain()
                    a.activation(ms, ms, ACT.Sqrt, bias=eps_c, scale=1.0 / C_DV).then_inc(g_root, 1)
                    a.wait_ge(g_r, 16 * h + 16)
                    a.activation(gvr[:, :, :], gvr[:, :, :], ACT.Silu).then_inc(g_silu, 1)

            a.wait_ge(s_const, 128)
            a.activation(cs[:, :], cs[:, :], ACT.Silu).then_inc(cs_done, 1)
            a.wait_ge(setup_done, 1)
            a.wait_ge(lam_dot, 1)
            a.activation(lam2, lam2, ACT.Exp).then_inc(lam_exp, 1)
            square(0, 0, 0)
            square(0, 0, 1)
            a.wait_ge(mod_done, 1)
            for k in range(KB):
                modulate(0, 0, 0, k, 0)
            for layer in range(2):
                if layer == 1:
                    square(1, 0, 1)
                project(layer, 0)
                for k in range(KB):
                    modulate(layer, 0, 1, k, in_base(layer, 1))
                project(layer, 1)
                if layer == 0:
                    attention()
                else:
                    gated()
                for half in range(2):
                    base = USE_OUT[layer] + KB * half
                    if layer == 0:
                        a.wait_ge(ta_free, 4 * sum(LANE) + 1)
                        a.wait_ge(td_free, 4 * sum(LANE) + 1)
                    else:
                        a.wait_ge(g_yt, 4 * C_HEADS + 1)
                    a.wait_ge(unit_used, base + 2)
                    for k in range(KB):
                        a.activation(h_hi[:, k, :], yT[:, k, half * HALF:(half + 1) * HALF], ACT.Copy).then_inc(hh_done, 1)
                    if half:
                        a.wait_ge(x_upd, upd(layer, 1, 0))
                    for i in range(PAIRS_OUT):
                        for s in range(2):
                            hi_at(base, i, s)
                        a.wait_ge(unit_used, base + 2 * i + 3)
                        a.activation(y3[:, 2 * i, :], bank(0), ACT.Copy).then_inc(free0, 1)
                    square(layer, 1, half)
                    square(layer, 2, half)
                for k in range(KB):
                    modulate(layer, 2, 0, k, ffn_base(layer, 0))
                for half in range(2):
                    base, tiles = ffn_base(layer, half), T_FFN[layer] + FB * half
                    with a.Fori(0, FB) as i:
                        for s in range(2):
                            hi_at(base, i, s)
                        a.wait_ge(unit_used, base + 2 * i + 3)
                        a.wait_ge(free1, tiles + i + 1)
                        a.activation(silu_g, bank(0), ACT.Exp, scale=-1.0).then_inc(exp_g, 1)
                    d = dn_idx(layer, half)
                    base += 2 * FB
                    for u in range(FB):
                        hi_at(base, u // 2, u % 2)
                        if u == 0:
                            a.wait_ge(free1, tiles + FB + 1)
                        a.activation(a_hi[:, u % 2, :], act[:, u, :], ACT.Copy).then_inc(ah_done, 1)
                        if u % 2 and 1 < u < 18 and (layer, half) != (1, 1):
                            nl, nk, nh = (layer, 2, 1) if half == 0 else (1, 0, 0)
                            modulate(nl, nk, nh, (u - 3) // 2, ffn_base(layer, half) + 2 * FB)
                    a.wait_ge(unit_used, base + FB + 2)
                    if (layer, half) != (1, 1):
                        nl, nk, nh = (layer, 2, 1) if half == 0 else (1, 0, 0)
                        a.wait_ge(hl_done, 8 * (h_job(nl, nk, nh) + 1))
                    for m in range(0, KB, 2):
                        a.activation(y3[:, m, :], bank(m), ACT.Copy).then_inc(dn_ev0, 1)
                    square(layer, 3, half)
                    if layer == 0 and half == 0:
                        square(1, 0, 0)

        @block.vector
        def _(v):
            for count in (free1, s_read[0], s_read[1], td_free, o_done, v_read, blk_done, w_done, g_st, g_yt, g_pred,
                          ada_used):
                v.sem_inc(count, 1)

            def rsum(layer, kind, half):
                n = stat_job(layer, kind, half)
                r = rinv[:, rinv_slot(kind, half), :]
                v.wait_ge(sq_done, n + 1)
                v.tensor_reduce(r, sq.rearrange("p k t -> p t k"), axis=AX.X, op=ALU.add).then_inc(ssum_done, 1)
                v.wait_ge(root_done, n + 1)
                v.reciprocal(r, r).then_inc(rinv_done, 1)
                v.drain()

            def xn(layer, kind, half, k):
                v.tensor_tensor(y3[:, k, :], x[:, k, half * HALF:(half + 1) * HALF], rinv[:, half, :], ALU.mult)\
                    .then_inc(xn_done, 1)

            def h_low(job, k, src):
                v.wait_ge(hh_done, 8 * job + k + 1)
                v.tensor_tensor(h_lo[:, k, :], src, h_hi[:, k, :].bitcast(f32), ALU.subtract).then_inc(hl_done, 1)

            def fill(layer, kind, half):
                for k in range(KB):
                    xn(layer, kind, half, k)
                    if k:
                        h_low(h_job(layer, kind, half), k - 1, y3[:, k - 1, :])
                h_low(h_job(layer, kind, half), KB - 1, y3[:, KB - 1, :])

            def update(layer, kind, half):
                g = 8 * (4 * layer + kind)
                v.tensor_tensor(y3, y3, bcast_k(rinv[:, 2, :]), ALU.mult)
                v.drain()
                for k in range(KB):
                    xs = x[:, k, half * HALF:(half + 1) * HALF]
                    op = v.scalar_tensor_tensor(xs, y3[:, k, :], gain[:, g + k:g + k + 1], xs, ALU.mult, ALU.add)
                v.drain().then_inc(x_upd, 1)

            def bcast_k(row):
                return row.rearrange("p (u t) -> p u t", u=1).broadcast_to([P, KB, HALF])

            def ada_unit(g, k, s, pair):
                v.wait_ge(ada_full[s], 16 * pair + 16)
                v.scalar_tensor_tensor(ada_acc_at(g), ada_raw[:, s, :], cs[:, k:k + 1], ada_acc_at(g),
                                       ALU.mult, ALU.add).then_inc(ada_used, 1)
                v.drain()

            def ada_acc_at(g):
                if isinstance(g, int):
                    return ada_acc[:, g, :]
                return ada_acc[:, bass.ds(g, 1), :].rearrange("p u n -> p (u n)")

            def columns(n, first, groups):
                v.drain().then_inc(acc_done, 1)
                v.wait_ge(ada_mm, n + 1)
                w = 8 * groups
                v.tensor_tensor(mod[:, 8 * first:8 * first + w], bank(6, w), ada_b[:, 8 * first:8 * first + w], ALU.add)
                v.drain()
                for grp in range(first, first + groups):
                    layer, g = divmod(grp, 6)
                    if g in (1, 2, 4, 5):
                        o = 8 * (4 * layer + {1: 0, 2: 1, 4: 2, 5: 3}[g])
                        v.scalar_tensor_tensor(gain[:, o:o + 8], mod[:, 8 * grp:8 * grp + 8], 1.0, ng[:, o:o + 8],
                                               ALU.add, ALU.mult)
                v.drain().then_inc(mod_done, 1)

            def project(layer, half):
                base, tiles = in_base(layer, half), T_IN[layer] + PAIRS_IN * half
                st = PAIRS_IN * (2 * layer + half)
                ada0 = [[8, 20], [32, 44]][layer][half]
                groups = [[3, 3], [3, 1]][layer][half]
                v.memset(ada_acc[:, 0:groups, :], 0.0)
                v.drain()

                def tile(i):
                    v.wait_ge(unit_used, base + 2 * i + 4)
                    v.wait_ge(st_done, 16 * (st + i) + 16)
                    v.tensor_copy(stage[:, 1, :], bank(1)).then_inc(free1, 1)

                with v.Fori(0, groups) as g:
                    for j in range(4):
                        for s in range(2):
                            ada_unit(g, 2 * j + s, s, ada0 + 4 * g + j)
                        tile(4 * g + j)
                if groups < 3:
                    with v.Fori(4 * groups, PAIRS_IN) as i:
                        tile(i)
                columns(1 + 2 * layer + half, ada0 // 4, groups)

            def attention():
                v.memset(slope[:, 0:1], 1.0)
                v.drain()
                v.wait_ge(tab_full, 32)

                def block_(kind, b):
                    before = (lambda t: LANE[0] * b + t) if kind == 0 else (lambda t: LANE[0] * 4 + LANE[1] * (b - 4) + t)
                    count = 0

                    def copy_d(dst, m):
                        nonlocal count
                        count += 1
                        v.wait_ge(td_done, before(count))
                        v.tensor_copy(dst, bank(5)[:, 0:m * P].rearrange("p (m q) -> p m q", q=P)).then_inc(td_free, 1)

                    def biased(n):
                        for c in range(2):
                            K = P * (n + 1)
                            col = 2 * n + c
                            v.wait_ge(s_done[c], 8 * b + n + 1)
                            v.wait_ge(exp_done, 16 * b + max(0, 2 * n - 1 + c) + 1)
                            v.sem_inc(waited, 1)
                            v.tensor_tensor_reduce(out=sc[:, c, 0:K], in0=ps[:, c * 1024:c * 1024 + K],
                                                   in1=bias[:, c if kind else 0, 1024 - K:1024], scale=SCORE_SCALE,
                                                   scalar=-3.0e38, op0=ALU.add, op1=ALU.max,
                                                   accum_out=mx[:, col:col + 1]).then_inc(s_read[c], 1)
                            v.drain()
                            v.tensor_scalar(nmx[:, col:col + 1], mx[:, col:col + 1], -1.0, None, ALU.mult).then_inc(nm_done, 1)

                    v.tensor_scalar(slope[:, 0:1], slope[:, 0:1], 0.25, None, ALU.mult)
                    v.drain()
                    if kind == 1:
                        v.tensor_scalar(slope[:, 1:2], slope[:, 0:1], 0.5, None, ALU.mult)
                        v.drain()
                    for c in range(kind + 1):
                        v.scalar_tensor_tensor(bias[:, c, :], dist, slope[:, c:c + 1], mask_bias, ALU.mult, ALU.add)
                    v.drain()
                    v.wait_ge(pv_done, 8 * b + 1)
                    copy_d(v_tok[:, 4:8, :], 4)
                    v.drain().then_inc(v_read, 1)
                    biased(0)
                    for n in range(8):
                        a0 = 2 * n
                        v.wait_ge(exp_done, 16 * b + 2 * n + 2 + 1)
                        if kind == 0:
                            v.reciprocal(r0[:, a0:a0 + 2], rs[:, a0:a0 + 2])
                            v.drain()
                            v.scalar_tensor_tensor(coef, r0[:, a0 + 1:a0 + 2], neglam, rs[:, a0:a0 + 1], ALU.mult, ALU.mult)
                            v.drain()
                            K = P * (n + 1)
                            v.scalar_tensor_tensor(pr[:, 0, 0:K], pr[:, 1, 0:K], coef, pr[:, 0, 0:K], ALU.mult, ALU.add)\
                                .then_inc(w_done, 1)
                        else:
                            v.reciprocal(r0[:, a0:a0 + 2], rs[:, a0:a0 + 2])
                        if n < 7:
                            biased(n + 1)
                        for c, lane, k0, m in lanes(kind, n):
                            if lane == 1:
                                v.wait_ge(pv_done, 8 * b + n + 1)
                                copy_d(wT[:, c, k0:k0 + m, :], m)
                        v.drain()
                        v.wait_ge(pv_done, 8 * b + n + 1 + 1)
                        if kind == 0:
                            v.tensor_scalar(o_sb[:, n, :], bank(6, P), r0[:, a0:a0 + 1], None, ALU.mult)
                            v.drain()
                            v.tensor_tensor_reduce(out=junk, in0=o_sb[:, n, :], in1=o_sb[:, n, :], scale=1.0, scalar=0.0,
                                                   op0=ALU.mult, op1=ALU.add, accum_out=ms[:, n:n + 1])
                        else:
                            for c in range(2):
                                v.tensor_scalar(o_sb[:, n, 64 * c:64 * c + 64], bank(6)[:, 192 * c:192 * c + 64],
                                                r0[:, a0 + c:a0 + c + 1], None, ALU.mult)
                        v.drain().then_inc(o_done, 1)
                    if kind == 0:
                        v.wait_ge(sub_root, b + 1)
                        v.reciprocal(ms, ms)
                        v.drain()
                        v.tensor_scalar(ms, ms, 1.0 - LAM_INIT, None, ALU.mult)
                        v.drain()
                        v.tensor_tensor(o_sb, o_sb, ms.rearrange("p (n u) -> p n u", u=1).broadcast_to([P, 8, P]), ALU.mult)
                    v.drain().then_inc(o_ready, 1)
                    count += 1
                    v.wait_ge(td_done, before(count))
                    dst = yT[:, bass.ds(b, 1), 512:1024].rearrange("p u t -> p (u t)")
                    if kind == 0:
                        v.tensor_scalar(dst, bank(5), sub_g, None, ALU.mult).then_inc(td_free, 1)
                    else:
                        v.tensor_copy(dst, bank(5)).then_inc(td_free, 1)
                    v.drain().then_inc(blk_done, 1)

                v.drain().then_inc(blk_done, 1)
                for kind in range(2):
                    if kind == 1:
                        v.wait_ge(tab_full, 48)
                        v.memset(slope[:, 0:1], 2.0)
                        v.drain()
                    with v.Fori(0, 2) as i:
                        for s in range(2):
                            block_(kind, 4 * kind + 2 * i + s)

            def gated():
                v.wait_ge(st_done, 16 * 4 * PAIRS_IN + 16)
                v.memset(attnT, 0.0)
                v.drain()
                chunk = lambda t: t.rearrange("p (n t) -> p n t", t=P)
                with v.Fori(0, C_HEADS) as h:
                    v.wait_ge(g_w, 32 * h + 32)
                    v.wait_ge(g_zread, 2 * h + 1)
                    v.tensor_scalar(gb, ps[:, 0:1024], bg2[:, :], 0.0, ALU.add, ALU.min).then_inc(g_zread, 1)
                    v.wait_ge(g_qk, 32 * h + 32)
                    v.tensor_scalar(gq, gq, C_DK ** -0.5, None, ALU.mult)
                    v.drain()
                    v.wait_ge(g_sp, h + 1)
                    v.tensor_tensor(gb, gb, gd, ALU.subtract)
                    v.drain()
                    for n in range(8):
                        v.tensor_tensor_scan(gx[:, 0, n * P:(n + 1) * P], ones[:, :], gb[:, n * P:(n + 1) * P], 0.0, ALU.mult, ALU.add)
                    v.drain()
                    v.tensor_copy(gb, gx[:, 0, :]).then_inc(g_b, 1)
                    v.drain()
                    v.tensor_tensor(chunk(ke), chunk(gb)[:, :, P - 1:P].broadcast_to([P, 8, P]), chunk(gb), ALU.subtract).then_inc(g_ekd, 1)

                    def masked(lv):
                        v.drain()
                        v.wait_ge(g_s, 8 * h + lv + 1)
                        v.sem_inc(waited, 1)
                        for n in range(2):
                            v.copy_predicated(attnT[:, 4 * n:4 * n + 4, :],
                                              masks[:, lv:lv + 1, :].broadcast_to([P, 4, P]),
                                              bank(2 * (lv % 2) + n).rearrange("p (n i) -> p n i", i=P)).then_inc(g_pred, 1)

                    for lv in range(LEVELS):
                        m = 64 >> lv
                        b4 = gb.rearrange("p (n t) -> p n t", t=2 * m)
                        v.tensor_tensor(gd.rearrange("p (n t) -> p n t", t=2 * m), b4,
                                        b4[:, :, m - 1:m].broadcast_to([P, S // (2 * m), 2 * m]), ALU.subtract).then_inc(g_d, 1)
                        if lv == 0:
                            v.wait_ge(g_eb, 2 * h + 2)
                            v.tensor_tensor(qe, qe, gq, ALU.mult).then_inc(g_qk_done, 1)
                            v.wait_ge(g_ek, h + 1)
                            v.tensor_tensor(ke, ke, gk, ALU.mult).then_inc(g_qk_done, 1)
                        if lv > 0:
                            masked(lv - 1)
                        half4 = lambda t: t.rearrange("p (n u t) -> p n u t", u=2, t=m)
                        v.wait_ge(g_f, 7 * h + lv + 1)
                        v.tensor_tensor(half4(gx[:, lv % 2, :])[:, :, 0, :], half4(gd)[:, :, 0, :], half4(gk)[:, :, 0, :], ALU.mult)
                        v.tensor_tensor(half4(gx[:, lv % 2, :])[:, :, 1, :], half4(gd)[:, :, 1, :], half4(gq)[:, :, 1, :], ALU.mult)
                        v.drain().then_inc(g_x, 1)
                    v.drain().then_inc(g_x, 1)
                    masked(LEVELS - 1)
                    masked(LEVELS)
                    for n in range(7):
                        v.wait_ge(g_u, 7 * h + n + 1)
                        if n == 0:
                            v.tensor_copy(state, bank(6)[:, 0:C_DV]).then_inc(g_st, 1)
                        else:
                            v.sem_inc(waited, 1)
                            v.drain()
                            v.wait_ge(g_o, 8 * h + n + 1)
                            v.scalar_tensor_tensor(state, state, eblast[:, n:n + 1], bank(6 + n % 2)[:, 0:C_DV],
                                                   ALU.mult, ALU.add).then_inc(g_st, 1)
                    v.drain().then_inc(g_st, 1)
                    v.wait_ge(g_root, h + 1)
                    v.reciprocal(ms, ms)
                    v.drain()
                    v.tensor_tensor(go, go, ms.rearrange("p (n u) -> p n u", u=1).broadcast_to([P, 8, C_DV]), ALU.mult).then_inc(g_on, 1)
                    v.wait_ge(g_silu, h + 1)
                    for b in range(2):
                        for n in range(2):
                            v.wait_ge(g_ot, 4 * h + 2 * b + n + 1)
                            dst = yT[:, bass.ds(2 * h + b, 1), n * 512:(n + 1) * 512].rearrange("p u t -> p (u t)")
                            v.scalar_tensor_tensor(dst, bank(2 * b + n), hg[:, b:b + 1], gvr[:, b, n * 512:(n + 1) * 512],
                                                   ALU.mult, ALU.mult).then_inc(g_yt, 1)

            junk = arena[:, 20480:20608]
            v.memset(mean_w[:, :], 1.0 / D)
            v.memset(ones[:, :], 1.0)
            v.memset(wg2[:, :], 0.0)
            v.memset(eps_c, EPS)
            v.memset(ada_acc[:, :, :], 0.0)
            v.drain().then_inc(setup_done, 1)
            v.wait_ge(s_const, 128)
            v.tensor_copy(masks.rearrange("p l i -> p (l i)"), ybuf[:, 1024:2048])
            for i in range(2):
                v.tensor_tensor_reduce(out=junk[:, 64 * i:64 * i + 64], in0=lamv[:, 128 * i:128 * i + 64], in1=lamv[:, 128 * i + 64:128 * i + 128],
                                       scale=1.0, scalar=0.0, op0=ALU.mult, op1=ALU.add, accum_out=lam2[:, i:i + 1])
            v.drain().then_inc(lam_dot, 1)
            v.wait_ge(lam_exp, 1)
            v.tensor_tensor(neglam, lam2[:, 1:2], lam2[:, 0:1], ALU.subtract)
            v.drain()
            v.tensor_scalar(neglam, neglam, -LAM_INIT, None, ALU.add)
            v.drain().then_inc(lam_dot, 1)
            rsum(0, 0, 0)
            rsum(0, 0, 1)
            v.wait_ge(cs_done, 1)
            with v.Fori(0, 2) as g:
                for j in range(4):
                    for s in range(2):
                        ada_unit(g, 2 * j + s, s, 4 * g + j)
            columns(0, 0, 2)
            fill(0, 0, 0)
            for layer in range(2):
                if layer == 1:
                    rsum(1, 0, 1)
                project(layer, 0)
                fill(layer, 0, 1)
                project(layer, 1)
                if layer == 0:
                    attention()
                else:
                    gated()
                for half in range(2):
                    base = USE_OUT[layer] + KB * half
                    for k in range(KB):
                        h_low(h_job(layer, 1, half), k, yT[:, k, half * HALF:(half + 1) * HALF])
                    for i in range(PAIRS_OUT):
                        v.wait_ge(unit_used, base + 2 * i + 4)
                        v.tensor_copy(y3[:, 2 * i + 1, :], bank(1)).then_inc(free1, 1)
                    rsum(layer, 1, half)
                    update(layer, 1, half)
                    rsum(layer, 2, half)
                fill(layer, 2, 0)
                for half in range(2):
                    base, tiles = ffn_base(layer, half), T_FFN[layer] + FB * half
                    with v.Fori(0, FB) as i:
                        v.wait_ge(exp_g, FB * dn_idx(layer, half) + i + 1)
                        v.tensor_scalar(silu_g, silu_g, 1.0, None, ALU.add)
                        v.drain()
                        v.reciprocal(silu_g, silu_g)
                        v.drain()
                        v.tensor_tensor(silu_g, bank(0), silu_g, ALU.mult).then_inc(free0, 1)
                        v.drain()
                        v.wait_ge(unit_used, base + 2 * i + 4)
                        v.tensor_tensor(act[:, bass.ds(i, 1), :].rearrange("p u t -> p (u t)"), silu_g, bank(1), ALU.mult)\
                            .then_inc(free1, 1)
                    d = dn_idx(layer, half)
                    base += 2 * FB
                    ahead = (layer, half) != (1, 1)
                    nl, nk, nh = (layer, 2, 1) if half == 0 else (1, 0, 0)
                    for u in range(FB):
                        v.wait_ge(ah_done, FB * d + u + 1)
                        v.tensor_tensor(a_lo[:, u % 2, :], act[:, u, :], a_hi[:, u % 2, :].bitcast(f32), ALU.subtract)\
                            .then_inc(al_done, 1)
                        if ahead and u % 2 == 0 and u < 16:
                            xn(nl, nk, nh, u // 2)
                        if ahead and u % 2 and 3 < u < 20:
                            h_low(h_job(nl, nk, nh), (u - 5) // 2, y3[:, (u - 5) // 2, :])
                    v.wait_ge(unit_used, base + FB + 2)
                    for m in range(1, KB, 2):
                        v.tensor_copy(y3[:, m, :], bank(m)).then_inc(dn_ev1, 1)
                    rsum(layer, 3, half)
                    update(layer, 3, half)
                    if layer == 0 and half == 0:
                        rsum(1, 0, 0)


def kernel(x, c, ada_w, ada_b, norm_g, ev_w_in, ev_lambda, ev_subln_g, ev_w_out, od_w_in, od_w_g2, od_b_g2,
           od_head_g, od_w_out, ffn_w_gate, ffn_w_up, ffn_w_down):
    import concourse.bacc as bacc
    from concourse.bass_utils import run_bass_kernel_spmd

    f = np.float32
    x, c, ada_w, ada_b, norm_g = (np.asarray(t) for t in (x, c, ada_w, ada_b, norm_g))
    ffn = [np.asarray(t) for t in (ffn_w_gate, ffn_w_up, ffn_w_down)]

    def columns_units(w):
        w = np.asarray(w)
        n = w.shape[1] // P
        return w.reshape(KB, P, n, P).transpose(2, 1, 0, 3).reshape(n, P, KB * P)

    pack = np.zeros((PACK_UNITS, P, 1024), f)
    for layer, (w_in, w_out) in enumerate(((ev_w_in, ev_w_out), (od_w_in, od_w_out))):
        w_in = np.asarray(w_in)[0]
        pack[PACK_IN[layer]:PACK_IN[layer] + 24] = columns_units(w_in[:, :3072])
        if layer == 1:
            last = w_in[:, 3072:].reshape(KB, P, C_RANK).transpose(1, 0, 2)
            pack[PACK_IN[1] + 24].reshape(P, KB, P)[:, :, :C_RANK] = last
        pack[PACK_OUT[layer]:PACK_OUT[layer] + KB] = columns_units(np.asarray(w_out)[0])
        at = PACK_FFN[layer]
        pack[at:at + 2 * FB:2] = columns_units(ffn[0][layer])
        pack[at + 1:at + 2 * FB:2] = columns_units(ffn[1][layer])
        pack[at + 2 * FB:at + 3 * FB] = ffn[2][layer].reshape(FB, P, D)

    d = 896.0 + np.arange(P)[:, None] - np.arange(S)[None, :]
    copies = (d <= 128).astype(int) + ((d % 4 == 0) & (d <= 512)) + (d % 16 == 0)
    reach = (d >= 0) & (copies > 0)
    dilated = np.where(reach, np.log(np.maximum(copies, 1)) / SCORE_SCALE, MASKED)
    levels = np.zeros((P, 8, P), f)
    j, i = np.arange(P)[:, None], np.arange(P)[None, :]
    for lv in range(LEVELS):
        m = 64 >> lv
        levels[:, lv] = (j // (2 * m) == i // (2 * m)) & (j % (2 * m) < m) & (i % (2 * m) >= m)
    levels[:, LEVELS] = i == j

    arrays = {
        "xT": x[0].T, "cT": c[0].reshape(KB, P).T, "weights": pack,
        "ada_w": ada_w.reshape(2, KB, P, 6, D).transpose(0, 3, 1, 2, 4).reshape(96, P, D),
        "ada_bT": ada_b.reshape(96, P).T, "norm_gT": norm_g.reshape(64, P).T,
        "lam_p": np.broadcast_to(np.asarray(ev_lambda).reshape(1, 4 * HEAD_DIM), (P, 4 * HEAD_DIM)),
        "subln_g": np.asarray(ev_subln_g).reshape(P, 1),
        "w_g2": np.asarray(od_w_g2)[0].reshape(C_RANK, C_HEADS, P).transpose(1, 0, 2),
        "b_g2": np.asarray(od_b_g2)[0].reshape(C_HEADS, P, 1),
        "head_g": np.asarray(od_head_g)[0].reshape(2, P).T,
        "identity": np.eye(P, dtype=f), "distance": (-d / SCORE_SCALE).astype(f),
        "causal_bias": np.where(d >= 0, 0.0, MASKED).astype(f), "dilated_bias": dilated.astype(f),
        "level_masks": levels,
    }
    arrays = {k: np.ascontiguousarray(a) for k, a in arrays.items()}
    nc = bacc.Bacc("TRN2", target_bir_lowering=False, num_devices=1)
    args = [nc.dram_tensor(k, a.shape, mybir.dt.from_np(a.dtype), kind="ExternalInput").ap() for k, a in arrays.items()]
    args.append(nc.dram_tensor("outT", (D, S), mybir.dt.float32, kind="ExternalOutput").ap())
    trunk_kernel(nc, *args)
    r = run_bass_kernel_spmd(nc, [arrays], core_ids=[0])
    return np.ascontiguousarray(r.results[0]["outT"].T)[None]
```

```python
from contextlib import ExitStack
import math

import numpy as np

import concourse.bass as bass
from concourse import mybir

D = 1024
S = 1024
P = 128
KB = D // P
HALF = S // 2
A_HEADS, B_HEADS, HEAD_DIM = 4, 8, 64
C_HEADS, C_DK, C_DV, C_RANK, C_TAU = 4, 128, 256, 16, 16.0
FFN = 2816
FB = FFN // P
NIN = [24, 25]
EPS = 1e-6
SCORE_SCALE = HEAD_DIM ** -0.5
LAM_INIT = 0.8 - 0.6 * math.exp(-0.3 * 0)
LEVELS = 7
MASKED = -1e30

FFN_UNITS = 3 * FB
PACK_IN = [0, NIN[0] + KB + FFN_UNITS]
PACK_OUT = [PACK_IN[0] + NIN[0], PACK_IN[1] + NIN[1]]
PACK_FFN = [PACK_OUT[0] + KB, PACK_OUT[1] + KB]
PACK_UNITS = PACK_FFN[1] + FFN_UNITS
USE_IN, USE_OUT, USE_FFN = [0, 0], [0, 0], [0, 0]
USE_OUT[0] = 2 * NIN[0]
USE_FFN[0] = USE_OUT[0] + 2 * KB
USE_IN[1] = USE_FFN[0] + 2 * FFN_UNITS
USE_OUT[1] = USE_IN[1] + 2 * NIN[1]
USE_FFN[1] = USE_OUT[1] + 2 * KB
PAIRS_IN, PAIRS_OUT = 12, KB // 2
T_IN = [0, 2 * PAIRS_IN + 2 * PAIRS_OUT + 2 * FB]
T_OUT = [T_IN[0] + 2 * PAIRS_IN, T_IN[1] + 2 * PAIRS_IN]
T_FFN = [T_OUT[0] + 2 * PAIRS_OUT, T_OUT[1] + 2 * PAIRS_OUT]


def trunk_kernel(nc, xT, cT, weights, ada_w, ada_bT, norm_gT, lam_p, subln_g, w_g2, b_g2, head_g,
                 identity, distance, causal_bias, dilated_bias, level_masks, outT):
    f32, f32r, u8 = mybir.dt.float32, mybir.dt.float32r, mybir.dt.uint8
    ALU, ACT, AX = mybir.AluOpType, mybir.ActivationFunctionType, mybir.AxisListType

    ctx = ExitStack()
    with ctx:
        def sb(name, shape, dt=f32):
            return ctx.enter_context(nc.sbuf_tensor(name, shape, dt))

        def sem(name):
            return ctx.enter_context(nc.semaphore(name))

        proj = nc.dram_tensor("proj", [24, P, S], f32, kind="Internal").ap()
        x = sb("x", [P, KB, S])
        h_hi = sb("h_hi", [P, KB, HALF], f32r)
        h_lo = sb("h_lo", [P, KB, HALF], f32r)
        w_raw = sb("w_raw", [P, 2, 1024])
        w_hi = sb("w_hi", [P, 2, 1024], f32r)
        w_lo = sb("w_lo", [P, 2, 1024], f32r)
        a_hi = sb("a_hi", [P, 2, HALF], f32r)
        a_lo = sb("a_lo", [P, 2, HALF], f32r)
        ybuf = sb("ybuf", [P, 8 * HALF])
        arena = sb("arena", [P, 20736])
        glr = sb("glr", [P, S])
        rinv = sb("rinv", [P, 3, HALF])
        ident = sb("ident", [P, P])
        mean_w = sb("mean_w", [P, P])
        ones = sb("ones", [P, P])
        masks = sb("masks", [P, 8, P], u8)
        wg2 = sb("wg2", [P, P])
        bg2 = sb("bg2", [P, 1])
        cs = sb("cs", [P, KB])
        ada_b = sb("ada_b", [P, 96])
        mod = sb("mod", [P, 96])
        ng = sb("ng", [P, 64])
        gain = sb("gain", [P, 64])
        small = sb("small", [P, 128])
        ps = ctx.enter_context(nc.psum_tensor("ps", [P, 4096], f32))

        def bank(b, n=512):
            return ps[:, b * 512:b * 512 + n]

        y3 = ybuf[:, :].rearrange("p (k t) -> p k t", k=KB)
        yT = arena[:, 0:8192].rearrange("p (k t) -> p k t", k=KB)
        act = arena[:, 0:FB * HALF].rearrange("p (k t) -> p k t", k=FB)
        exp_buf = [arena[:, 11264:11776], arena[:, 19968:20480]]
        sq = arena[:, 11776:15872].rearrange("p (k t) -> p k t", k=KB)
        y_out1 = arena[:, 15872:19968].rearrange("p (k t) -> p k t", k=KB)
        ada_first = arena[:, 0:16384].rearrange("p (g u n) -> p g u n", g=2, u=KB)
        acc_first = arena[:, 16384:18432].rearrange("p (g n) -> p g n", g=2)
        lamv, mask_f = arena[:, 18432:18688], arena[:, 18688:19712]
        stage = arena[:, 0:1024].rearrange("p (s t) -> p s t", s=2)
        ada_raw = arena[:, 1024:3072].rearrange("p (s n) -> p s n", s=2)
        ada_acc = arena[:, 3072:6144].rearrange("p (g n) -> p g n", g=3)
        q_dup = arena[:, 8192:10240].rearrange("p (c t) -> p c t", c=2)
        k_dup = arena[:, 10240:12288].rearrange("p (c t) -> p c t", c=2)
        hf, lf = (t[:, :, :].rearrange("p k t -> p (k t)") for t in (h_hi, h_lo))
        wf, wg = (t[:, :, :].rearrange("p k t -> p (k t)") for t in (w_hi, w_lo))
        two = lambda t: t.rearrange("p (c t) -> p c t", c=2)
        q_split = [two(hf[:, 0:2048]), two(lf[:, 2048:4096])]
        k_high = [two(hf[:, 2048:4096]), two(wf)]
        k_low = [two(lf[:, 0:2048]), two(wg)]
        v_sb = arena[:, 12288:13312]
        v_tok = arena[:, 13312:14336].rearrange("p (n d) -> p n d", d=P)
        wT = arena[:, 14336:16384].rearrange("p (c k q) -> p c k q", c=2, q=P)
        dist = arena[:, 16384:17408]
        mask_bias = arena[:, 17408:18432]
        bias = arena[:, 18432:20480].rearrange("p (c k) -> p c k", c=2)
        sc = ybuf[:, 0:2048].rearrange("p (c k) -> p c k", c=2)
        pr = ybuf[:, 2048:4096].rearrange("p (c k) -> p c k", c=2)
        o_sb = glr[:, :].rearrange("p (n d) -> p n d", d=P)
        gq = arena[:, 8192:9216]
        gk = arena[:, 9216:10240]
        gvr = arena[:, 10240:12288].rearrange("p (b t) -> p b t", b=2)
        gb = arena[:, 12288:13312]
        gd = arena[:, 13312:14336]
        gx = arena[:, 14336:16384].rearrange("p (s t) -> p s t", s=2)
        attnT = arena[:, 16384:17408].rearrange("p (n i) -> p n i", i=P)
        qe = arena[:, 17408:18432]
        ke = arena[:, 18432:19456]
        ke_tok = arena[:, 19456:20480].rearrange("p (n d) -> p n d", d=P)
        state = arena[:, 20480:20736]
        gv_tok = ybuf[:, 0:2048].rearrange("p (n d) -> p n d", d=C_DV)
        go = ybuf[:, 2048:4096].rearrange("p (n d) -> p n d", d=C_DV)
        mx, nmx, rs = small[:, 0:16], small[:, 16:32], small[:, 32:48]
        r0, ms = small[:, 48:64], small[:, 64:72]
        coef, neglam = small[:, 72:73], small[:, 73:74]
        slope = small[:, 74:76]
        lam2 = small[:, 76:78]
        eps_c = small[:, 78:79]
        sub_g = small[:, 79:80]
        hg = small[:, 80:82]
        eblast = small[:, 82:90]
        r1 = small[:, 90:92]

        s_const, s_x = sem("consts_loaded"), [sem("x_loaded0"), sem("x_loaded1")]
        ada_big = [sem(f"ada_first{i}") for i in range(4)]
        raw_full = [sem("raw_full0"), sem("raw_full1")]
        hi_done, lo_done = sem("w_hi_done"), sem("w_lo_done")
        unit_used = sem("unit_used")
        free0, free1 = sem("bank0_free"), sem("bank1_free")
        exp_g = sem("exp_gate_done")
        st_done = sem("proj_stored")
        ah_done, al_done = sem("a_hi_done"), sem("a_lo_done")
        dn_done, dn_ev0, dn_ev1 = sem("down_done"), sem("down_read_act"), sem("down_read_dve")
        xn_done, hh_done, hl_done = sem("xn_done"), sem("h_hi_done"), sem("h_lo_done")
        sq_done, ssum_done, mean_done = sem("square_done"), sem("square_summed"), sem("mean_done")
        root_done, rinv_done, x_upd = sem("root_done"), sem("rinv_done"), sem("x_updated")
        ada_full = [sem("ada_full0"), sem("ada_full1")]
        ada_used, acc_done, ada_mm, mod_done = sem("ada_used"), sem("ada_summed"), sem("ada_mm"), sem("mod_done")
        cs_done, setup_done, lam_dot, lam_exp = sem("silu_c_done"), sem("setup_done"), sem("lam_dot"), sem("lam_exp")
        glr_mm, glr_done = sem("gate_rank_mm"), sem("gate_rank_done")
        outs = sem("out_stored")
        tab_full = sem("bias_tables")
        qk_full, qk_hi, qk_lo = sem("qk_full"), sem("qk_high"), sem("qk_low")
        v_full, v_read = sem("v_full"), sem("v_read")
        s_done = [sem("scores0"), sem("scores1")]
        s_read = [sem("scores_read0"), sem("scores_read1")]
        nm_done, exp_done, w_done = sem("neg_max"), sem("exp_done"), sem("weights_done")
        ta_done, ta_free = sem("turned_a"), sem("turned_a_read")
        td_done, td_free = sem("turned_d"), sem("turned_d_read")
        pv_done, o_done = sem("pv_done"), sem("o_read")
        sub_root, o_ready, blk_done = sem("sub_root"), sem("o_ready"), sem("block_done")
        g_qk, g_v, g_r, g_w = sem("g_qk"), sem("g_v"), sem("g_r"), sem("g_w")
        g_z, g_zread, g_sp, g_b = sem("g_z"), sem("g_zread"), sem("g_softplus"), sem("g_cumsum")
        g_eb, g_ekd, g_ek, g_qk_done = sem("g_exp_b"), sem("g_last_minus_b"), sem("g_exp_k"), sem("g_qe_ke")
        g_d, g_f, g_x, g_s, g_pred = sem("g_diff"), sem("g_factor"), sem("g_level"), sem("g_scores"), sem("g_masked")
        g_vt, g_vtr, g_kt, g_ktr = sem("g_v_turned"), sem("g_v_copied"), sem("g_k_turned"), sem("g_k_copied")
        g_o, g_or, g_u, g_st = sem("g_out"), sem("g_out_read"), sem("g_update"), sem("g_state")
        g_root, g_on, g_silu, g_ot, g_yt = sem("g_root"), sem("g_normed"), sem("g_silu_r"), sem("g_out_turned"), sem("g_y")

        waited = sem("wait_carried")

        block = ctx.enter_context(nc.Block())

        def h_job(layer, kind, half):
            return 6 * layer + 2 * kind + half

        def stat_job(layer, kind, half):
            return {(0, 0): 7, (0, 1): 9, (1, 0): 10, (2, 0): 11, (1, 1): 12, (2, 1): 13, (3, 0): 14, (3, 1): 15}[(kind, half)] \
                if layer else \
                {(0, 0): 0, (0, 1): 1, (1, 0): 2, (2, 0): 3, (1, 1): 4, (2, 1): 5, (3, 0): 6, (3, 1): 8}[(kind, half)]

        def hosted(layer, phase, half):
            if phase == "in" and half == 0:
                return (((0, 3, 1), y3) if layer else None), (layer, 0, 1)
            if phase == "out" and half == 1:
                return ((layer, 1, 0), y3), (layer, 2, 0)
            if phase == "ffn" and half == 0:
                return ((layer, 1, 1), y_out1), (layer, 2, 1)
            if phase == "ffn" and half == 1:
                return ((layer, 3, 0), y3), (None if layer else (1, 0, 0))
            return None, None

        def rinv_slot(kind, half):
            return half if kind in (0, 2) else 2

        def fill_job(layer, kind, half):
            return 2 * (2 * layer + (kind == 2)) + half

        def upd(layer, kind, half):
            return 4 * layer + (0 if kind == 1 else 2) + half + 1

        def in_base(layer, half):
            return USE_IN[layer] + half * NIN[layer]

        def ffn_base(layer, half):
            return USE_FFN[layer] + half * FFN_UNITS

        def dn_idx(layer, half):
            return 2 * layer + half

        LANE = [8, 14]

        def lanes(kind, n):
            if kind == 0:
                if n < 4:
                    return [(0, n % 2, 0, n + 1)]
                return [(0, 0, 0, 4), (0, 1, 4, n - 3)]
            out = []
            for c in (0, 1):
                for k0 in range(0, n + 1, 4):
                    out.append((c, c, k0, min(4, n + 1 - k0)))
            return out

        def lane_count(kind, n, lane):
            return 1 + sum(g[1] == lane for m in range(n) for g in lanes(kind, m))

        @block.sync
        def _(sp):
            sp.sem_inc(st_done, 16)
            sp.dma_start(cs[:, :], cT).then_inc(s_const, 16)
            sp.dma_start(ada_b[:, :], ada_bT).then_inc(s_const, 16)
            sp.dma_start(ng[:, :], norm_gT).then_inc(s_const, 16)
            sp.dma_start(ident[:, :], identity).then_inc(s_const, 16)
            sp.dma_start(lamv, lam_p).then_inc(s_const, 16)
            sp.dma_start(sub_g, subln_g).then_inc(s_const, 16)
            sp.dma_start(hg, head_g).then_inc(s_const, 16)
            sp.dma_start(mask_f, level_masks.rearrange("p l i -> p (l i)")).then_inc(s_const, 16)
            x_in = xT.rearrange("(k p) t -> p k t", p=P)
            sp.dma_start(x[:, :, 0:HALF], x_in[:, :, 0:HALF]).then_inc(s_x[0], 16)
            for g in range(2):
                for u in range(0, KB, 4):
                    sp.dma_start(ada_first[:, g, u:u + 4, :], ada_w[KB * g + u:KB * g + u + 4].rearrange("u p n -> p u n"))\
                        .then_inc(ada_big[2 * g + u // 4], 16)
            sp.dma_start(x[:, :, HALF:S], x_in[:, :, HALF:S]).then_inc(s_x[1], 16)

            def ada_pair(pair):
                sp.wait_ge(ada_used, 2 * (pair - 8) + 1)
                for s in range(2):
                    sp.dma_start(ada_raw[:, s, :], ada_w[bass.ds(2 * pair + s, 1)] .rearrange("u p n -> (u p) n")
                                 if not isinstance(pair, int) else ada_w[2 * pair + s]).then_inc(ada_full[s], 16)

            def unit(pack, use, s):
                sp.wait_ge(lo_done, use + 1)
                src = weights[pack] if isinstance(pack, int) else weights[bass.ds(pack, 1)].rearrange("u p n -> (u p) n")
                sp.dma_start(w_raw[:, s, :], src).then_inc(raw_full[s], 16)

            def stream(pack, use, pairs):
                with sp.Fori(0, pairs) as i:
                    for s in range(2):
                        unit(pack + 2 * i + s, use + 2 * i + s, (use + s) % 2)

            def project(layer, half):
                use, n_ada = in_base(layer, half), [[12, 12], [12, 4]][layer][half]
                ada0 = [[8, 20], [32, 44]][layer][half]
                done = PAIRS_IN * (2 * layer + half)

                def store(i):
                    sp.wait_ge(free0, T_IN[layer] + PAIRS_IN * half + i + 2)
                    sp.wait_ge(free1, T_IN[layer] + PAIRS_IN * half + i + 2)
                    dst = proj[2 * i:2 * i + 2] if isinstance(i, int) else proj[bass.ds(2 * i, 2)]
                    sp.dma_start(dst.rearrange("b p t -> p b t")[:, :, half * HALF:(half + 1) * HALF],
                                 stage[:, :, :]).then_inc(st_done, 16)

                def body(i, ada):
                    for s in range(2):
                        unit(PACK_IN[layer] + 2 * i + s, use + 2 * i + s, (use + s) % 2)
                    if ada:
                        ada_pair(ada0 + i)

                body(0, True)
                with sp.Fori(1, n_ada) as i:
                    body(i, True)
                    store(i - 1)
                if n_ada < PAIRS_IN:
                    with sp.Fori(n_ada, PAIRS_IN) as i:
                        body(i, False)
                        store(i - 1)
                if layer == 1:
                    unit(PACK_IN[1] + 24, use + 24, (use + 24) % 2)
                store(PAIRS_IN - 1)

            def attention():
                sp.wait_ge(st_done, 16 * 2 * PAIRS_IN + 16)
                sp.wait_ge(hl_done, 16)
                sp.wait_ge(mod_done, 3)
                sp.dma_start(dist, distance).then_inc(tab_full, 16)
                sp.dma_start(mask_bias, causal_bias).then_inc(tab_full, 16)

                def load(b, slot, kind, j):
                    rows = (0, 4, 8) if kind == 0 else (12, 16, 20)

                    def row(r):
                        i = rows[r] + j
                        return proj[i] if isinstance(i, int) else proj[bass.ds(i, 1)].rearrange("u p n -> (u p) n")
                    sp.wait_ge(qk_lo, 4 * b + 1)
                    for c in range(2):
                        for top in (0, 64):
                            sp.dma_start(q_dup[top:top + 64, c, :], row(0)[64 * c:64 * c + 64, :]).then_inc(qk_full, 16)
                            sp.dma_start(k_dup[top:top + 64, c, :], row(1)[64 * c:64 * c + 64, :]).then_inc(qk_full, 16)
                    sp.wait_ge(v_read, b + 1)
                    sp.dma_start(v_sb, row(2)).then_inc(v_full, 16)

                with sp.Fori(0, 2) as i:
                    for s in range(2):
                        load(2 * i + s, s, 0, 2 * i + s)
                load(4, 0, 1, 0)
                sp.dma_start(mask_bias, dilated_bias).then_inc(tab_full, 16)
                load(5, 1, 1, 1)
                load(6, 0, 1, 2)
                load(7, 1, 1, 3)

            def gated():
                sp.wait_ge(st_done, 16 * 4 * PAIRS_IN + 16)
                sp.wait_ge(hl_done, 8 * (h_job(1, 0, 1) + 1))
                sp.wait_ge(mod_done, 5)
                with sp.Fori(0, C_HEADS) as h:
                    def row(i, n=1):
                        return proj[bass.ds(i, n)].rearrange("u p n -> p u n")
                    sp.wait_ge(g_yt, 4 * h + 1)
                    sp.dma_start(wg2[0:C_RANK, :], w_g2[bass.ds(h, 1)].rearrange("u p n -> (u p) n")).then_inc(g_w, 16)
                    sp.dma_start(bg2[:, :], b_g2[bass.ds(h, 1)].rearrange("u p n -> (u p) n")).then_inc(g_w, 16)
                    sp.dma_start(gq, proj[bass.ds(h, 1)].rearrange("u p n -> (u p) n")).then_inc(g_qk, 16)
                    sp.dma_start(gk, proj[bass.ds(4 + h, 1)].rearrange("u p n -> (u p) n")).then_inc(g_qk, 16)
                    sp.dma_start(gvr[:, :, :], row(8 + 2 * h, 2)).then_inc(g_v, 16)
                    sp.wait_ge(g_vt, 4 * h + 4)
                    sp.dma_start(gvr[:, :, :], row(16 + 2 * h, 2)).then_inc(g_r, 16)

            sp.wait_ge(mod_done, 1)
            for layer in range(2):
                for half in range(2):
                    project(layer, half)
                if layer == 0:
                    attention()
                else:
                    gated()
                for half in range(2):
                    stream(PACK_OUT[layer], USE_OUT[layer] + KB * half, KB // 2)
                for half in range(2):
                    use = ffn_base(layer, half)
                    stream(PACK_FFN[layer], use, FFN_UNITS // 2)
            for half in range(2):
                sp.wait_ge(x_upd, upd(1, 3, half))
                sp.dma_start(outT.rearrange("(k p) t -> p k t", p=P)[:, :, half * HALF:(half + 1) * HALF],
                             x[:, :, half * HALF:(half + 1) * HALF]).then_inc(outs, 16)
            sp.wait_ge(outs, 32)

        @block.gpsimd
        def _(pool):
            pool.sem_inc(lo_done, 2)

            def lo(use, s):
                pool.wait_ge(hi_done, use + 1)
                pool.tensor_tensor(w_lo[:, s, :], w_raw[:, s, :], w_hi[:, s, :].bitcast(f32),
                                   ALU.subtract).then_inc(lo_done, 1)

            def split_qk(b, s):
                for c in range(2):
                    pool.drain()
                    pool.wait_ge(qk_hi, 4 * b + 2 * c + 1)
                    pool.tensor_tensor(q_split[s][64:128, c, :], q_dup[64:128, c, :],
                                       q_split[s][64:128, c, :].bitcast(f32), ALU.subtract).then_inc(qk_lo, 1)
                    pool.drain()
                    pool.wait_ge(qk_hi, 4 * b + 2 * c + 2)
                    pool.tensor_tensor(k_low[s][:, c, :], k_dup[:, c, :],
                                       k_high[s][:, c, :].bitcast(f32), ALU.subtract).then_inc(qk_lo, 1)

            pool.sem_inc(qk_lo, 1)
            with pool.Fori(0, USE_OUT[0] // 2) as i:
                for s in range(2):
                    lo(2 * i + s, s)
            with pool.Fori(0, 4) as i:
                for s in range(2):
                    split_qk(2 * i + s, s)
            with pool.Fori(USE_OUT[0] // 2, (USE_FFN[1] + 2 * FFN_UNITS) // 2) as i:
                for s in range(2):
                    lo(2 * i + s, s)

        @block.tensor
        def _(pe):
            pe.sem_inc(unit_used, 2)
            pe.sem_inc(pv_done, 1)

            def unit(use, s, b, job=None):
                pe.wait_ge(hi_done, use + 1)
                for k in range(KB):
                    w = w_hi[:, s, k * P:(k + 1) * P]
                    if job is not None:
                        pe.wait_ge(hl_done, KB * job + k + 1)
                    pe.matmul(bank(b), w, h_hi[:, k, :], start=k == 0, stop=False)
                    pe.matmul(bank(b), w, h_lo[:, k, :], start=False, stop=False)
                pe.wait_ge(lo_done, use + 3)
                for k in range(KB):
                    mm = pe.matmul(bank(b), w_lo[:, s, k * P:(k + 1) * P], h_hi[:, k, :], start=False, stop=k == KB - 1)
                mm.then_inc(unit_used, 1)

            def two_pairs(use, tiles, i, job):
                for j in range(2):
                    for s in range(2):
                        pe.wait_ge((free0, free1)[s], tiles + 2 * i + j)
                        unit(use + 4 * i + 2 * j + s, (use + s) % 2, 2 * j + s, job if j == s == 0 else None)

            def pairs(layer, phase, half, use, tiles, n, job):
                post, pre = hosted(layer, phase, half)
                if phase == "out":
                    for i in range(PAIRS_OUT):
                        for s in range(2):
                            pe.wait_ge((free0, free1)[s], tiles + i)
                            unit(use + 2 * i + s, (use + s) % 2, 2 * (i % 2) + s, job if i == s == 0 else None)
                            if post and (i, s) == (0, 1):
                                mean(*post[0])
                            if pre and (i, s) == (PAIRS_OUT - 1, 0):
                                mean(*pre)
                    return
                two_pairs(use, tiles, 0, job)
                if post:
                    mean(*post[0])
                at = 1
                if pre:
                    two_pairs(use, tiles, 1, None)
                    two_pairs(use, tiles, 2, None)
                    mean(*pre)
                    at = 3
                with pe.Fori(at, n // 2) as i:
                    two_pairs(use, tiles, i, None)

            def mean(layer, kind, half):
                n = stat_job(layer, kind, half)
                pe.wait_ge(ssum_done, n + 1)
                if n:
                    pe.wait_ge(root_done, n)
                pe.matmul(bank(7), mean_w[:, :], rinv[:, rinv_slot(kind, half), :], start=True, stop=True)\
                    .then_inc(mean_done, 1)

            def ada_turn(n, groups, acc=ada_acc):
                pe.wait_ge(acc_done, n + 1)
                if n:
                    pe.wait_ge(mod_done, n)
                for g in range(groups):
                    for m in range(KB):
                        mm = pe.matmul(bank(6)[:, g * 8 + m:g * 8 + m + 1], acc[:, g, m * P:(m + 1) * P],
                                       ones[:, 0:1], start=True, stop=True)
                mm.then_inc(ada_mm, 1)

            def attention_block(kind, b, slot):
                before = (lambda t: LANE[0] * b + t) if kind == 0 else (lambda t: LANE[0] * 4 + LANE[1] * (b - 4) + t)

                def turn_v():
                    pe.wait_ge(v_full, 16 * b + 16)
                    for lane in range(2):
                        pe.wait_ge((ta_free, td_free)[lane], before(0) + 1)
                        for n in range(4):
                            m = 4 * lane + n
                            mm = pe.transpose(bank(4 + lane)[:, n * P:(n + 1) * P], v_sb[:, m * P:(m + 1) * P], ident[:, :])
                        mm.then_inc((ta_done, td_done)[lane], 1)

                def scores(n):
                    for c in range(2):
                        pe.wait_ge(s_read[c], 8 * b + n + 1)
                        if n == 0:
                            pe.wait_ge(qk_lo, 4 * b + 2 * c + 3)
                        W = 256 * ((n + 2) // 2)
                        for k0 in range(0, W, 512):
                            w = min(512, W - k0)
                            for part in (k_high, k_low):
                                mm = pe.matmul(ps[:, c * 1024 + k0:c * 1024 + k0 + w],
                                               q_split[slot][:, c, n * P:(n + 1) * P], part[slot][:, c, k0:k0 + w],
                                               start=part is k_high, stop=part is k_low)
                        mm.then_inc(s_done[c], 1)

                def weigh(n):
                    count = [lane_count(kind, n, 0), lane_count(kind, n, 1)]
                    done = [(0, 0)] * 2
                    if kind == 0:
                        pe.wait_ge(w_done, 8 * b + n + 1 + 1)
                    for c, lane, k0, m in lanes(kind, n):
                        if kind == 1:
                            pe.wait_ge(exp_done, 16 * b + 2 * n + c + 1 + 1)
                        pe.wait_ge((ta_free, td_free)[lane], before(count[lane]) + 1)
                        for i in range(m):
                            mm = pe.transpose(bank(4 + lane)[:, i * P:(i + 1) * P],
                                              pr[:, c, (k0 + i) * P:(k0 + i + 1) * P], ident[:, :])
                        mm.then_inc((ta_done, td_done)[lane], 1)
                        count[lane] += 1
                    pe.wait_ge(ta_free, before(count[0]) + 1)
                    pe.wait_ge(td_free, before(count[1]) + 1)
                    pe.wait_ge(o_done, 8 * b + n + 1)
                    for c in range(1 if kind == 0 else 2):
                        for kb in range(n + 1):
                            mm = pe.matmul(bank(6)[:, c * P:(c + 1) * P], wT[:, c, kb, :], v_tok[:, kb, :],
                                           start=kb == 0, stop=kb == n)
                    mm.then_inc(pv_done, 1)

                def turn_out():
                    pe.wait_ge(o_ready, b + 1)
                    for lane in range(2):
                        pe.wait_ge((ta_free, td_free)[lane], before(LANE[kind] - 1) + 1)
                        for n in range(4):
                            mm = pe.transpose(bank(4 + lane)[:, n * P:(n + 1) * P], o_sb[:, 4 * lane + n, :], ident[:, :])
                        mm.then_inc((ta_done, td_done)[lane], 1)

                turn_v()
                scores(0)
                for n in range(8):
                    if n < 7:
                        scores(n + 1)
                    weigh(n)
                turn_out()

            def attention():
                pe.wait_ge(free0, T_OUT[0] + 1)
                pe.wait_ge(free1, T_OUT[0] + 1)
                for kind in range(2):
                    with pe.Fori(0, 2) as i:
                        for s in range(2):
                            attention_block(kind, 4 * kind + 2 * i + s, s)
                pe.wait_ge(ta_free, 4 * sum(LANE) + 1)
                pe.wait_ge(td_free, 4 * sum(LANE) + 1)

            def gated():
                pe.wait_ge(free0, T_OUT[1] + 1)
                pe.wait_ge(free1, T_OUT[1] + 1)
                pe.wait_ge(glr_done, 2)
                pe.wait_ge(mod_done, 5)
                with pe.Fori(0, C_HEADS) as h:
                    pe.wait_ge(g_w, 32 * h + 32)
                    pe.wait_ge(g_yt, 4 * h + 1)
                    for n in range(2):
                        mm = pe.matmul(bank(n), wg2[:, :], glr[:, n * 512:(n + 1) * 512], start=True, stop=True)
                    mm.then_inc(g_z, 1)
                    pe.wait_ge(g_v, 16 * h + 16)
                    pe.wait_ge(g_or, 8 * h + 1)
                    pe.wait_ge(g_st, 8 * h + 1)
                    for n in range(4):
                        for i in range(2):
                            for b in range(2):
                                m = 2 * n + i
                                mm = pe.transpose(bank(4 + n)[:, i * 256 + b * P:i * 256 + (b + 1) * P],
                                                  gvr[:, b, m * P:(m + 1) * P], ident[:, :])
                        mm.then_inc(g_vt, 1)
                    pe.wait_ge(g_zread, 2 * h + 2)
                    for lv in range(LEVELS + 1):
                        pe.wait_ge(g_x, 8 * h + lv + 1)
                        pe.wait_ge(g_pred, 16 * h + 2 * max(0, lv - 1) + 1)
                        for n in range(8):
                            t = slice(n * P, (n + 1) * P)
                            a, b = (gx[:, lv % 2, t], gx[:, lv % 2, t]) if lv < LEVELS else (gk[:, t], gq[:, t])
                            mm = pe.matmul(bank(2 * (lv % 2) + n // 4)[:, (n % 4) * P:(n % 4 + 1) * P], a, b,
                                           start=True, stop=True)
                        mm.then_inc(g_s, 1)
                        if lv == 0:
                            pe.wait_ge(g_qk_done, 2 * h + 2)
                            for n in range(2):
                                pe.wait_ge(g_vtr, 4 * h + 4)
                                for i in range(4):
                                    m = 4 * n + i
                                    mm = pe.transpose(bank(4 + n)[:, i * P:(i + 1) * P], ke[:, m * P:(m + 1) * P], ident[:, :])
                                mm.then_inc(g_kt, 1)
                    pe.wait_ge(g_pred, 16 * h + 16 + 1)
                    pe.wait_ge(g_ktr, 2 * h + 2)
                    for n in range(8):
                        t = slice(n * P, (n + 1) * P)
                        if n < 7:
                            if n >= 2:
                                pe.wait_ge(g_st, 8 * h + n - 1 + 1)
                            pe.matmul(bank(6 + n % 2)[:, 0:C_DV], ke_tok[:, n, :], gv_tok[:, n, :], start=True, stop=True)\
                                .then_inc(g_u, 1)
                        if n >= 2:
                            pe.wait_ge(g_or, 8 * h + n - 1 + 1)
                        mm = pe.matmul(bank(4 + n % 2)[:, 0:C_DV], attnT[:, n, :], gv_tok[:, n, :], start=True, stop=n == 0)
                        if n:
                            pe.wait_ge(g_st, 8 * h + n + 1)
                            mm = pe.matmul(bank(4 + n % 2)[:, 0:C_DV], qe[:, t], state, start=False, stop=True)
                        mm.then_inc(g_o, 1)
                    pe.wait_ge(g_on, h + 1)
                    for b in range(2):
                        for n in range(2):
                            for i in range(4):
                                mm = pe.transpose(bank(2 * b + n)[:, i * P:(i + 1) * P],
                                                  go[:, 4 * n + i, b * P:(b + 1) * P], ident[:, :])
                            mm.then_inc(g_ot, 1)
                pe.wait_ge(g_yt, 4 * C_HEADS + 1)

            def down(layer, half):
                use, d = ffn_base(layer, half) + 2 * FB, dn_idx(layer, half)
                tiles = T_FFN[layer] + FB * (half + 1)
                pe.wait_ge(free0, tiles + 1)
                pe.wait_ge(free1, tiles + 1)
                pe.wait_ge(root_done, [[6, 8], [14, 15]][layer][half])

                def row(i, s, first, last):
                    u = use + 2 * i + s
                    slot = (use + s) % 2
                    cols = [slice(m * P, (m + 1) * P) for m in range(KB)]
                    pe.wait_ge(hi_done, u + 1)
                    pe.wait_ge(ah_done, FB * d + 2 * i + s + 1)
                    for m in range(KB):
                        pe.matmul(bank(m), w_hi[:, slot, cols[m]], a_hi[:, s, :], start=first, stop=False)
                    pe.wait_ge(al_done, FB * d + 2 * i + s + 1)
                    for m in range(KB):
                        pe.matmul(bank(m), w_hi[:, slot, cols[m]], a_lo[:, s, :], start=False, stop=False)
                    pe.wait_ge(lo_done, u + 3)
                    for m in range(KB):
                        mm = pe.matmul(bank(m), w_lo[:, slot, cols[m]], a_hi[:, s, :], start=False, stop=last)
                    mm.then_inc(unit_used, 1)

                row(0, 0, True, False)
                row(0, 1, False, False)
                with pe.Fori(1, FB // 2 - 1) as i:
                    for s in range(2):
                        row(i, s, False, False)
                row(FB // 2 - 1, 0, False, False)
                row(FB // 2 - 1, 1, False, True)
                pe.wait_ge(dn_ev0, 4 * (d + 1))
                pe.wait_ge(dn_ev1, 4 * (d + 1))

            pe.wait_ge(s_const, 128)
            pe.wait_ge(setup_done, 1)
            mean(0, 0, 0)
            ada_turn(0, 2, acc_first)
            for layer in range(2):
                for half in range(2):
                    use = in_base(layer, half)
                    pairs(layer, "in", half, use, T_IN[layer] + PAIRS_IN * half, PAIRS_IN, h_job(layer, 0, half))
                    if layer == 1:
                        if half:
                            pe.wait_ge(glr_done, 1)
                        unit(use + 24, (use + 24) % 2, 5)
                        pe.matmul(bank(4)[:, 0:1], ident[:, :], ones[:, 0:1], start=True, stop=True).then_inc(glr_mm, 1)
                    ada_turn(1 + 2 * layer + half, [[3, 3], [3, 1]][layer][half])
                if layer == 0:
                    attention()
                else:
                    gated()
                for half in range(2):
                    pairs(layer, "out", half, USE_OUT[layer] + KB * half, T_OUT[layer] + PAIRS_OUT * half, PAIRS_OUT,
                          h_job(layer, 1, half))
                for half in range(2):
                    pairs(layer, "ffn", half, ffn_base(layer, half), T_FFN[layer] + FB * half, FB,
                          h_job(layer, 2, half))
                    down(layer, half)
            mean(1, 3, 1)

        @block.scalar
        def _(a):
            for count in (free0, exp_done, ta_free, g_or):
                a.sem_inc(count, 1)

            def hi_at(base, i, s):
                slot = (base + s) % 2
                a.wait_ge(raw_full[slot], 16 * ((base + s) // 2 + i) + 16)
                a.wait_ge(unit_used, base + 2 * i + s + 1)
                a.activation(w_hi[:, slot, :], w_raw[:, slot, :], ACT.Copy).then_inc(hi_done, 1)

            def square(layer, kind, half, src):
                n = stat_job(layer, kind, half)
                if kind in (0, 2):
                    if layer == 0 and kind == 0:
                        a.wait_ge(s_x[half], 16)
                    else:
                        a.wait_ge(x_upd, upd(layer - (kind == 0), 3 if kind == 0 else 1, half))
                    src = x[:, :, half * HALF:(half + 1) * HALF]
                elif kind == 3:
                    a.wait_ge(dn_ev1, 4 * (dn_idx(layer, half) + 1))
                else:
                    a.wait_ge(free1, T_OUT[layer] + PAIRS_OUT * (half + 1) + 1)
                if kind in (1, 3):
                    a.drain()
                if n:
                    a.wait_ge(ssum_done, n)
                dst = y3 if n == 0 else sq
                a.activation(dst[:, 0:4, :], src[:, 0:4, :], ACT.Square)
                a.activation(dst[:, 4:8, :], src[:, 4:8, :], ACT.Square).then_inc(sq_done, 1)

            def root(layer, kind, half):
                a.wait_ge(mean_done, stat_job(layer, kind, half) + 1)
                a.activation(rinv[:, rinv_slot(kind, half), :], bank(7), ACT.Sqrt, bias=eps_c).then_inc(root_done, 1)

            def modulate(layer, kind, half, k):
                g = 8 * (4 * layer + (0 if kind == 0 else 2)) + k
                sh = 48 * layer + (0 if kind == 0 else 24) + k
                a.wait_ge(xn_done, 8 * fill_job(layer, kind, half) + k + 1)
                a.activation(y3[:, k, :], y3[:, k, :], ACT.Identity, bias=mod[:, sh:sh + 1], scale=gain[:, g:g + 1])

            def write_h(k, src, first_unit):
                if k == 0:
                    a.drain()
                    a.wait_ge(unit_used, first_unit + 2)
                a.activation(h_hi[:, k, :], src, ACT.Copy).then_inc(hh_done, 1)

            def hooks(layer, phase, half):
                post, pre = hosted(layer, phase, half)
                at = {}

                def put(n, f, *args):
                    at.setdefault(n, []).append((f, args))
                if post:
                    put(-1, square, *post[0], post[1])
                    put(0 if phase == "out" else 1, root, *post[0])
                if pre:
                    put(1 if phase == "out" else 3, square, *pre, None)
                    put(2.5 if phase == "out" else 5, root, *pre)
                    for k in range(KB):
                        if phase == "in":
                            put(6 + k // 2, modulate, *pre, k)
                        if phase == "out":
                            put(2.5, modulate, *pre, k)
                return at

            def run(at, n):
                for f, args in at.get(n, []):
                    f(*args)

            def project(layer, half):
                base = in_base(layer, half)
                st = PAIRS_IN * (2 * layer + half)
                at = hooks(layer, "in", half)

                def pair(i, j):
                    for s in range(2):
                        hi_at(base, i, s)
                    a.wait_ge(unit_used, base + 2 * i + 3)
                    a.wait_ge(st_done, 16 * (st + i) + 16)
                    a.activation(stage[:, 0, :], bank(2 * j), ACT.Copy).then_inc(free0, 1)

                run(at, -1)
                if at:
                    for i in range(PAIRS_IN):
                        pair(i, i % 2)
                        run(at, i)
                else:
                    with a.Fori(0, PAIRS_IN // 2) as i:
                        for j in range(2):
                            pair(2 * i + j, j)
                if layer == 1:
                    hi_at(base + 24, 0, 0)
                    a.wait_ge(glr_mm, half + 1)
                    a.activation(glr[:, half * HALF:(half + 1) * HALF], bank(5), ACT.Copy).then_inc(glr_done, 1)

            def attention():
                a.wait_ge(lam_dot, 2)

                def split(b, slot, n, last=False):
                    if last:
                        return
                    a.wait_ge(qk_full, 128 * b + 128)
                    c = n // 2
                    dst, src = ((q_split, q_dup), (k_high, k_dup))[n % 2]
                    a.activation(dst[slot][:, c, :], src[:, c, :], ACT.Copy).then_inc(qk_hi, 1)

                def block_(kind, b, slot, last):
                    before = (lambda t: LANE[0] * b + t) if kind == 0 else (lambda t: LANE[0] * 4 + LANE[1] * (b - 4) + t)
                    count = 0

                    def copy_a(dst, m):
                        nonlocal count
                        count += 1
                        a.wait_ge(ta_done, before(count))
                        a.activation(dst, bank(4)[:, 0:m * P].rearrange("p (m q) -> p m q", q=P), ACT.Copy).then_inc(ta_free, 1)

                    def exps(n):
                        for c in range(2):
                            a.wait_ge(nm_done, 16 * b + 2 * n + c + 1)
                            if kind == 0:
                                a.wait_ge(w_done, 8 * b + n + 1)
                            K = P * (n + 1)
                            a.activation(pr[:, c, 0:K], sc[:, c, 0:K], ACT.Exp, bias=nmx[:, 2 * n + c:2 * n + c + 1],
                                         accum_out=rs[:, 2 * n + c:2 * n + c + 1]).then_inc(exp_done, 1)

                    a.wait_ge(pv_done, 8 * b + 1)
                    copy_a(v_tok[:, 0:4, :], 4)
                    exps(0)
                    for n in range(8):
                        for c, lane, k0, m in lanes(kind, n):
                            if lane == 0:
                                a.wait_ge(pv_done, 8 * b + n + 1)
                                copy_a(wT[:, c, k0:k0 + m, :], m)
                        a.wait_ge(td_done, before(lane_count(kind, n + 1, 1)))
                        if n < 7:
                            exps(n + 1)
                        if n < 4:
                            split(b + 1, 1 - slot, n, last)
                    if kind == 0:
                        a.wait_ge(o_done, 8 * b + 8 + 1)
                        a.activation(ms, ms, ACT.Sqrt, bias=eps_c, scale=1.0 / P).then_inc(sub_root, 1)
                    count += 1
                    a.wait_ge(ta_done, before(count))
                    dst = yT[:, b, 0:512] if isinstance(b, int) else yT[:, bass.ds(b, 1), 0:512].rearrange("p u t -> p (u t)")
                    a.activation(dst, bank(4), ACT.Copy if kind else ACT.Identity,
                                 **({} if kind else {"scale": sub_g})).then_inc(ta_free, 1)

                a.wait_ge(unit_used, USE_OUT[0] + 2)
                for n in range(4):
                    split(0, 0, n)
                with a.Fori(0, 2) as i:
                    for s in range(2):
                        block_(0, 2 * i + s, s, False)
                with a.Fori(0, 1) as i:
                    for s in range(2):
                        block_(1, 4 + 2 * i + s, s, False)
                block_(1, 6, 0, False)
                block_(1, 7, 1, True)

            def gated():
                with a.Fori(0, C_HEADS) as h:
                    a.wait_ge(g_z, h + 1)
                    a.activation(gd, ps[:, 0:1024], ACT.Abs, bias=bg2[:, :]).then_inc(g_zread, 1)
                    a.drain()
                    a.activation(gd, gd, ACT.Exp, scale=-1.0)
                    a.drain()
                    a.activation(gd, gd, ACT.Ln, bias=1.0).then_inc(g_sp, 1)
                    for n in range(4):
                        a.wait_ge(g_vt, 4 * h + n + 1)
                        a.activation(gv_tok[:, 2 * n:2 * n + 2, :], bank(4 + n).rearrange("p (i d) -> p i d", i=2), ACT.Copy)\
                            .then_inc(g_vtr, 1)
                    a.wait_ge(g_b, h + 1)
                    a.activation(qe, gb, ACT.Exp, scale=1.0 / C_TAU).then_inc(g_eb, 1)
                    a.activation(eblast, gb.rearrange("p (n t) -> p n t", t=P)[:, :, P - 1], ACT.Exp, scale=1.0 / C_TAU)\
                        .then_inc(g_eb, 1)
                    a.wait_ge(g_ekd, h + 1)
                    a.activation(ke, ke, ACT.Exp, scale=1.0 / C_TAU).then_inc(g_ek, 1)
                    for lv in range(LEVELS):
                        m = 64 >> lv
                        v = gd.rearrange("p (n u t) -> p n u t", u=2, t=m)
                        a.wait_ge(g_d, 7 * h + lv + 1)
                        a.activation(v[:, :, 0, :], v[:, :, 0, :], ACT.Exp, scale=-1.0 / C_TAU)
                        a.activation(v[:, :, 1, :], v[:, :, 1, :], ACT.Exp, scale=1.0 / C_TAU)
                        a.drain().then_inc(g_f, 1)
                        if lv == 0:
                            for n in range(2):
                                a.wait_ge(g_kt, 2 * h + n + 1)
                                a.activation(ke_tok[:, 4 * n:4 * n + 4, :], bank(4 + n).rearrange("p (i d) -> p i d", i=4), ACT.Copy)\
                                    .then_inc(g_ktr, 1)
                    for n in range(8):
                        a.wait_ge(g_o, 8 * h + n + 1)
                        a.activation(gd[:, 0:C_DV], bank(4 + n % 2)[:, 0:C_DV], ACT.Square, accum_out=ms[:, n:n + 1])
                        a.activation(go[:, n, :], bank(4 + n % 2)[:, 0:C_DV], ACT.Copy).then_inc(g_or, 1)
                        a.drain()
                    a.activation(ms, ms, ACT.Sqrt, bias=eps_c, scale=1.0 / C_DV).then_inc(g_root, 1)
                    a.wait_ge(g_r, 16 * h + 16)
                    a.activation(gvr[:, :, :], gvr[:, :, :], ACT.Silu).then_inc(g_silu, 1)

            a.wait_ge(s_const, 128)
            a.activation(cs[:, :], cs[:, :], ACT.Silu).then_inc(cs_done, 1)
            a.wait_ge(setup_done, 1)
            a.wait_ge(lam_dot, 1)
            a.activation(lam2, lam2, ACT.Exp).then_inc(lam_exp, 1)
            square(0, 0, 0, None)
            root(0, 0, 0)
            a.wait_ge(mod_done, 1)
            for k in range(KB):
                modulate(0, 0, 0, k)
                a.drain()
                write_h(k, y3[:, k, :], 0)
            for layer in range(2):
                project(layer, 0)
                for k in range(KB):
                    write_h(k, y3[:, k, :], in_base(layer, 1))
                project(layer, 1)
                if layer == 0:
                    attention()
                    a.wait_ge(ta_free, 4 * sum(LANE) + 1)
                    a.wait_ge(td_free, 4 * sum(LANE) + 1)
                else:
                    gated()
                    a.wait_ge(g_yt, 4 * C_HEADS + 1)
                for half in range(2):
                    base = USE_OUT[layer] + KB * half
                    for k in range(KB):
                        write_h(k, yT[:, k, half * HALF:(half + 1) * HALF], base)
                        if k in (3, 7) and not half:
                            hi_at(base, 0, k // 4)
                    at = hooks(layer, "out", half)
                    if half:
                        hi_at(base, 0, 0)
                        hi_at(base, 0, 1)
                    run(at, -1)
                    for i in range(PAIRS_OUT):
                        for s in range(2):
                            if i:
                                hi_at(base, i, s)
                        run(at, i - 0.5)
                        a.wait_ge(unit_used, base + 2 * i + 3)
                        a.activation((y3, y_out1)[half][:, 2 * i, :], bank(2 * (i % 2)), ACT.Copy).then_inc(free0, 1)
                        run(at, i)
                for k in range(KB):
                    write_h(k, y3[:, k, :], ffn_base(layer, 0))
                for half in range(2):
                    base, tiles, d = ffn_base(layer, half), T_FFN[layer] + FB * half, dn_idx(layer, half)

                    def pair(i, j):
                        for s in range(2):
                            hi_at(base, i, s)
                        a.wait_ge(unit_used, base + 2 * i + 3)
                        a.wait_ge(free1, tiles + i)
                        a.activation(exp_buf[j], bank(2 * j), ACT.Exp, scale=-1.0).then_inc(exp_g, 1)

                    at = hooks(layer, "ffn", half)
                    run(at, -1)
                    for i in range(6):
                        pair(i, i % 2)
                        run(at, i)
                    with a.Fori(3, FB // 2) as i:
                        for j in range(2):
                            pair(2 * i + j, j)
                    base += 2 * FB
                    for u in range(FB):
                        hi_at(base, u // 2, u % 2)
                        if u == 0:
                            a.wait_ge(free1, tiles + FB + 1)
                        a.activation(a_hi[:, u % 2, :], act[:, u, :], ACT.Copy).then_inc(ah_done, 1)
                        if (layer, half) != (1, 1):
                            nl, nk, nh = (layer, 2, 1) if half == 0 else (1, 0, 0)
                            if u % 2 == 0 and u < 16:
                                modulate(nl, nk, nh, u // 2)
                            if u % 2 and 2 < u < 19:
                                a.drain()
                                write_h((u - 3) // 2, y3[:, (u - 3) // 2, :], base)
                    a.wait_ge(unit_used, base + FB + 2)
                    if (layer, half) != (1, 1):
                        a.wait_ge(hl_done, 8 * (h_job(nl, nk, nh) + 1))
                    for m in range(0, KB, 2):
                        a.activation(y3[:, m, :], bank(m), ACT.Copy).then_inc(dn_ev0, 1)
            square(1, 3, 1, y3)
            root(1, 3, 1)

        @block.vector
        def _(v):
            for count in (free1, s_read[0], s_read[1], td_free, o_done, v_read, blk_done, w_done, g_st, g_yt, g_pred,
                          ada_used):
                v.sem_inc(count, 1)

            def sum_squares(layer, kind, half):
                n = stat_job(layer, kind, half)
                r = rinv[:, rinv_slot(kind, half), :]
                v.wait_ge(sq_done, n + 1)
                v.tensor_reduce(r, (sq if n else y3).rearrange("p k t -> p t k"), axis=AX.X, op=ALU.add).then_inc(ssum_done, 1)

            def inverse(layer, kind, half):
                r = rinv[:, rinv_slot(kind, half), :]
                v.wait_ge(root_done, stat_job(layer, kind, half) + 1)
                v.reciprocal(r, r)
                v.drain()

            def xn(layer, kind, half, k):
                v.tensor_tensor(y3[:, k, :], x[:, k, half * HALF:(half + 1) * HALF], rinv[:, half, :], ALU.mult)\
                    .then_inc(xn_done, 1)

            def h_low(job, k, src):
                v.wait_ge(hh_done, 8 * job + k + 1)
                v.tensor_tensor(h_lo[:, k, :], src, h_hi[:, k, :].bitcast(f32), ALU.subtract).then_inc(hl_done, 1)

            def normed(layer, kind, half):
                for k in range(KB):
                    xn(layer, kind, half, k)

            def low(layer, kind, half, src):
                for k in range(KB):
                    h_low(h_job(layer, kind, half), k, src[:, k, :])

            def scaled(y):
                v.tensor_tensor(y, y, bcast_k(rinv[:, 2, :]), ALU.mult)

            def update(layer, kind, half, y):
                g = 8 * (4 * layer + kind)
                v.drain()
                for k in range(KB):
                    xs = x[:, k, half * HALF:(half + 1) * HALF]
                    v.scalar_tensor_tensor(xs, y[:, k, :], gain[:, g + k:g + k + 1], xs, ALU.mult, ALU.add)
                v.drain().then_inc(x_upd, 1)

            def hooks(layer, phase, half):
                post, pre = hosted(layer, phase, half)
                at = {}

                def put(n, f, *args):
                    at.setdefault(n, []).append((f, args))
                out = phase == "out"
                if post:
                    put(-1, sum_squares, *post[0])
                    put(0 if out else 1, inverse, *post[0])
                    put(0 if out else 1, scaled, post[1])
                    put(1 if out else 2, update, *post[0], post[1])
                if pre:
                    put(2 if out else 3, sum_squares, *pre)
                    put(2 if out else 5, inverse, *pre)
                    if phase == "in":
                        put(6, normed, *pre)
                    if out:
                        put(2, normed, *pre)
                return at

            def run(at, n):
                for f, args in at.get(n, []):
                    f(*args)

            def bcast_k(row):
                return row.rearrange("p (u t) -> p u t", u=1).broadcast_to([P, KB, HALF])

            def ada_unit(g, k, s, pair):
                v.wait_ge(ada_full[s], 16 * (pair - 8) + 16)
                v.scalar_tensor_tensor(ada_acc_at(g), ada_raw[:, s, :], cs[:, k:k + 1], ada_acc_at(g),
                                       ALU.mult, ALU.add).then_inc(ada_used, 1)
                v.drain()

            def ada_acc_at(g):
                if isinstance(g, int):
                    return ada_acc[:, g, :]
                return ada_acc[:, bass.ds(g, 1), :].rearrange("p u n -> p (u n)")

            def columns(n, first, groups):
                v.drain().then_inc(acc_done, 1)
                v.wait_ge(ada_mm, n + 1)
                w = 8 * groups
                v.tensor_tensor(mod[:, 8 * first:8 * first + w], bank(6, w), ada_b[:, 8 * first:8 * first + w], ALU.add)
                v.drain()
                for grp in range(first, first + groups):
                    layer, g = divmod(grp, 6)
                    if g in (1, 2, 4, 5):
                        o = 8 * (4 * layer + {1: 0, 2: 1, 4: 2, 5: 3}[g])
                        v.scalar_tensor_tensor(gain[:, o:o + 8], mod[:, 8 * grp:8 * grp + 8], 1.0, ng[:, o:o + 8],
                                               ALU.add, ALU.mult)
                v.drain().then_inc(mod_done, 1)

            def project(layer, half):
                base, tiles = in_base(layer, half), T_IN[layer] + PAIRS_IN * half
                st = PAIRS_IN * (2 * layer + half)
                ada0 = [[8, 20], [32, 44]][layer][half]
                groups = [[3, 3], [3, 1]][layer][half]
                v.memset(ada_acc[:, 0:groups, :], 0.0)
                v.drain()

                def tile(i, j):
                    v.wait_ge(unit_used, base + 2 * i + 4)
                    v.wait_ge(st_done, 16 * (st + i) + 16)
                    v.tensor_copy(stage[:, 1, :], bank(2 * j + 1)).then_inc(free1, 1)

                at = hooks(layer, "in", half)

                def group(g):
                    for j in range(4):
                        for s in range(2):
                            ada_unit(g, 2 * j + s, s, ada0 + 4 * g + j)
                        tile(4 * g + j, j % 2)
                        if at:
                            run(at, 4 * g + j)

                run(at, -1)
                if at:
                    for g in range(groups):
                        group(g)
                else:
                    with v.Fori(0, groups) as g:
                        group(g)
                if groups < 3:
                    with v.Fori(2 * groups, PAIRS_IN // 2) as i:
                        for j in range(2):
                            tile(2 * i + j, j)
                columns(1 + 2 * layer + half, ada0 // 4, groups)

            def attention():
                v.memset(slope[:, 0:1], 1.0)
                v.drain()
                v.wait_ge(tab_full, 32)

                def block_(kind, b):
                    before = (lambda t: LANE[0] * b + t) if kind == 0 else (lambda t: LANE[0] * 4 + LANE[1] * (b - 4) + t)
                    count = 0

                    def copy_d(dst, m):
                        nonlocal count
                        count += 1
                        v.wait_ge(td_done, before(count))
                        v.tensor_copy(dst, bank(5)[:, 0:m * P].rearrange("p (m q) -> p m q", q=P)).then_inc(td_free, 1)

                    def biased(n):
                        for c in range(2):
                            K = P * (n + 1)
                            col = 2 * n + c
                            v.wait_ge(s_done[c], 8 * b + n + 1)
                            v.wait_ge(exp_done, 16 * b + max(0, 2 * n - 1 + c) + 1)
                            v.sem_inc(waited, 1)
                            v.tensor_tensor_reduce(out=sc[:, c, 0:K], in0=ps[:, c * 1024:c * 1024 + K],
                                                   in1=bias[:, c if kind else 0, 1024 - K:1024], scale=SCORE_SCALE,
                                                   scalar=-3.0e38, op0=ALU.add, op1=ALU.max,
                                                   accum_out=mx[:, col:col + 1]).then_inc(s_read[c], 1)
                            v.drain()
                            v.tensor_scalar(nmx[:, col:col + 1], mx[:, col:col + 1], -1.0, None, ALU.mult).then_inc(nm_done, 1)

                    v.tensor_scalar(slope[:, 0:1], slope[:, 0:1], 0.25, None, ALU.mult)
                    v.drain()
                    if kind == 1:
                        v.tensor_scalar(slope[:, 1:2], slope[:, 0:1], 0.5, None, ALU.mult)
                        v.drain()
                    for c in range(kind + 1):
                        v.scalar_tensor_tensor(bias[:, c, :], dist, slope[:, c:c + 1], mask_bias, ALU.mult, ALU.add)
                    v.drain()
                    v.wait_ge(pv_done, 8 * b + 1)
                    copy_d(v_tok[:, 4:8, :], 4)
                    v.drain().then_inc(v_read, 1)
                    biased(0)
                    for n in range(8):
                        a0 = 2 * n
                        v.wait_ge(exp_done, 16 * b + 2 * n + 2 + 1)
                        if kind == 0:
                            v.reciprocal(r0[:, a0:a0 + 2], rs[:, a0:a0 + 2])
                            v.drain()
                            v.scalar_tensor_tensor(coef, r0[:, a0 + 1:a0 + 2], neglam, rs[:, a0:a0 + 1], ALU.mult, ALU.mult)
                            v.drain()
                            K = P * (n + 1)
                            v.scalar_tensor_tensor(pr[:, 0, 0:K], pr[:, 1, 0:K], coef, pr[:, 0, 0:K], ALU.mult, ALU.add)\
                                .then_inc(w_done, 1)
                        else:
                            v.reciprocal(r0[:, a0:a0 + 2], rs[:, a0:a0 + 2])
                        if n < 7:
                            biased(n + 1)
                        for c, lane, k0, m in lanes(kind, n):
                            if lane == 1:
                                v.wait_ge(pv_done, 8 * b + n + 1)
                                copy_d(wT[:, c, k0:k0 + m, :], m)
                        v.drain()
                        v.wait_ge(pv_done, 8 * b + n + 1 + 1)
                        if kind == 0:
                            v.tensor_scalar(o_sb[:, n, :], bank(6, P), r0[:, a0:a0 + 1], None, ALU.mult)
                            v.drain()
                            v.tensor_tensor_reduce(out=junk, in0=o_sb[:, n, :], in1=o_sb[:, n, :], scale=1.0, scalar=0.0,
                                                   op0=ALU.mult, op1=ALU.add, accum_out=ms[:, n:n + 1])
                        else:
                            for c in range(2):
                                v.tensor_scalar(o_sb[:, n, 64 * c:64 * c + 64], bank(6)[:, 192 * c:192 * c + 64],
                                                r0[:, a0 + c:a0 + c + 1], None, ALU.mult)
                        v.drain().then_inc(o_done, 1)
                    if kind == 0:
                        v.wait_ge(sub_root, b + 1)
                        v.reciprocal(ms, ms)
                        v.drain()
                        v.tensor_scalar(ms, ms, 1.0 - LAM_INIT, None, ALU.mult)
                        v.drain()
                        v.tensor_tensor(o_sb, o_sb, ms.rearrange("p (n u) -> p n u", u=1).broadcast_to([P, 8, P]), ALU.mult)
                    v.drain().then_inc(o_ready, 1)
                    count += 1
                    v.wait_ge(td_done, before(count))
                    dst = yT[:, bass.ds(b, 1), 512:1024].rearrange("p u t -> p (u t)")
                    if kind == 0:
                        v.tensor_scalar(dst, bank(5), sub_g, None, ALU.mult).then_inc(td_free, 1)
                    else:
                        v.tensor_copy(dst, bank(5)).then_inc(td_free, 1)
                    v.drain().then_inc(blk_done, 1)

                v.drain().then_inc(blk_done, 1)
                for kind in range(2):
                    if kind == 1:
                        v.wait_ge(tab_full, 48)
                        v.memset(slope[:, 0:1], 2.0)
                        v.drain()
                    with v.Fori(0, 2) as i:
                        for s in range(2):
                            block_(kind, 4 * kind + 2 * i + s)

            def gated():
                v.wait_ge(st_done, 16 * 4 * PAIRS_IN + 16)
                v.memset(attnT, 0.0)
                v.drain()
                chunk = lambda t: t.rearrange("p (n t) -> p n t", t=P)
                with v.Fori(0, C_HEADS) as h:
                    v.wait_ge(g_w, 32 * h + 32)
                    v.wait_ge(g_zread, 2 * h + 1)
                    v.tensor_scalar(gb, ps[:, 0:1024], bg2[:, :], 0.0, ALU.add, ALU.min).then_inc(g_zread, 1)
                    v.wait_ge(g_qk, 32 * h + 32)
                    v.tensor_scalar(gq, gq, C_DK ** -0.5, None, ALU.mult)
                    v.drain()
                    v.wait_ge(g_sp, h + 1)
                    v.tensor_tensor(gb, gb, gd, ALU.subtract)
                    v.drain()
                    for n in range(8):
                        v.tensor_tensor_scan(gx[:, 0, n * P:(n + 1) * P], ones[:, :], gb[:, n * P:(n + 1) * P], 0.0, ALU.mult, ALU.add)
                    v.drain()
                    v.tensor_copy(gb, gx[:, 0, :]).then_inc(g_b, 1)
                    v.drain()
                    v.tensor_tensor(chunk(ke), chunk(gb)[:, :, P - 1:P].broadcast_to([P, 8, P]), chunk(gb), ALU.subtract).then_inc(g_ekd, 1)

                    def masked(lv):
                        v.drain()
                        v.wait_ge(g_s, 8 * h + lv + 1)
                        v.sem_inc(waited, 1)
                        for n in range(2):
                            v.copy_predicated(attnT[:, 4 * n:4 * n + 4, :],
                                              masks[:, lv:lv + 1, :].broadcast_to([P, 4, P]),
                                              bank(2 * (lv % 2) + n).rearrange("p (n i) -> p n i", i=P)).then_inc(g_pred, 1)

                    for lv in range(LEVELS):
                        m = 64 >> lv
                        b4 = gb.rearrange("p (n t) -> p n t", t=2 * m)
                        v.tensor_tensor(gd.rearrange("p (n t) -> p n t", t=2 * m), b4,
                                        b4[:, :, m - 1:m].broadcast_to([P, S // (2 * m), 2 * m]), ALU.subtract).then_inc(g_d, 1)
                        if lv == 0:
                            v.wait_ge(g_eb, 2 * h + 2)
                            v.tensor_tensor(qe, qe, gq, ALU.mult).then_inc(g_qk_done, 1)
                            v.wait_ge(g_ek, h + 1)
                            v.tensor_tensor(ke, ke, gk, ALU.mult).then_inc(g_qk_done, 1)
                        if lv > 0:
                            masked(lv - 1)
                        half4 = lambda t: t.rearrange("p (n u t) -> p n u t", u=2, t=m)
                        v.wait_ge(g_f, 7 * h + lv + 1)
                        v.tensor_tensor(half4(gx[:, lv % 2, :])[:, :, 0, :], half4(gd)[:, :, 0, :], half4(gk)[:, :, 0, :], ALU.mult)
                        v.tensor_tensor(half4(gx[:, lv % 2, :])[:, :, 1, :], half4(gd)[:, :, 1, :], half4(gq)[:, :, 1, :], ALU.mult)
                        v.drain().then_inc(g_x, 1)
                    v.drain().then_inc(g_x, 1)
                    masked(LEVELS - 1)
                    masked(LEVELS)
                    for n in range(7):
                        v.wait_ge(g_u, 7 * h + n + 1)
                        if n == 0:
                            v.tensor_copy(state, bank(6)[:, 0:C_DV]).then_inc(g_st, 1)
                        else:
                            v.sem_inc(waited, 1)
                            v.drain()
                            v.wait_ge(g_o, 8 * h + n + 1)
                            v.scalar_tensor_tensor(state, state, eblast[:, n:n + 1], bank(6 + n % 2)[:, 0:C_DV],
                                                   ALU.mult, ALU.add).then_inc(g_st, 1)
                    v.drain().then_inc(g_st, 1)
                    v.wait_ge(g_root, h + 1)
                    v.reciprocal(ms, ms)
                    v.drain()
                    v.tensor_tensor(go, go, ms.rearrange("p (n u) -> p n u", u=1).broadcast_to([P, 8, C_DV]), ALU.mult).then_inc(g_on, 1)
                    v.wait_ge(g_silu, h + 1)
                    for b in range(2):
                        for n in range(2):
                            v.wait_ge(g_ot, 4 * h + 2 * b + n + 1)
                            dst = yT[:, bass.ds(2 * h + b, 1), n * 512:(n + 1) * 512].rearrange("p u t -> p (u t)")
                            v.scalar_tensor_tensor(dst, bank(2 * b + n), hg[:, b:b + 1], gvr[:, b, n * 512:(n + 1) * 512],
                                                   ALU.mult, ALU.mult).then_inc(g_yt, 1)

            junk = arena[:, 20480:20608]
            v.memset(mean_w[:, :], 1.0 / D)
            v.memset(ones[:, :], 1.0)
            v.memset(wg2[:, :], 0.0)
            v.memset(eps_c, EPS)
            v.drain().then_inc(setup_done, 1)
            v.wait_ge(s_const, 128)
            v.tensor_copy(masks.rearrange("p l i -> p (l i)"), mask_f)
            for i in range(2):
                v.tensor_tensor_reduce(out=junk[:, 64 * i:64 * i + 64], in0=lamv[:, 128 * i:128 * i + 64], in1=lamv[:, 128 * i + 64:128 * i + 128],
                                       scale=1.0, scalar=0.0, op0=ALU.mult, op1=ALU.add, accum_out=lam2[:, i:i + 1])
            v.drain().then_inc(lam_dot, 1)
            v.wait_ge(lam_exp, 1)
            v.tensor_tensor(neglam, lam2[:, 1:2], lam2[:, 0:1], ALU.subtract)
            v.drain()
            v.tensor_scalar(neglam, neglam, -LAM_INIT, None, ALU.add)
            v.drain().then_inc(lam_dot, 1)
            v.wait_ge(cs_done, 1)
            for g in range(2):
                for k in range(KB):
                    v.wait_ge(ada_big[2 * g + k // 4], 16)
                    if k == 0:
                        v.tensor_scalar(acc_first[:, g, :], ada_first[:, g, k, :], cs[:, k:k + 1], None, ALU.mult)
                    else:
                        v.scalar_tensor_tensor(acc_first[:, g, :], ada_first[:, g, k, :], cs[:, k:k + 1], acc_first[:, g, :],
                                               ALU.mult, ALU.add)
                    v.drain()
                if g == 0:
                    sum_squares(0, 0, 0)
            columns(0, 0, 2)
            inverse(0, 0, 0)
            normed(0, 0, 0)
            low(0, 0, 0, y3)
            for layer in range(2):
                project(layer, 0)
                low(layer, 0, 1, y3)
                project(layer, 1)
                if layer == 0:
                    attention()
                else:
                    gated()
                for half in range(2):
                    base = USE_OUT[layer] + KB * half
                    low(layer, 1, half, yT[:, :, half * HALF:(half + 1) * HALF])
                    at = hooks(layer, "out", half)
                    run(at, -1)
                    for i in range(PAIRS_OUT):
                        v.wait_ge(unit_used, base + 2 * i + 4)
                        v.tensor_copy((y3, y_out1)[half][:, 2 * i + 1, :], bank(2 * (i % 2) + 1)).then_inc(free1, 1)
                        run(at, i)
                low(layer, 2, 0, y3)
                for half in range(2):
                    base, tiles, d = ffn_base(layer, half), T_FFN[layer] + FB * half, dn_idx(layer, half)

                    def pair(i, j):
                        e = exp_buf[j]
                        v.wait_ge(exp_g, FB * d + i + 1)
                        v.tensor_scalar(e, e, 1.0, None, ALU.add)
                        v.drain()
                        v.reciprocal(e, e)
                        v.drain()
                        v.tensor_tensor(e, bank(2 * j), e, ALU.mult).then_inc(free0, 1)
                        v.drain()
                        v.wait_ge(unit_used, base + 2 * i + 4)
                        dst = act[:, i, :] if isinstance(i, int) else act[:, bass.ds(i, 1), :].rearrange("p u t -> p (u t)")
                        v.tensor_tensor(dst, e, bank(2 * j + 1), ALU.mult).then_inc(free1, 1)

                    at = hooks(layer, "ffn", half)
                    run(at, -1)
                    for i in range(6):
                        pair(i, i % 2)
                        run(at, i)
                    with v.Fori(3, FB // 2) as i:
                        for j in range(2):
                            pair(2 * i + j, j)
                    base += 2 * FB
                    ahead = (layer, half) != (1, 1)
                    nl, nk, nh = (layer, 2, 1) if half == 0 else (1, 0, 0)
                    for u in range(FB):
                        v.wait_ge(ah_done, FB * d + u + 1)
                        v.tensor_tensor(a_lo[:, u % 2, :], act[:, u, :], a_hi[:, u % 2, :].bitcast(f32), ALU.subtract)\
                            .then_inc(al_done, 1)
                        if ahead and u % 2 == 0 and u < 16:
                            xn(nl, nk, nh, u // 2)
                        if ahead and u % 2 and 3 < u < 20:
                            h_low(h_job(nl, nk, nh), (u - 5) // 2, y3[:, (u - 5) // 2, :])
                    v.wait_ge(unit_used, base + FB + 2)
                    for m in range(1, KB, 2):
                        v.tensor_copy(y3[:, m, :], bank(m)).then_inc(dn_ev1, 1)
            sum_squares(1, 3, 1)
            inverse(1, 3, 1)
            scaled(y3)
            update(1, 3, 1, y3)


def kernel(x, c, ada_w, ada_b, norm_g, ev_w_in, ev_lambda, ev_subln_g, ev_w_out, od_w_in, od_w_g2, od_b_g2,
           od_head_g, od_w_out, ffn_w_gate, ffn_w_up, ffn_w_down):
    import concourse.bacc as bacc
    from concourse.bass_utils import run_bass_kernel_spmd

    f = np.float32
    x, c, ada_w, ada_b, norm_g = (np.asarray(t) for t in (x, c, ada_w, ada_b, norm_g))
    ffn = [np.asarray(t) for t in (ffn_w_gate, ffn_w_up, ffn_w_down)]

    def columns_units(w):
        w = np.asarray(w)
        n = w.shape[1] // P
        return w.reshape(KB, P, n, P).transpose(2, 1, 0, 3).reshape(n, P, KB * P)

    pack = np.zeros((PACK_UNITS, P, 1024), f)
    for layer, (w_in, w_out) in enumerate(((ev_w_in, ev_w_out), (od_w_in, od_w_out))):
        w_in = np.asarray(w_in)[0]
        pack[PACK_IN[layer]:PACK_IN[layer] + 24] = columns_units(w_in[:, :3072])
        if layer == 1:
            last = w_in[:, 3072:].reshape(KB, P, C_RANK).transpose(1, 0, 2)
            pack[PACK_IN[1] + 24].reshape(P, KB, P)[:, :, :C_RANK] = last
        pack[PACK_OUT[layer]:PACK_OUT[layer] + KB] = columns_units(np.asarray(w_out)[0])
        at = PACK_FFN[layer]
        pack[at:at + 2 * FB:2] = columns_units(ffn[0][layer])
        pack[at + 1:at + 2 * FB:2] = columns_units(ffn[1][layer])
        pack[at + 2 * FB:at + 3 * FB] = ffn[2][layer].reshape(FB, P, D)

    d = 896.0 + np.arange(P)[:, None] - np.arange(S)[None, :]
    copies = (d <= 128).astype(int) + ((d % 4 == 0) & (d <= 512)) + (d % 16 == 0)
    reach = (d >= 0) & (copies > 0)
    dilated = np.where(reach, np.log(np.maximum(copies, 1)) / SCORE_SCALE, MASKED)
    levels = np.zeros((P, 8, P), f)
    j, i = np.arange(P)[:, None], np.arange(P)[None, :]
    for lv in range(LEVELS):
        m = 64 >> lv
        levels[:, lv] = (j // (2 * m) == i // (2 * m)) & (j % (2 * m) < m) & (i % (2 * m) >= m)
    levels[:, LEVELS] = i == j

    arrays = {
        "xT": x[0].T, "cT": c[0].reshape(KB, P).T, "weights": pack,
        "ada_w": ada_w.reshape(2, KB, P, 6, D).transpose(0, 3, 1, 2, 4).reshape(96, P, D),
        "ada_bT": ada_b.reshape(96, P).T, "norm_gT": norm_g.reshape(64, P).T,
        "lam_p": np.broadcast_to(np.asarray(ev_lambda).reshape(1, 4 * HEAD_DIM), (P, 4 * HEAD_DIM)),
        "subln_g": np.asarray(ev_subln_g).reshape(P, 1),
        "w_g2": np.asarray(od_w_g2)[0].reshape(C_RANK, C_HEADS, P).transpose(1, 0, 2),
        "b_g2": np.asarray(od_b_g2)[0].reshape(C_HEADS, P, 1),
        "head_g": np.asarray(od_head_g)[0].reshape(2, P).T,
        "identity": np.eye(P, dtype=f), "distance": (-d / SCORE_SCALE).astype(f),
        "causal_bias": np.where(d >= 0, 0.0, MASKED).astype(f), "dilated_bias": dilated.astype(f),
        "level_masks": levels,
    }
    arrays = {k: np.ascontiguousarray(a) for k, a in arrays.items()}
    nc = bacc.Bacc("TRN2", target_bir_lowering=False, num_devices=1)
    args = [nc.dram_tensor(k, a.shape, mybir.dt.from_np(a.dtype), kind="ExternalInput").ap() for k, a in arrays.items()]
    args.append(nc.dram_tensor("outT", (D, S), mybir.dt.float32, kind="ExternalOutput").ap())
    trunk_kernel(nc, *args)
    r = run_bass_kernel_spmd(nc, [arrays], core_ids=[0])
    return np.ascontiguousarray(r.results[0]["outT"].T)[None]
```

```python
from contextlib import ExitStack
import math

import numpy as np

import concourse.bass as bass
from concourse import mybir

D = 1024
S = 1024
P = 128
KB = D // P
HALF = S // 2
A_HEADS, B_HEADS, HEAD_DIM = 4, 8, 64
C_HEADS, C_DK, C_DV, C_RANK, C_TAU = 4, 128, 256, 16, 16.0
FFN = 2816
FB = FFN // P
NIN = [24, 25]
EPS = 1e-6
SCORE_SCALE = HEAD_DIM ** -0.5
LAM_INIT = 0.8 - 0.6 * math.exp(-0.3 * 0)
LEVELS = 7
MASKED = -1e30

FFN_UNITS = 3 * FB
PACK_IN = [0, NIN[0] + KB + FFN_UNITS]
PACK_OUT = [PACK_IN[0] + NIN[0], PACK_IN[1] + NIN[1]]
PACK_FFN = [PACK_OUT[0] + KB, PACK_OUT[1] + KB]
PACK_UNITS = PACK_FFN[1] + FFN_UNITS
USE_IN, USE_OUT, USE_FFN = [0, 0], [0, 0], [0, 0]
USE_OUT[0] = 2 * NIN[0]
USE_FFN[0] = USE_OUT[0] + 2 * KB
USE_IN[1] = USE_FFN[0] + 2 * FFN_UNITS
USE_OUT[1] = USE_IN[1] + 2 * NIN[1]
USE_FFN[1] = USE_OUT[1] + 2 * KB
PAIRS_IN, PAIRS_OUT = 12, KB // 2
T_IN = [0, 2 * PAIRS_IN + 2 * PAIRS_OUT + 2 * FB]
T_OUT = [T_IN[0] + 2 * PAIRS_IN, T_IN[1] + 2 * PAIRS_IN]
T_FFN = [T_OUT[0] + 2 * PAIRS_OUT, T_OUT[1] + 2 * PAIRS_OUT]


def trunk_kernel(nc, xT, cT, weights, ada_w, ada_bT, norm_gT, lam_p, subln_g, w_g2, b_g2, head_g,
                 identity, distance, causal_bias, dilated_bias, level_masks, outT):
    f32, f32r, u8 = mybir.dt.float32, mybir.dt.float32r, mybir.dt.uint8
    ALU, ACT, AX = mybir.AluOpType, mybir.ActivationFunctionType, mybir.AxisListType

    ctx = ExitStack()
    with ctx:
        def sb(name, shape, dt=f32):
            return ctx.enter_context(nc.sbuf_tensor(name, shape, dt))

        def sem(name):
            return ctx.enter_context(nc.semaphore(name))

        proj = nc.dram_tensor("proj", [24, P, S], f32, kind="Internal").ap()
        x = sb("x", [P, KB, S])
        h_hi = sb("h_hi", [P, KB, HALF], f32r)
        h_lo = sb("h_lo", [P, KB, HALF], f32r)
        w_raw = sb("w_raw", [P, 2, 1024])
        w_hi = sb("w_hi", [P, 2, 1024], f32r)
        w_lo = sb("w_lo", [P, 2, 1024], f32r)
        a_hi = sb("a_hi", [P, 2, HALF], f32r)
        a_lo = sb("a_lo", [P, 2, HALF], f32r)
        ybuf = sb("ybuf", [P, 8 * HALF])
        arena = sb("arena", [P, 20736])
        glr = sb("glr", [P, S])
        rinv = sb("rinv", [P, 3, HALF])
        ident = sb("ident", [P, P])
        mean_w = sb("mean_w", [P, P])
        ones = sb("ones", [P, P])
        masks = sb("masks", [P, 8, P], u8)
        wg2 = sb("wg2", [P, P])
        bg2 = sb("bg2", [P, 1])
        cs = sb("cs", [P, KB])
        ada_b = sb("ada_b", [P, 96])
        mod = sb("mod", [P, 96])
        ng = sb("ng", [P, 64])
        gain = sb("gain", [P, 64])
        small = sb("small", [P, 128])
        ps = ctx.enter_context(nc.psum_tensor("ps", [P, 4096], f32))

        def bank(b, n=512):
            return ps[:, b * 512:b * 512 + n]

        y3 = ybuf[:, :].rearrange("p (k t) -> p k t", k=KB)
        yT = arena[:, 0:8192].rearrange("p (k t) -> p k t", k=KB)
        act = arena[:, 0:FB * HALF].rearrange("p (k t) -> p k t", k=FB)
        exp_buf = [arena[:, 11264:11776], arena[:, 19968:20480]]
        sq = arena[:, 11776:15872].rearrange("p (k t) -> p k t", k=KB)
        y_out1 = arena[:, 15872:19968].rearrange("p (k t) -> p k t", k=KB)
        ada_first = arena[:, 0:16384].rearrange("p (g u n) -> p g u n", g=2, u=KB)
        acc_first = arena[:, 16384:18432].rearrange("p (g n) -> p g n", g=2)
        lamv, mask_f = arena[:, 18432:18688], arena[:, 18688:19712]
        stage = arena[:, 0:1024].rearrange("p (s t) -> p s t", s=2)
        ada_raw = arena[:, 1024:3072].rearrange("p (s n) -> p s n", s=2)
        ada_acc = arena[:, 3072:6144].rearrange("p (g n) -> p g n", g=3)
        q_dup = arena[:, 8192:10240].rearrange("p (c t) -> p c t", c=2)
        k_dup = arena[:, 10240:12288].rearrange("p (c t) -> p c t", c=2)
        hf, lf = (t[:, :, :].rearrange("p k t -> p (k t)") for t in (h_hi, h_lo))
        wf, wg = (t[:, :, :].rearrange("p k t -> p (k t)") for t in (w_hi, w_lo))
        two = lambda t: t.rearrange("p (c t) -> p c t", c=2)
        q_split = [two(hf[:, 0:2048]), two(lf[:, 2048:4096])]
        k_high = [two(hf[:, 2048:4096]), two(wf)]
        k_low = [two(lf[:, 0:2048]), two(wg)]
        v_sb = arena[:, 12288:13312]
        v_tok = arena[:, 13312:14336].rearrange("p (n d) -> p n d", d=P)
        keys = lambda t: t.rearrange("p (k q) -> p k q", q=P)
        wT = [[keys(arena[:, 14336:15360]), keys(arena[:, 15360:16384])],
              [keys(w_raw[:, s, :]) for s in range(2)]]
        dist = arena[:, 16384:17408]
        mask_bias = arena[:, 17408:18432]
        bias = arena[:, 18432:20480].rearrange("p (c k) -> p c k", c=2)
        pr = [ybuf[:, t:t + 2048].rearrange("p (c k) -> p c k", c=2) for t in (0, 2048)]
        junk = arena[:, 20480:20608]
        o_sb = glr[:, :].rearrange("p (n d) -> p n d", d=P)
        gq = arena[:, 8192:9216]
        gk = arena[:, 9216:10240]
        gvr = arena[:, 10240:12288].rearrange("p (b t) -> p b t", b=2)
        gb = arena[:, 12288:13312]
        gd = arena[:, 13312:14336]
        g_dif = [gd, ybuf[:, 2048:3072]]
        gx = arena[:, 14336:16384].rearrange("p (s t) -> p s t", s=2)
        attnT = arena[:, 16384:17408].rearrange("p (n i) -> p n i", i=P)
        qe = arena[:, 17408:18432]
        ke = arena[:, 18432:19456]
        ke_tok = arena[:, 19456:20480].rearrange("p (n d) -> p n d", d=P)
        state = arena[:, 20480:20736]
        gv_tok = ybuf[:, 0:2048].rearrange("p (n d) -> p n d", d=C_DV)
        go = ybuf[:, 2048:4096].rearrange("p (n d) -> p n d", d=C_DV)
        mx, nmx, rs = small[:, 0:16], small[:, 16:32], small[:, 32:48]
        r0, ms = small[:, 48:64], small[:, 64:72]
        coef, neglam = small[:, 72:73], small[:, 73:74]
        slope = small[:, 74:76]
        lam2 = small[:, 76:78]
        eps_c = small[:, 78:79]
        sub_g = small[:, 79:80]
        hg = small[:, 80:82]
        eblast = small[:, 82:90]
        unused = small[:, 90:91]

        s_const, s_x = sem("consts_loaded"), [sem("x_loaded0"), sem("x_loaded1")]
        ada_big = [sem(f"ada_first{i}") for i in range(4)]
        raw_full = [sem("raw_full0"), sem("raw_full1")]
        hi_done, lo_done = sem("w_hi_done"), sem("w_lo_done")
        unit_used = sem("unit_used")
        free0, free1 = sem("even_tile_read"), sem("odd_tile_read")
        exp_g = sem("exp_gate_done")
        st_done = sem("proj_stored")
        ah_done, al_done = sem("a_hi_done"), sem("a_lo_done")
        dn_done, dn_ev0, dn_ev1 = sem("down_done"), sem("down_read_act"), sem("down_read_dve")
        xn_done, hh_done, hl_done = sem("xn_done"), sem("h_hi_done"), sem("h_lo_done")
        sq_done, ssum_done, mean_done = sem("square_done"), sem("square_summed"), sem("mean_done")
        root_done, x_upd = sem("root_done"), sem("x_updated")
        ada_full = [sem("ada_full0"), sem("ada_full1")]
        ada_used, acc_done, ada_mm, mod_done = sem("ada_used"), sem("ada_summed"), sem("ada_mm"), sem("mod_done")
        cs_done, setup_done, lam_dot, lam_exp = sem("silu_c_done"), sem("setup_done"), sem("lam_dot"), sem("lam_exp")
        glr_mm, glr_done = sem("gate_rank_mm"), sem("gate_rank_done")
        outs, x_final = sem("out_stored"), sem("x_final_blocks")
        tab_full = sem("bias_tables")
        qk_full, qk_hi, qk_lo = sem("qk_full"), sem("qk_high"), sem("qk_low")
        v_full, v_read = sem("v_full"), sem("v_read")
        s_done = [sem("scores0"), sem("scores1")]
        s_read = [sem("scores_read0"), sem("scores_read1")]
        nm_done, exp_done, w_done = sem("neg_max"), sem("exp_done"), sem("weights_done")
        ta_done, ta_free = sem("turned_a"), sem("turned_a_read")
        td_done, td_free = sem("turned_d"), sem("turned_d_read")
        pv_done, o_done = sem("pv_done"), sem("o_read")
        sub_root, o_ready, blk_done = sem("sub_root"), sem("o_ready"), sem("block_done")
        g_qk, g_v, g_r, g_w = sem("g_qk"), sem("g_v"), sem("g_r"), sem("g_w")
        g_z, g_zread, g_sp, g_b = sem("g_z"), sem("g_zread"), sem("g_softplus"), sem("g_cumsum")
        g_eb, g_ekd, g_ek, g_qk_done = sem("g_exp_b"), sem("g_last_minus_b"), sem("g_exp_k"), sem("g_qe_ke")
        g_d, g_f, g_x, g_s, g_pred = sem("g_diff"), sem("g_factor"), sem("g_level"), sem("g_scores"), sem("g_masked")
        g_vt, g_vtr, g_kt, g_ktr = sem("g_v_turned"), sem("g_v_copied"), sem("g_k_turned"), sem("g_k_copied")
        g_o, g_or, g_u, g_st = sem("g_out"), sem("g_out_read"), sem("g_update"), sem("g_state")
        g_root, g_on, g_silu, g_ot, g_yt = sem("g_root"), sem("g_normed"), sem("g_silu_r"), sem("g_out_turned"), sem("g_y")

        waited = sem("wait_carried")

        block = ctx.enter_context(nc.Block())

        def h_job(layer, kind, half):
            return 6 * layer + 2 * kind + half

        def stat_job(layer, kind, half):
            return {(0, 0): 7, (0, 1): 9, (1, 0): 10, (2, 0): 11, (1, 1): 12, (2, 1): 13, (3, 0): 14, (3, 1): 15}[(kind, half)] \
                if layer else \
                {(0, 0): 0, (0, 1): 1, (1, 0): 2, (2, 0): 3, (1, 1): 4, (2, 1): 5, (3, 0): 6, (3, 1): 8}[(kind, half)]

        def hosted(layer, phase, half):
            if phase == "in" and half == 0:
                return (((0, 3, 1), y3) if layer else None), (layer, 0, 1)
            if phase == "out" and half == 1:
                return ((layer, 1, 0), y3), (layer, 2, 0)
            if phase == "ffn" and half == 0:
                return ((layer, 1, 1), y_out1), (layer, 2, 1)
            if phase == "ffn" and half == 1:
                return ((layer, 3, 0), y3), (None if layer else (1, 0, 0))
            return None, None

        def rinv_slot(kind, half):
            return half if kind in (0, 2) else 2

        def fill_job(layer, kind, half):
            return 2 * (2 * layer + (kind == 2)) + half

        def upd(layer, kind, half):
            return 4 * layer + (0 if kind == 1 else 2) + half + 1

        def in_base(layer, half):
            return USE_IN[layer] + half * NIN[layer]

        def ffn_base(layer, half):
            return USE_FFN[layer] + half * FFN_UNITS

        def dn_idx(layer, half):
            return 2 * layer + half

        LANE = [8, 14]

        def lanes(kind, n):
            if kind == 0:
                if n < 4:
                    return [(0, n % 2, 0, n + 1)]
                return [(0, 0, 0, 4), (0, 1, 4, n - 3)]
            out = []
            for k0 in range(0, n + 1, 4):
                for c in (0, 1):
                    out.append((c, c, k0, min(4, n + 1 - k0)))
            return out

        def lane_count(kind, n, lane):
            return 1 + sum(g[1] == lane for m in range(n) for g in lanes(kind, m))

        @block.sync
        def _(sp):
            sp.sem_inc(st_done, 16)
            sp.dma_start(cs[:, :], cT).then_inc(s_const, 16)
            sp.dma_start(ada_b[:, :], ada_bT).then_inc(s_const, 16)
            sp.dma_start(ng[:, :], norm_gT).then_inc(s_const, 16)
            sp.dma_start(ident[:, :], identity).then_inc(s_const, 16)
            sp.dma_start(lamv, lam_p).then_inc(s_const, 16)
            sp.dma_start(sub_g, subln_g).then_inc(s_const, 16)
            sp.dma_start(hg, head_g).then_inc(s_const, 16)
            sp.dma_start(mask_f, level_masks.rearrange("p l i -> p (l i)")).then_inc(s_const, 16)
            x_in = xT.rearrange("(k p) t -> p k t", p=P)
            sp.dma_start(x[:, :, 0:HALF], x_in[:, :, 0:HALF]).then_inc(s_x[0], 16)
            for g in range(2):
                for u in range(0, KB, 4):
                    sp.dma_start(ada_first[:, g, u:u + 4, :], ada_w[KB * g + u:KB * g + u + 4].rearrange("u p n -> p u n"))\
                        .then_inc(ada_big[2 * g + u // 4], 16)
            sp.dma_start(x[:, :, HALF:S], x_in[:, :, HALF:S]).then_inc(s_x[1], 16)

            def ada_pair(pair):
                sp.wait_ge(ada_used, 2 * (pair - 8) + 1)
                for s in range(2):
                    sp.dma_start(ada_raw[:, s, :], ada_w[bass.ds(2 * pair + s, 1)] .rearrange("u p n -> (u p) n")
                                 if not isinstance(pair, int) else ada_w[2 * pair + s]).then_inc(ada_full[s], 16)

            def unit(pack, use, s):
                sp.wait_ge(lo_done, use + 1)
                src = weights[pack] if isinstance(pack, int) else weights[bass.ds(pack, 1)].rearrange("u p n -> (u p) n")
                sp.dma_start(w_raw[:, s, :], src).then_inc(raw_full[s], 16)

            def stream(pack, use, pairs):
                with sp.Fori(0, pairs) as i:
                    for s in range(2):
                        unit(pack + 2 * i + s, use + 2 * i + s, (use + s) % 2)

            def project(layer, half):
                use, n_ada = in_base(layer, half), [[12, 12], [12, 4]][layer][half]
                ada0 = [[8, 20], [32, 44]][layer][half]
                done = PAIRS_IN * (2 * layer + half)

                def store(i):
                    sp.wait_ge(free0, T_IN[layer] + PAIRS_IN * half + i + 2)
                    sp.wait_ge(free1, T_IN[layer] + PAIRS_IN * half + i + 2)
                    dst = proj[2 * i:2 * i + 2] if isinstance(i, int) else proj[bass.ds(2 * i, 2)]
                    sp.dma_start(dst.rearrange("b p t -> p b t")[:, :, half * HALF:(half + 1) * HALF],
                                 stage[:, :, :]).then_inc(st_done, 16)

                def body(i, ada):
                    for s in range(2):
                        unit(PACK_IN[layer] + 2 * i + s, use + 2 * i + s, (use + s) % 2)
                    if layer == half == 0 and isinstance(i, int):
                        sp.wait_ge(mod_done, 1)
                    if ada:
                        ada_pair(ada0 + i)

                body(0, True)
                with sp.Fori(1, n_ada) as i:
                    body(i, True)
                    store(i - 1)
                if n_ada < PAIRS_IN:
                    with sp.Fori(n_ada, PAIRS_IN) as i:
                        body(i, False)
                        store(i - 1)
                if layer == 1:
                    unit(PACK_IN[1] + 24, use + 24, (use + 24) % 2)
                store(PAIRS_IN - 1)

            def attention():
                sp.wait_ge(st_done, 16 * 2 * PAIRS_IN + 16)
                sp.wait_ge(hl_done, 16)
                sp.wait_ge(mod_done, 3)
                sp.dma_start(dist, distance).then_inc(tab_full, 16)
                sp.dma_start(mask_bias, causal_bias).then_inc(tab_full, 16)

                def load(b, slot, kind, j):
                    rows = (0, 4, 8) if kind == 0 else (12, 16, 20)

                    def row(r):
                        i = rows[r] + j
                        return proj[i] if isinstance(i, int) else proj[bass.ds(i, 1)].rearrange("u p n -> (u p) n")
                    sp.wait_ge(qk_lo, 4 * b + 1)
                    for c in range(2):
                        for top in (0, 64):
                            sp.dma_start(q_dup[top:top + 64, c, :], row(0)[64 * c:64 * c + 64, :]).then_inc(qk_full, 16)
                            sp.dma_start(k_dup[top:top + 64, c, :], row(1)[64 * c:64 * c + 64, :]).then_inc(qk_full, 16)
                    sp.wait_ge(v_read, b + 1)
                    sp.dma_start(v_sb, row(2)).then_inc(v_full, 16)

                with sp.Fori(0, 2) as i:
                    for s in range(2):
                        load(2 * i + s, s, 0, 2 * i + s)
                load(4, 0, 1, 0)
                sp.wait_ge(blk_done, 6)
                sp.dma_start(mask_bias, dilated_bias).then_inc(tab_full, 16)
                load(5, 1, 1, 1)
                load(6, 0, 1, 2)
                load(7, 1, 1, 3)
                sp.wait_ge(pv_done, 8 * 8 + 1)

            def gated():
                sp.wait_ge(st_done, 16 * 4 * PAIRS_IN + 16)
                sp.wait_ge(hl_done, 8 * (h_job(1, 0, 1) + 1))
                sp.wait_ge(mod_done, 5)
                with sp.Fori(0, C_HEADS) as h:
                    def row(i, n=1):
                        return proj[bass.ds(i, n)].rearrange("u p n -> p u n")
                    sp.wait_ge(g_pred, 16 * h + 1)
                    sp.dma_start(wg2[0:C_RANK, :], w_g2[bass.ds(h, 1)].rearrange("u p n -> (u p) n")).then_inc(g_w, 16)
                    sp.dma_start(bg2[:, :], b_g2[bass.ds(h, 1)].rearrange("u p n -> (u p) n")).then_inc(g_w, 16)
                    sp.dma_start(gq, proj[bass.ds(h, 1)].rearrange("u p n -> (u p) n")).then_inc(g_qk, 16)
                    sp.dma_start(gk, proj[bass.ds(4 + h, 1)].rearrange("u p n -> (u p) n")).then_inc(g_qk, 16)
                    sp.wait_ge(g_yt, 4 * h + 1)
                    sp.dma_start(gvr[:, :, :], row(8 + 2 * h, 2)).then_inc(g_v, 16)
                    sp.wait_ge(g_vt, 4 * h + 4)
                    sp.dma_start(gvr[:, :, :], row(16 + 2 * h, 2)).then_inc(g_r, 16)

            for layer in range(2):
                for half in range(2):
                    project(layer, half)
                if layer == 0:
                    attention()
                else:
                    gated()
                for half in range(2):
                    stream(PACK_OUT[layer], USE_OUT[layer] + KB * half, KB // 2)
                for half in range(2):
                    use = ffn_base(layer, half)
                    stream(PACK_FFN[layer], use, FFN_UNITS // 2)
            out = outT.rearrange("(k p) t -> p k t", p=P)
            sp.wait_ge(x_upd, upd(1, 3, 0))
            sp.dma_start(out[:, :, 0:HALF], x[:, :, 0:HALF]).then_inc(outs, 16)
            for k in range(0, KB, 2):
                sp.wait_ge(x_final, k + 2)
                sp.dma_start(out[:, k:k + 2, HALF:S], x[:, k:k + 2, HALF:S]).then_inc(outs, 16)
            sp.wait_ge(outs, 16 * 5)

        @block.gpsimd
        def _(pool):
            pool.sem_inc(lo_done, 2)

            def lo(use, s):
                pool.wait_ge(hi_done, use + 1)
                pool.tensor_tensor(w_lo[:, s, :], w_raw[:, s, :], w_hi[:, s, :].bitcast(f32),
                                   ALU.subtract).then_inc(lo_done, 1)

            def split_qk(b, s):
                for c in range(2):
                    pool.drain()
                    pool.wait_ge(qk_hi, 4 * b + 2 * c + 1)
                    pool.tensor_tensor(q_split[s][64:128, c, :], q_dup[64:128, c, :],
                                       q_split[s][64:128, c, :].bitcast(f32), ALU.subtract).then_inc(qk_lo, 1)
                    pool.drain()
                    pool.wait_ge(qk_hi, 4 * b + 2 * c + 2)
                    pool.tensor_tensor(k_low[s][:, c, :], k_dup[:, c, :],
                                       k_high[s][:, c, :].bitcast(f32), ALU.subtract).then_inc(qk_lo, 1)

            def differences(h, lv):
                m = 64 >> lv
                if lv == 0:
                    pool.wait_ge(g_b, h + 1)
                if lv > 1:
                    pool.wait_ge(g_x, 8 * h + lv)
                b4 = gb.rearrange("p (n t) -> p n t", t=2 * m)
                pool.tensor_tensor(g_dif[lv % 2].rearrange("p (n t) -> p n t", t=2 * m), b4,
                                   b4[:, :, m - 1:m].broadcast_to([P, S // (2 * m), 2 * m]), ALU.subtract).then_inc(g_d, 1)

            pool.sem_inc(qk_lo, 1)
            with pool.Fori(0, USE_OUT[0] // 2) as i:
                for s in range(2):
                    lo(2 * i + s, s)
            with pool.Fori(0, 4) as i:
                for s in range(2):
                    split_qk(2 * i + s, s)
            with pool.Fori(USE_OUT[0] // 2, USE_OUT[1] // 2) as i:
                for s in range(2):
                    lo(2 * i + s, s)
            with pool.Fori(0, C_HEADS) as h:
                for lv in range(LEVELS):
                    differences(h, lv)
            with pool.Fori(USE_OUT[1] // 2, (USE_FFN[1] + 2 * FFN_UNITS) // 2) as i:
                for s in range(2):
                    lo(2 * i + s, s)

        @block.tensor
        def _(pe):
            pe.sem_inc(unit_used, 2)
            pe.sem_inc(pv_done, 1)

            def unit(use, s, b, job=None):
                pe.wait_ge(hi_done, use + 1)
                for k in range(KB):
                    w = w_hi[:, s, k * P:(k + 1) * P]
                    if job is not None:
                        pe.wait_ge(hl_done, KB * job + k + 1)
                    pe.matmul(bank(b), w, h_hi[:, k, :], start=k == 0, stop=False)
                    pe.matmul(bank(b), w, h_lo[:, k, :], start=False, stop=False)
                pe.wait_ge(lo_done, use + 3)
                for k in range(KB):
                    mm = pe.matmul(bank(b), w_lo[:, s, k * P:(k + 1) * P], h_hi[:, k, :], start=False, stop=k == KB - 1)
                mm.then_inc(unit_used, 1)

            def two_pairs(use, tiles, i, job, down_before=None):
                for j in range(2):
                    for s in range(2):
                        if down_before is not None:
                            pe.wait_ge((dn_ev0, dn_ev1)[s], 4 * down_before + j + 1)
                        pe.wait_ge((free0, free1)[s], tiles + 2 * i + j)
                        unit(use + 4 * i + 2 * j + s, (use + s) % 2, 2 * j + s, job if j == s == 0 else None)

            def pairs(layer, phase, half, use, tiles, n, job):
                post, pre = hosted(layer, phase, half)
                if phase == "out":
                    for i in range(PAIRS_OUT):
                        for s in range(2):
                            pe.wait_ge((free0, free1)[s], tiles + i)
                            unit(use + 2 * i + s, (use + s) % 2, 2 * (i % 2) + s, job if i == s == 0 else None)
                            if post and (i, s) == (0, 1):
                                mean(*post[0])
                            if pre and (i, s) == (PAIRS_OUT - 1, 0):
                                mean(*pre)
                    return
                two_pairs(use, tiles, 0, job, {("in", 1, 0): 1, ("ffn", 0, 1): 0, ("ffn", 1, 1): 2}.get((phase, layer, half)))
                if post:
                    mean(*post[0])
                at = 1
                if pre:
                    two_pairs(use, tiles, 1, None)
                    two_pairs(use, tiles, 2, None)
                    mean(*pre)
                    at = 3
                with pe.Fori(at, n // 2) as i:
                    two_pairs(use, tiles, i, None)

            def mean(layer, kind, half):
                n = stat_job(layer, kind, half)
                if n == 0:
                    pe.wait_ge(sq_done, 1)
                    for k in range(KB):
                        mm = pe.matmul(bank(7), mean_w[:, :], y3[:, k, :], start=k == 0, stop=k == KB - 1)
                    mm.then_inc(mean_done, 1)
                    return
                pe.wait_ge(ssum_done, n)
                pe.wait_ge(root_done, n)
                pe.matmul(bank(7), mean_w[:, :], rinv[:, rinv_slot(kind, half), :], start=True, stop=True)\
                    .then_inc(mean_done, 1)

            def ada_turn(n, groups, acc=ada_acc):
                pe.wait_ge(acc_done, n + 1)
                if n:
                    pe.wait_ge(mod_done, n)
                for g in range(groups):
                    for m in range(KB):
                        mm = pe.matmul(bank(6)[:, g * 8 + m:g * 8 + m + 1], acc[:, g, m * P:(m + 1) * P],
                                       ones[:, 0:1], start=True, stop=True)
                mm.then_inc(ada_mm, 1)

            def turn_v(b, group):
                pe.wait_ge(v_full, 16 * b + 16)
                for lane in range(2):
                    pe.wait_ge((ta_free, td_free)[lane], group)
                    for n in range(4):
                        m = 4 * lane + n
                        mm = pe.transpose(bank(4 + lane)[:, n * P:(n + 1) * P], v_sb[:, m * P:(m + 1) * P], ident[:, :])
                    mm.then_inc((ta_done, td_done)[lane], 1)

            def scores(n, b, slot):
                for c in range(2):
                    pe.wait_ge(s_read[c], 8 * b + n + 1)
                    if n == 0:
                        pe.wait_ge(qk_lo, 4 * b + 2 * c + 3)
                    W = 256 * ((n + 2) // 2)
                    for k0 in range(0, W, 512):
                        w = min(512, W - k0)
                        for part in (k_high, k_low):
                            mm = pe.matmul(ps[:, c * 1024 + k0:c * 1024 + k0 + w],
                                           q_split[slot][:, c, n * P:(n + 1) * P], part[slot][:, c, k0:k0 + w],
                                           start=part is k_high, stop=part is k_low)
                    mm.then_inc(s_done[c], 1)

            def attention_block(kind, b, slot, last=False):
                before = (lambda t: LANE[0] * b + t) if kind == 0 else (lambda t: LANE[0] * 4 + LANE[1] * (b - 4) + t)

                def turn_weights(n, part=0):
                    count = [lane_count(kind, n, lane) + part for lane in range(2)]
                    if kind == 0:
                        pe.wait_ge(w_done, 8 * b + n + 1 + 1)
                    for c, lane, k0, m in lanes(kind, n):
                        if kind == 1 and k0 != 4 * part:
                            continue
                        if kind == 1:
                            pe.wait_ge(exp_done, 16 * b + 2 * n + c + 1 + 1)
                        pe.wait_ge((ta_free, td_free)[lane], before(count[lane]) + 1)
                        for i in range(m):
                            mm = pe.transpose(bank(4 + lane)[:, i * P:(i + 1) * P],
                                              pr[n % 2][:, c, (k0 + i) * P:(k0 + i + 1) * P], ident[:, :])
                        mm.then_inc((ta_done, td_done)[lane], 1)
                        count[lane] += 1

                def weigh(n):
                    pe.wait_ge(ta_free, before(lane_count(kind, n + 1, 0)) + 1)
                    pe.wait_ge(td_free, before(lane_count(kind, n + 1, 1)) + 1)
                    pe.wait_ge(o_done, 8 * b + max(n, 1))
                    for c in range(1 if kind == 0 else 2):
                        for kb in range(n + 1):
                            mm = pe.matmul(bank(6 + n % 2)[:, c * P:(c + 1) * P], wT[n % 2][c][:, kb, :],
                                           v_tok[:, kb, :], start=kb == 0, stop=kb == n)
                    mm.then_inc(pv_done, 1)

                def turn_out():
                    if kind == 0:
                        pe.wait_ge(o_ready, b + 1)
                    else:
                        pe.wait_ge(o_done, 8 * b + 8 + 1)
                    for lane in range(2):
                        pe.wait_ge((ta_free, td_free)[lane], before(LANE[kind] + (not last)))
                        for n in range(4):
                            mm = pe.transpose(bank(4 + lane)[:, n * P:(n + 1) * P], o_sb[:, 4 * lane + n, :], ident[:, :])
                        mm.then_inc((ta_done, td_done)[lane], 1)

                scores(1, b, slot)
                for n in range(8):
                    if kind == 1:
                        turn_weights(n)
                        if n:
                            weigh(n - 1)
                    if n < 6:
                        scores(n + 2, b, slot)
                    if kind == 0:
                        turn_weights(n)
                        if n:
                            weigh(n - 1)
                    elif n > 3:
                        turn_weights(n, 1)
                weigh(7)
                if not last:
                    turn_v(b + 1, before(LANE[kind]))
                    scores(0, b + 1, 1 - slot)
                turn_out()

            def attention():
                pe.wait_ge(free0, T_OUT[0] + 1)
                pe.wait_ge(free1, T_OUT[0] + 1)
                turn_v(0, 1)
                scores(0, 0, 0)
                with pe.Fori(0, 2) as i:
                    for s in range(2):
                        attention_block(0, 2 * i + s, s)
                for b in range(4, 8):
                    attention_block(1, b, b % 2, b == 7)
                pe.wait_ge(ta_free, 4 * sum(LANE) + 1)
                pe.wait_ge(td_free, 4 * sum(LANE) + 1)

            def gated():
                pe.wait_ge(free0, T_OUT[1] + 1)
                pe.wait_ge(free1, T_OUT[1] + 1)
                pe.wait_ge(glr_done, 2)
                pe.wait_ge(mod_done, 5)
                with pe.Fori(0, C_HEADS) as h:
                    pe.wait_ge(g_w, 32 * h + 32)
                    pe.wait_ge(g_yt, 4 * h + 1)
                    for n in range(2):
                        mm = pe.matmul(bank(n), wg2[:, :], glr[:, n * 512:(n + 1) * 512], start=True, stop=True)
                    mm.then_inc(g_z, 1)
                    pe.wait_ge(g_v, 16 * h + 16)
                    pe.wait_ge(g_or, 8 * h + 1)
                    pe.wait_ge(g_st, 8 * h + 1)
                    for n in range(4):
                        for i in range(2):
                            for b in range(2):
                                m = 2 * n + i
                                mm = pe.transpose(bank(4 + n)[:, i * 256 + b * P:i * 256 + (b + 1) * P],
                                                  gvr[:, b, m * P:(m + 1) * P], ident[:, :])
                        mm.then_inc(g_vt, 1)
                    pe.wait_ge(g_zread, 2 * h + 2)
                    for j in range(LEVELS + 1):
                        pe.wait_ge(g_x, 8 * h + j + 1)
                        pe.wait_ge(g_pred, 16 * h + 2 * max(0, j - 1) + 1)
                        for n in range(8):
                            t = slice(n * P, (n + 1) * P)
                            a, b = (gx[:, (j - 1) % 2, t], gx[:, (j - 1) % 2, t]) if j else (gk[:, t], gq[:, t])
                            mm = pe.matmul(bank(2 * (j % 2) + n // 4)[:, (n % 4) * P:(n % 4 + 1) * P], a, b,
                                           start=True, stop=True)
                        mm.then_inc(g_s, 1)
                        if j == 1:
                            pe.wait_ge(g_qk_done, 2 * h + 2)
                            for n in range(2):
                                pe.wait_ge(g_vtr, 4 * h + 4)
                                for i in range(4):
                                    m = 4 * n + i
                                    mm = pe.transpose(bank(4 + n)[:, i * P:(i + 1) * P], ke[:, m * P:(m + 1) * P], ident[:, :])
                                mm.then_inc(g_kt, 1)
                    pe.wait_ge(g_pred, 16 * h + 16 + 1)
                    pe.wait_ge(g_ktr, 2 * h + 2)
                    for n in range(8):
                        t = slice(n * P, (n + 1) * P)
                        if n < 7:
                            if n >= 2:
                                pe.wait_ge(g_st, 8 * h + n - 1 + 1)
                            pe.matmul(bank(6 + n % 2)[:, 0:C_DV], ke_tok[:, n, :], gv_tok[:, n, :], start=True, stop=True)\
                                .then_inc(g_u, 1)
                        if n >= 2:
                            pe.wait_ge(g_or, 8 * h + n - 1 + 1)
                        mm = pe.matmul(bank(4 + n % 2)[:, 0:C_DV], attnT[:, n, :], gv_tok[:, n, :], start=True, stop=n == 0)
                        if n:
                            pe.wait_ge(g_st, 8 * h + n + 1)
                            mm = pe.matmul(bank(4 + n % 2)[:, 0:C_DV], qe[:, t], state, start=False, stop=True)
                        mm.then_inc(g_o, 1)
                    for b in range(2):
                        for n in range(2):
                            pe.wait_ge(g_on, 2 * h + n + 1)
                            for i in range(4):
                                mm = pe.transpose(bank(2 * b + n)[:, i * P:(i + 1) * P],
                                                  go[:, 4 * n + i, b * P:(b + 1) * P], ident[:, :])
                            mm.then_inc(g_ot, 1)
                pe.wait_ge(g_yt, 4 * C_HEADS + 1)

            def down(layer, half):
                use, d = ffn_base(layer, half) + 2 * FB, dn_idx(layer, half)
                tiles = T_FFN[layer] + FB * (half + 1)
                pe.wait_ge(free0, tiles + 1)
                pe.wait_ge(free1, tiles + 1)
                pe.wait_ge(root_done, [[6, 8], [14, 15]][layer][half])

                def row(i, s, first, last):
                    u = use + 2 * i + s
                    slot = (use + s) % 2
                    cols = [slice(m * P, (m + 1) * P) for m in range(KB)]
                    pe.wait_ge(hi_done, u + 1)
                    pe.wait_ge(ah_done, FB * d + 2 * i + s + 1)
                    for m in range(KB):
                        pe.matmul(bank(m), w_hi[:, slot, cols[m]], a_hi[:, s, :], start=first, stop=False)
                    pe.wait_ge(al_done, FB * d + 2 * i + s + 1)
                    for m in range(KB):
                        pe.matmul(bank(m), w_hi[:, slot, cols[m]], a_lo[:, s, :], start=False, stop=False)
                    pe.wait_ge(lo_done, u + 3)
                    for m in range(KB):
                        mm = pe.matmul(bank(m), w_lo[:, slot, cols[m]], a_hi[:, s, :], start=False, stop=last)
                    mm.then_inc(unit_used, 1)

                row(0, 0, True, False)
                row(0, 1, False, False)
                with pe.Fori(1, FB // 2 - 1) as i:
                    for s in range(2):
                        row(i, s, False, False)
                row(FB // 2 - 1, 0, False, False)
                row(FB // 2 - 1, 1, False, True)

            pe.wait_ge(s_const, 128)
            pe.wait_ge(setup_done, 1)
            mean(0, 0, 0)
            ada_turn(0, 2, acc_first)
            for layer in range(2):
                for half in range(2):
                    use = in_base(layer, half)
                    pairs(layer, "in", half, use, T_IN[layer] + PAIRS_IN * half, PAIRS_IN, h_job(layer, 0, half))
                    if layer == 1:
                        if half:
                            pe.wait_ge(glr_done, 1)
                        unit(use + 24, (use + 24) % 2, 5)
                        pe.matmul(bank(4)[:, 0:1], ident[:, :], ones[:, 0:1], start=True, stop=True).then_inc(glr_mm, 1)
                    ada_turn(1 + 2 * layer + half, [[3, 3], [3, 1]][layer][half])
                if layer == 0:
                    attention()
                else:
                    gated()
                for half in range(2):
                    pairs(layer, "out", half, USE_OUT[layer] + KB * half, T_OUT[layer] + PAIRS_OUT * half, PAIRS_OUT,
                          h_job(layer, 1, half))
                for half in range(2):
                    pairs(layer, "ffn", half, ffn_base(layer, half), T_FFN[layer] + FB * half, FB,
                          h_job(layer, 2, half))
                    down(layer, half)
            mean(1, 3, 1)

        @block.scalar
        def _(a):
            for count in (free0, exp_done, ta_free, o_done, g_or):
                a.sem_inc(count, 1)

            def hi_at(base, i, s):
                slot = (base + s) % 2
                a.wait_ge(raw_full[slot], 16 * ((base + s) // 2 + i) + 16)
                a.wait_ge(unit_used, base + 2 * i + s + 1)
                a.activation(w_hi[:, slot, :], w_raw[:, slot, :], ACT.Copy).then_inc(hi_done, 1)

            def square(layer, kind, half, src):
                n = stat_job(layer, kind, half)
                if kind in (0, 2):
                    if layer == 0 and kind == 0:
                        a.wait_ge(s_x[half], 16)
                    else:
                        a.wait_ge(x_upd, upd(layer - (kind == 0), 3 if kind == 0 else 1, half))
                    src = x[:, :, half * HALF:(half + 1) * HALF]
                elif kind == 3:
                    a.wait_ge(dn_ev1, 4 * (dn_idx(layer, half) + 1))
                else:
                    a.wait_ge(free1, T_OUT[layer] + PAIRS_OUT * (half + 1) + 1)
                if kind in (1, 3):
                    a.drain()
                if n > 1:
                    a.wait_ge(ssum_done, n - 1)
                dst = y3 if n == 0 else sq
                a.activation(dst[:, 0:4, :], src[:, 0:4, :], ACT.Square)
                a.activation(dst[:, 4:8, :], src[:, 4:8, :], ACT.Square).then_inc(sq_done, 1)

            def root(layer, kind, half):
                a.wait_ge(mean_done, stat_job(layer, kind, half) + 1)
                a.activation(rinv[:, rinv_slot(kind, half), :], bank(7), ACT.Sqrt, bias=eps_c).then_inc(root_done, 1)

            def write_h(k, src, first_unit, norm=None):
                if k == 0:
                    a.wait_ge(unit_used, first_unit + 2)
                if norm:
                    layer, kind, half = norm
                    sh = 48 * layer + (0 if kind == 0 else 24) + k
                    a.wait_ge(xn_done, 8 * fill_job(layer, kind, half) + k + 1)
                    a.activation(h_hi[:, k, :], y3[:, k, :], ACT.Identity, bias=mod[:, sh:sh + 1]).then_inc(hh_done, 1)
                else:
                    a.activation(h_hi[:, k, :], src, ACT.Copy).then_inc(hh_done, 1)

            def load_sqrt():
                a.activation(unused, eps_c, ACT.Sqrt)

            def hooks(layer, phase, half):
                post, pre = hosted(layer, phase, half)
                at = {}

                def put(n, f, *args):
                    at.setdefault(n, []).append((f, args))
                if post:
                    put(-1, square, *post[0], post[1])
                    put(0 if phase == "out" else 1, root, *post[0])
                if pre:
                    put(1.5 if phase == "out" else 3, square, *pre, None)
                    put(2.5 if phase == "out" else 5, root, *pre)
                return at

            def run(at, n):
                for f, args in at.get(n, []):
                    f(*args)

            def project(layer, half):
                base = in_base(layer, half)
                st = PAIRS_IN * (2 * layer + half)
                at = hooks(layer, "in", half)

                def pair(i, j):
                    for s in range(2):
                        if half or not isinstance(i, int) or i:
                            hi_at(base, i, s)
                    a.wait_ge(unit_used, base + 2 * i + 3)
                    a.wait_ge(st_done, 16 * (st + i) + 16)
                    a.activation(stage[:, 0, :], bank(2 * j), ACT.Copy).then_inc(free0, 1)

                run(at, -1)
                if at:
                    for i in range(PAIRS_IN):
                        pair(i, i % 2)
                        run(at, i)
                else:
                    with a.Fori(0, PAIRS_IN // 2) as i:
                        for j in range(2):
                            pair(2 * i + j, j)
                if layer == 1:
                    hi_at(base + 24, 0, 0)
                    a.wait_ge(glr_mm, half + 1)
                    a.activation(glr[:, half * HALF:(half + 1) * HALF], bank(5), ACT.Copy).then_inc(glr_done, 1)

            def attention():
                a.wait_ge(lam_dot, 2)

                def split(b, slot, n, last=False):
                    if last:
                        return
                    a.wait_ge(qk_full, 128 * b + 128)
                    c = n // 2
                    dst, src = ((q_split, q_dup), (k_high, k_dup))[n % 2]
                    a.activation(dst[slot][:, c, :], src[:, c, :], ACT.Copy).then_inc(qk_hi, 1)

                def copy_v(b, group):
                    a.wait_ge(pv_done, 8 * b + 1)
                    a.wait_ge(ta_done, group)
                    a.activation(v_tok[:, 0:4, :], bank(4).rearrange("p (m q) -> p m q", q=P), ACT.Copy).then_inc(ta_free, 1)

                def block_(kind, b, slot, last):
                    before = (lambda t: LANE[0] * b + t) if kind == 0 else (lambda t: LANE[0] * 4 + LANE[1] * (b - 4) + t)
                    count = 1

                    def copy_a(dst, m):
                        nonlocal count
                        count += 1
                        a.wait_ge(ta_done, before(count))
                        a.activation(dst, bank(4)[:, 0:m * P].rearrange("p (m q) -> p m q", q=P), ACT.Copy).then_inc(ta_free, 1)

                    def exps(n):
                        for c in range(2):
                            a.wait_ge(nm_done, 8 * b + n + 1)
                            K = P * (n + 1)
                            a.activation(pr[n % 2][:, c, 0:K], pr[n % 2][:, c, 0:K], ACT.Exp, bias=nmx[:, 2 * n + c:2 * n + c + 1],
                                         accum_out=rs[:, 2 * n + c:2 * n + c + 1]).then_inc(exp_done, 1)

                    def output(n):
                        a.drain()
                        a.wait_ge(pv_done, 8 * b + n + 1 + 1)
                        if kind == 0:
                            r = r0[:, 2 * n:2 * n + 1]
                            out = bank(6 + n % 2, P)
                            a.activation(junk, out, ACT.Square, scale=r, accum_out=ms[:, n:n + 1])
                            a.activation(o_sb[:, n, :], out, ACT.Copy, scale=r).then_inc(o_done, 1)
                        else:
                            a.wait_ge(w_done, 8 * b + n + 1 + 1)
                            for c in range(2):
                                op = a.activation(o_sb[:, n, 64 * c:64 * c + 64], bank(6 + n % 2)[:, 192 * c:192 * c + 64], ACT.Copy,
                                                  scale=r0[:, 2 * n + c:2 * n + c + 1])
                            op.then_inc(o_done, 1)

                    exps(0)
                    def copies(n):
                        for c, lane, k0, m in lanes(kind, n):
                            if lane == 0:
                                if n > 1:
                                    a.wait_ge(pv_done, 8 * b + n)
                                copy_a(wT[n % 2][c][:, k0:k0 + m, :], m)

                    exps(1)
                    for n in range(1, 8):
                        copies(n - 1)
                        if n > 1:
                            output(n - 2)
                        if n < 7:
                            exps(n + 1)
                        if n < 5:
                            split(b + 1, 1 - slot, n - 1, last)
                    if kind == 0:
                        load_sqrt()
                    output(6)
                    copies(7)
                    output(7)
                    if kind == 0:
                        a.drain()
                        a.activation(ms, ms, ACT.Sqrt, bias=eps_c, scale=1.0 / P).then_inc(sub_root, 1)
                    if not last:
                        copy_v(b + 1, before(LANE[kind]))
                    a.wait_ge(ta_done, before(LANE[kind] + (not last)))
                    dst = yT[:, b, 0:512] if isinstance(b, int) else yT[:, bass.ds(b, 1), 0:512].rearrange("p u t -> p (u t)")
                    a.activation(dst, bank(4), ACT.Copy if kind else ACT.Identity,
                                 **({} if kind else {"scale": sub_g})).then_inc(ta_free, 1)

                a.wait_ge(unit_used, USE_OUT[0] + 2)
                for n in range(4):
                    split(0, 0, n)
                copy_v(0, 1)
                with a.Fori(0, 2) as i:
                    for s in range(2):
                        block_(0, 2 * i + s, s, False)
                for b in range(4, 8):
                    block_(1, b, b % 2, b == 7)

            def gated():
                with a.Fori(0, C_HEADS) as h:
                    a.wait_ge(g_z, h + 1)
                    a.activation(gd, ps[:, 0:1024], ACT.Abs, bias=bg2[:, :]).then_inc(g_zread, 1)
                    a.drain()
                    a.activation(gd, gd, ACT.Exp, scale=-1.0)
                    a.drain()
                    a.activation(gd, gd, ACT.Ln, bias=1.0).then_inc(g_sp, 1)
                    for n in range(4):
                        a.wait_ge(g_vt, 4 * h + n + 1)
                        a.activation(gv_tok[:, 2 * n:2 * n + 2, :], bank(4 + n).rearrange("p (i d) -> p i d", i=2), ACT.Copy)\
                            .then_inc(g_vtr, 1)
                    for lv in range(LEVELS):
                        m = 64 >> lv
                        v = g_dif[lv % 2].rearrange("p (n u t) -> p n u t", u=2, t=m)
                        a.wait_ge(g_d, 7 * h + lv + 1)
                        a.activation(v[:, :, 0, :], v[:, :, 0, :], ACT.Exp, scale=-1.0 / C_TAU)
                        a.activation(v[:, :, 1, :], v[:, :, 1, :], ACT.Exp, scale=1.0 / C_TAU)
                        a.drain().then_inc(g_f, 1)
                        if lv == 0:
                            a.activation(qe, gb, ACT.Exp, scale=1.0 / C_TAU).then_inc(g_eb, 1)
                            a.activation(eblast, gb.rearrange("p (n t) -> p n t", t=P)[:, :, P - 1], ACT.Exp, scale=1.0 / C_TAU)\
                                .then_inc(g_eb, 1)
                            a.wait_ge(g_ekd, h + 1)
                            a.activation(ke, ke, ACT.Exp, scale=1.0 / C_TAU).then_inc(g_ek, 1)
                        if lv == 2:
                            for n in range(2):
                                a.wait_ge(g_kt, 2 * h + n + 1)
                                a.activation(ke_tok[:, 4 * n:4 * n + 4, :], bank(4 + n).rearrange("p (i d) -> p i d", i=4), ACT.Copy)\
                                    .then_inc(g_ktr, 1)
                    a.wait_ge(g_r, 16 * h + 16)
                    a.activation(gvr[:, :, :], gvr[:, :, :], ACT.Silu).then_inc(g_silu, 1)
                    load_sqrt()
                    for n in range(8):
                        a.wait_ge(g_o, 8 * h + n + 1)
                        a.activation(gd[:, 0:C_DV], bank(4 + n % 2)[:, 0:C_DV], ACT.Square, accum_out=ms[:, n:n + 1])
                        a.activation(go[:, n, :], bank(4 + n % 2)[:, 0:C_DV], ACT.Copy).then_inc(g_or, 1)
                        a.drain()
                    a.activation(ms, ms, ACT.Sqrt, bias=eps_c, scale=1.0 / C_DV).then_inc(g_root, 1)

            a.wait_ge(s_const, 128)
            a.activation(cs[:, :], cs[:, :], ACT.Silu).then_inc(cs_done, 1)
            a.wait_ge(setup_done, 1)
            a.wait_ge(lam_dot, 1)
            a.activation(lam2, lam2, ACT.Exp).then_inc(lam_exp, 1)
            square(0, 0, 0, None)
            root(0, 0, 0)
            hi_at(0, 0, 0)
            hi_at(0, 0, 1)
            a.wait_ge(mod_done, 1)
            for k in range(KB):
                write_h(k, None, 0, (0, 0, 0))
            for layer in range(2):
                project(layer, 0)
                for k in range(KB):
                    write_h(k, None, in_base(layer, 1), (layer, 0, 1))
                project(layer, 1)
                if layer == 0:
                    attention()
                    a.wait_ge(ta_free, 4 * sum(LANE) + 1)
                    a.wait_ge(td_free, 4 * sum(LANE) + 1)
                else:
                    gated()
                    a.wait_ge(g_yt, 4 * C_HEADS + 1)
                for half in range(2):
                    base = USE_OUT[layer] + KB * half
                    hi_at(base, 0, 0)
                    for k in range(KB):
                        write_h(k, yT[:, k, half * HALF:(half + 1) * HALF], base)
                        if k == 3:
                            hi_at(base, 0, 1)
                    at = hooks(layer, "out", half)
                    run(at, -1)
                    for i in range(PAIRS_OUT):
                        for s in range(2):
                            if i:
                                hi_at(base, i, s)
                        run(at, i - 0.5)
                        a.wait_ge(unit_used, base + 2 * i + 3)
                        a.activation((y3, y_out1)[half][:, 2 * i, :], bank(2 * (i % 2)), ACT.Copy).then_inc(free0, 1)
                        run(at, i)
                for k in range(KB):
                    write_h(k, None, ffn_base(layer, 0), (layer, 2, 0))
                    if k == 0:
                        hi_at(ffn_base(layer, 0), 0, 0)
                    if k == 3:
                        hi_at(ffn_base(layer, 0), 0, 1)
                for half in range(2):
                    base, tiles, d = ffn_base(layer, half), T_FFN[layer] + FB * half, dn_idx(layer, half)

                    def pair(i, j):
                        for s in range(2):
                            if not isinstance(i, int) or i:
                                hi_at(base, i, s)
                        a.wait_ge(unit_used, base + 2 * i + 3)
                        a.wait_ge(free1, tiles + i)
                        a.activation(exp_buf[j], bank(2 * j), ACT.Exp, scale=-1.0).then_inc(exp_g, 1)

                    at = hooks(layer, "ffn", half)
                    run(at, -1)
                    for i in range(6):
                        pair(i, i % 2)
                        run(at, i)
                    with a.Fori(3, FB // 2) as i:
                        for j in range(2):
                            pair(2 * i + j, j)
                    base += 2 * FB
                    for u in range(FB):
                        hi_at(base, u // 2, u % 2)
                        if u == 0:
                            a.wait_ge(free1, tiles + FB + 1)
                        a.activation(a_hi[:, u % 2, :], act[:, u, :], ACT.Copy).then_inc(ah_done, 1)
                        if (layer, half) != (1, 1):
                            nl, nk, nh = (layer, 2, 1) if half == 0 else (1, 0, 0)
                            if u % 2 and u < 16:
                                write_h(u // 2, None, base, (nl, nk, nh))
                    a.wait_ge(unit_used, base + FB + 2)
                    if (layer, half) != (1, 1):
                        a.wait_ge(hl_done, 8 * (h_job(nl, nk, nh) + 1))
                    for m in range(0, KB, 2):
                        a.activation(y3[:, m, :], bank(m), ACT.Copy).then_inc(dn_ev0, 1)
                        if m in (2, 4) and (layer, half) != (1, 1):
                            hi_at(base + FB, 0, m // 2 - 1)
            square(1, 3, 1, y3)
            root(1, 3, 1)

        @block.vector
        def _(v):
            for count in (free1, s_read[0], s_read[1], td_free, v_read, blk_done, w_done, g_st, g_yt, g_pred,
                          ada_used):
                v.sem_inc(count, 1)

            def sum_squares(layer, kind, half):
                n = stat_job(layer, kind, half)
                r = rinv[:, rinv_slot(kind, half), :]
                v.wait_ge(sq_done, n + 1)
                v.tensor_reduce(r, sq.rearrange("p k t -> p t k"), axis=AX.X, op=ALU.add).then_inc(ssum_done, 1)

            def inverse(layer, kind, half):
                r = rinv[:, rinv_slot(kind, half), :]
                v.wait_ge(root_done, stat_job(layer, kind, half) + 1)
                v.reciprocal(r, r)
                v.drain()

            def xn(layer, kind, half, k):
                g = 8 * (4 * layer + (0 if kind == 0 else 2)) + k
                v.scalar_tensor_tensor(y3[:, k, :], x[:, k, half * HALF:(half + 1) * HALF], gain[:, g:g + 1],
                                       rinv[:, half, :], ALU.mult, ALU.mult).then_inc(xn_done, 1)

            def h_low(layer, kind, half, k, src=None):
                v.wait_ge(hh_done, 8 * h_job(layer, kind, half) + k + 1)
                if kind == 1:
                    v.tensor_tensor(h_lo[:, k, :], src[:, k, :], h_hi[:, k, :].bitcast(f32), ALU.subtract).then_inc(hl_done, 1)
                else:
                    sh = 48 * layer + (0 if kind == 0 else 24) + k
                    v.scalar_tensor_tensor(h_lo[:, k, :], y3[:, k, :], mod[:, sh:sh + 1], h_hi[:, k, :].bitcast(f32),
                                           ALU.add, ALU.subtract).then_inc(hl_done, 1)

            def normed(layer, kind, half, first=0, last=KB):
                for k in range(first, last):
                    xn(layer, kind, half, k)

            def low(layer, kind, half, src=None):
                for k in range(KB):
                    h_low(layer, kind, half, k, src)

            def scaled(y):
                v.tensor_tensor(y, y, bcast_k(rinv[:, 2, :]), ALU.mult)

            def update(layer, kind, half, y):
                g = 8 * (4 * layer + kind)
                v.drain()
                for k in range(KB):
                    xs = x[:, k, half * HALF:(half + 1) * HALF]
                    op = v.scalar_tensor_tensor(xs, y[:, k, :], gain[:, g + k:g + k + 1], xs, ALU.mult, ALU.add)
                    if (layer, kind, half) == (1, 3, 1):
                        op.then_inc(x_final, 1)
                v.drain().then_inc(x_upd, 1)

            def hooks(layer, phase, half):
                post, pre = hosted(layer, phase, half)
                at = {}

                def put(n, f, *args):
                    at.setdefault(n, []).append((f, args))
                out = phase == "out"
                if post:
                    put(-1, sum_squares, *post[0])
                    put(0 if out else 1, inverse, *post[0])
                    put(0 if out else 1, scaled, post[1])
                    put(1 if out else 2, update, *post[0], post[1])
                if pre:
                    put(2 if out else 3, sum_squares, *pre)
                    put(2 if out else 5, inverse, *pre)
                    if phase == "in":
                        put(6, normed, *pre)
                    if out:
                        put(2, normed, *pre, 0, 4)
                return at

            def run(at, n):
                for f, args in at.get(n, []):
                    f(*args)

            def bcast_k(row):
                return row.rearrange("p (u t) -> p u t", u=1).broadcast_to([P, KB, HALF])

            def ada_unit(g, k, s, pair):
                v.wait_ge(ada_full[s], 16 * (pair - 8) + 16)
                v.scalar_tensor_tensor(ada_acc_at(g), ada_raw[:, s, :], cs[:, k:k + 1], ada_acc_at(g),
                                       ALU.mult, ALU.add).then_inc(ada_used, 1)
                v.drain()

            def ada_acc_at(g):
                if isinstance(g, int):
                    return ada_acc[:, g, :]
                return ada_acc[:, bass.ds(g, 1), :].rearrange("p u n -> p (u n)")

            def columns(n, first, groups):
                v.drain().then_inc(acc_done, 1)
                if n == 0:
                    inverse(0, 0, 0)
                v.wait_ge(ada_mm, n + 1)
                w = 8 * groups
                v.tensor_tensor(mod[:, 8 * first:8 * first + w], bank(6, w), ada_b[:, 8 * first:8 * first + w], ALU.add)
                v.drain()
                for grp in range(first, first + groups):
                    layer, g = divmod(grp, 6)
                    if g in (1, 2, 4, 5):
                        o = 8 * (4 * layer + {1: 0, 2: 1, 4: 2, 5: 3}[g])
                        v.scalar_tensor_tensor(gain[:, o:o + 8], mod[:, 8 * grp:8 * grp + 8], 1.0, ng[:, o:o + 8],
                                               ALU.add, ALU.mult)
                v.drain().then_inc(mod_done, 1)

            def project(layer, half):
                base, tiles = in_base(layer, half), T_IN[layer] + PAIRS_IN * half
                st = PAIRS_IN * (2 * layer + half)
                ada0 = [[8, 20], [32, 44]][layer][half]
                groups = [[3, 3], [3, 1]][layer][half]
                v.memset(ada_acc[:, 0:groups, :], 0.0)
                v.drain()

                def tile(i, j):
                    v.wait_ge(unit_used, base + 2 * i + 4)
                    v.wait_ge(st_done, 16 * (st + i) + 16)
                    v.tensor_copy(stage[:, 1, :], bank(2 * j + 1)).then_inc(free1, 1)

                at = hooks(layer, "in", half)

                def group(g):
                    for j in range(4):
                        for s in range(2):
                            ada_unit(g, 2 * j + s, s, ada0 + 4 * g + j)
                        tile(4 * g + j, j % 2)
                        if at:
                            run(at, 4 * g + j)

                run(at, -1)
                if at:
                    for g in range(groups):
                        group(g)
                else:
                    with v.Fori(0, groups) as g:
                        group(g)
                if groups < 3:
                    with v.Fori(2 * groups, PAIRS_IN // 2) as i:
                        for j in range(2):
                            tile(2 * i + j, j)
                columns(1 + 2 * layer + half, ada0 // 4, groups)

            def attention():
                def biases(kind):
                    for c in range(kind + 1):
                        v.scalar_tensor_tensor(bias[:, c, :], dist, slope[:, c:c + 1], mask_bias, ALU.mult, ALU.add)
                    v.drain()

                def copy_v(b, group):
                    v.wait_ge(pv_done, 8 * b + 1)
                    v.wait_ge(td_done, group)
                    v.tensor_copy(v_tok[:, 4:8, :], bank(5).rearrange("p (m q) -> p m q", q=P)).then_inc(td_free, 1)
                    v.drain().then_inc(v_read, 1)

                def block_(kind, b, last=False):
                    before = (lambda t: LANE[0] * b + t) if kind == 0 else (lambda t: LANE[0] * 4 + LANE[1] * (b - 4) + t)
                    count = 1

                    def copy_d(dst, m):
                        nonlocal count
                        count += 1
                        v.wait_ge(td_done, before(count))
                        v.tensor_copy(dst, bank(5)[:, 0:m * P].rearrange("p (m q) -> p m q", q=P)).then_inc(td_free, 1)

                    def biased(n):
                        for c in range(2):
                            K = P * (n + 1)
                            col = 2 * n + c
                            v.wait_ge(s_done[c], 8 * b + n + 1)
                            if n > 1:
                                v.wait_ge(ta_done, before(lane_count(kind, n - 1, 0)))
                                v.wait_ge(td_done, before(lane_count(kind, n - 1, 1)))
                            v.sem_inc(waited, 1)
                            v.tensor_tensor_reduce(out=pr[n % 2][:, c, 0:K], in0=ps[:, c * 1024:c * 1024 + K],
                                                   in1=bias[:, c if kind else 0, 1024 - K:1024], scale=SCORE_SCALE,
                                                   scalar=-3.0e38, op0=ALU.add, op1=ALU.max,
                                                   accum_out=mx[:, col:col + 1]).then_inc(s_read[c], 1)
                        v.drain()
                        v.tensor_scalar(nmx[:, 2 * n:2 * n + 2], mx[:, 2 * n:2 * n + 2], -1.0, None, ALU.mult).then_inc(nm_done, 1)

                    biased(0)
                    def copies(n):
                        for c, lane, k0, m in lanes(kind, n):
                            if lane == 1:
                                if n > 1:
                                    v.wait_ge(pv_done, 8 * b + n)
                                copy_d(wT[n % 2][c][:, k0:k0 + m, :], m)

                    for n in range(8):
                        a0 = 2 * n
                        if n and kind == 1:
                            copies(n - 1)
                        if n < 7:
                            biased(n + 1)
                        if n and kind == 0:
                            copies(n - 1)
                        v.wait_ge(exp_done, 16 * b + 2 * n + 2 + 1)
                        if kind == 0:
                            v.reciprocal(r0[:, a0:a0 + 2], rs[:, a0:a0 + 2])
                            v.drain()
                            v.scalar_tensor_tensor(coef, r0[:, a0 + 1:a0 + 2], neglam, rs[:, a0:a0 + 1], ALU.mult, ALU.mult)
                            v.drain()
                            K = P * (n + 1)
                            p = pr[n % 2]
                            v.scalar_tensor_tensor(p[:, 0, 0:K], p[:, 1, 0:K], coef, p[:, 0, 0:K], ALU.mult, ALU.add)\
                                .then_inc(w_done, 1)
                        else:
                            v.reciprocal(r0[:, a0:a0 + 2], rs[:, a0:a0 + 2]).then_inc(w_done, 1)
                    copies(7)
                    v.tensor_scalar(slope, slope, 0.25, None, ALU.mult)
                    v.drain()
                    biases(kind)
                    if kind == 0:
                        v.wait_ge(sub_root, b + 1)
                        v.reciprocal(ms, ms)
                        v.drain()
                        v.tensor_scalar(ms, ms, 1.0 - LAM_INIT, None, ALU.mult)
                        v.drain()
                        v.tensor_tensor(o_sb, o_sb, ms.rearrange("p (n u) -> p n u", u=1).broadcast_to([P, 8, P]), ALU.mult)
                        v.drain().then_inc(o_ready, 1)
                    if not last:
                        copy_v(b + 1, before(LANE[kind]))
                    v.wait_ge(td_done, before(LANE[kind] + (not last)))
                    dst = yT[:, b, 512:1024] if isinstance(b, int) else yT[:, bass.ds(b, 1), 512:1024].rearrange("p u t -> p (u t)")
                    if kind == 0:
                        v.tensor_scalar(dst, bank(5), sub_g, None, ALU.mult).then_inc(td_free, 1)
                    else:
                        v.tensor_copy(dst, bank(5)).then_inc(td_free, 1)
                    v.drain().then_inc(blk_done, 1)

                v.drain().then_inc(blk_done, 1)
                for kind in range(2):
                    v.wait_ge(tab_full, 32 + 16 * kind)
                    v.memset(slope[:, 0:1], 0.5 if kind else 0.25)
                    v.memset(slope[:, 1:2], 0.25)
                    v.drain()
                    biases(kind)
                    if kind == 0:
                        copy_v(0, 1)
                        with v.Fori(0, 2) as i:
                            for s in range(2):
                                block_(0, 2 * i + s)
                    else:
                        for b in range(4, 8):
                            block_(1, b, b == 7)

            def gated():
                v.wait_ge(st_done, 16 * 4 * PAIRS_IN + 16)
                v.memset(attnT, 0.0)
                v.drain()
                chunk = lambda t: t.rearrange("p (n t) -> p n t", t=P)
                with v.Fori(0, C_HEADS) as h:
                    v.wait_ge(g_w, 32 * h + 32)
                    v.wait_ge(g_zread, 2 * h + 1)
                    v.tensor_scalar(gb, ps[:, 0:1024], bg2[:, :], 0.0, ALU.add, ALU.min).then_inc(g_zread, 1)
                    v.wait_ge(g_qk, 32 * h + 32)
                    v.tensor_scalar(gq, gq, C_DK ** -0.5, None, ALU.mult)
                    v.drain().then_inc(g_x, 1)
                    v.wait_ge(g_sp, h + 1)
                    v.tensor_tensor(gb, gb, gd, ALU.subtract)
                    v.drain()
                    for n in range(8):
                        v.tensor_tensor_scan(gx[:, 0, n * P:(n + 1) * P], ones[:, :], gb[:, n * P:(n + 1) * P], 0.0, ALU.mult, ALU.add)
                    v.drain()
                    v.tensor_copy(gb, gx[:, 0, :]).then_inc(g_b, 1)
                    v.drain()

                    def masked(j):
                        v.drain()
                        v.wait_ge(g_s, 8 * h + j + 1)
                        v.sem_inc(waited, 1)
                        mask = (j - 1) % (LEVELS + 1)
                        for n in range(2):
                            v.copy_predicated(attnT[:, 4 * n:4 * n + 4, :],
                                              masks[:, mask:mask + 1, :].broadcast_to([P, 4, P]),
                                              bank(2 * (j % 2) + n).rearrange("p (n i) -> p n i", i=P)).then_inc(g_pred, 1)

                    v.tensor_tensor(chunk(ke), chunk(gb)[:, :, P - 1:P].broadcast_to([P, 8, P]), chunk(gb), ALU.subtract).then_inc(g_ekd, 1)
                    for lv in range(LEVELS):
                        half4 = lambda t: t.rearrange("p (n u t) -> p n u t", u=2, t=64 >> lv)
                        v.wait_ge(g_f, 7 * h + lv + 1)
                        v.tensor_tensor(half4(gx[:, lv % 2, :])[:, :, 0, :], half4(g_dif[lv % 2])[:, :, 0, :], half4(gk)[:, :, 0, :], ALU.mult)
                        v.tensor_tensor(half4(gx[:, lv % 2, :])[:, :, 1, :], half4(g_dif[lv % 2])[:, :, 1, :], half4(gq)[:, :, 1, :], ALU.mult)
                        v.drain().then_inc(g_x, 1)
                        if lv == 0:
                            v.wait_ge(g_eb, 2 * h + 2)
                            v.tensor_tensor(qe, qe, gq, ALU.mult).then_inc(g_qk_done, 1)
                            v.wait_ge(g_ek, h + 1)
                            v.tensor_tensor(ke, ke, gk, ALU.mult).then_inc(g_qk_done, 1)
                        masked(lv)
                    masked(LEVELS)
                    for n in range(7):
                        v.wait_ge(g_u, 7 * h + n + 1)
                        if n == 0:
                            v.tensor_copy(state, bank(6)[:, 0:C_DV]).then_inc(g_st, 1)
                        else:
                            v.sem_inc(waited, 1)
                            v.drain()
                            v.wait_ge(g_o, 8 * h + n + 1)
                            v.scalar_tensor_tensor(state, state, eblast[:, n:n + 1], bank(6 + n % 2)[:, 0:C_DV],
                                                   ALU.mult, ALU.add).then_inc(g_st, 1)
                    v.drain().then_inc(g_st, 1)
                    v.wait_ge(g_root, h + 1)
                    v.reciprocal(ms, ms)
                    v.drain()
                    for n in range(0, 8, 4):
                        v.tensor_tensor(go[:, n:n + 4, :], go[:, n:n + 4, :],
                                        ms[:, n:n + 4].rearrange("p (n u) -> p n u", u=1).broadcast_to([P, 4, C_DV]), ALU.mult)\
                            .then_inc(g_on, 1)
                    v.wait_ge(g_silu, h + 1)
                    for b in range(2):
                        for n in range(2):
                            v.wait_ge(g_ot, 4 * h + 2 * b + n + 1)
                            dst = yT[:, bass.ds(2 * h + b, 1), n * 512:(n + 1) * 512].rearrange("p u t -> p (u t)")
                            v.scalar_tensor_tensor(dst, bank(2 * b + n), hg[:, b:b + 1], gvr[:, b, n * 512:(n + 1) * 512],
                                                   ALU.mult, ALU.mult).then_inc(g_yt, 1)

            v.memset(mean_w[:, :], 1.0 / D)
            v.memset(ones[:, :], 1.0)
            v.memset(wg2[:, :], 0.0)
            v.memset(eps_c, EPS)
            v.drain().then_inc(setup_done, 1)
            v.wait_ge(s_const, 128)
            v.tensor_copy(masks.rearrange("p l i -> p (l i)"), mask_f)
            for i in range(2):
                v.tensor_tensor_reduce(out=junk[:, 64 * i:64 * i + 64], in0=lamv[:, 128 * i:128 * i + 64], in1=lamv[:, 128 * i + 64:128 * i + 128],
                                       scale=1.0, scalar=0.0, op0=ALU.mult, op1=ALU.add, accum_out=lam2[:, i:i + 1])
            v.drain().then_inc(lam_dot, 1)
            v.wait_ge(lam_exp, 1)
            v.tensor_tensor(neglam, lam2[:, 1:2], lam2[:, 0:1], ALU.subtract)
            v.drain()
            v.tensor_scalar(neglam, neglam, -LAM_INIT, None, ALU.add)
            v.drain().then_inc(lam_dot, 1)
            v.wait_ge(cs_done, 1)
            for g in range(2):
                for k in range(KB):
                    v.wait_ge(ada_big[2 * g + k // 4], 16)
                    if k == 0:
                        v.tensor_scalar(acc_first[:, g, :], ada_first[:, g, k, :], cs[:, k:k + 1], None, ALU.mult)
                    else:
                        v.scalar_tensor_tensor(acc_first[:, g, :], ada_first[:, g, k, :], cs[:, k:k + 1], acc_first[:, g, :],
                                               ALU.mult, ALU.add)
                    v.drain()
            columns(0, 0, 2)
            for k in range(KB + 1):
                if k < KB:
                    xn(0, 0, 0, k)
                if k:
                    h_low(0, 0, 0, k - 1)
            for layer in range(2):
                project(layer, 0)
                low(layer, 0, 1)
                project(layer, 1)
                if layer == 0:
                    attention()
                else:
                    gated()
                for half in range(2):
                    base = USE_OUT[layer] + KB * half
                    low(layer, 1, half, yT[:, :, half * HALF:(half + 1) * HALF])
                    at = hooks(layer, "out", half)
                    run(at, -1)
                    for i in range(PAIRS_OUT):
                        v.wait_ge(unit_used, base + 2 * i + 4)
                        v.tensor_copy((y3, y_out1)[half][:, 2 * i + 1, :], bank(2 * (i % 2) + 1)).then_inc(free1, 1)
                        run(at, i)
                for k in range(KB):
                    if k < 4:
                        xn(layer, 2, 0, 4 + k)
                    h_low(layer, 2, 0, k)
                for half in range(2):
                    base, tiles, d = ffn_base(layer, half), T_FFN[layer] + FB * half, dn_idx(layer, half)

                    def pair(i, j):
                        e = exp_buf[j]
                        v.wait_ge(exp_g, FB * d + i + 1)
                        v.tensor_scalar(e, e, 1.0, None, ALU.add)
                        v.drain()
                        v.reciprocal(e, e)
                        v.drain()
                        v.tensor_tensor(e, bank(2 * j), e, ALU.mult).then_inc(free0, 1)
                        v.drain()
                        v.wait_ge(unit_used, base + 2 * i + 4)
                        dst = act[:, i, :] if isinstance(i, int) else act[:, bass.ds(i, 1), :].rearrange("p u t -> p (u t)")
                        v.tensor_tensor(dst, e, bank(2 * j + 1), ALU.mult).then_inc(free1, 1)

                    at = hooks(layer, "ffn", half)
                    run(at, -1)
                    for i in range(6):
                        pair(i, i % 2)
                        run(at, i)
                    with v.Fori(3, FB // 2) as i:
                        for j in range(2):
                            pair(2 * i + j, j)
                    base += 2 * FB
                    ahead = (layer, half) != (1, 1)
                    nl, nk, nh = (layer, 2, 1) if half == 0 else (1, 0, 0)
                    for u in range(FB):
                        v.wait_ge(ah_done, FB * d + u + 1)
                        v.tensor_tensor(a_lo[:, u % 2, :], act[:, u, :], a_hi[:, u % 2, :].bitcast(f32), ALU.subtract)\
                            .then_inc(al_done, 1)
                        if ahead and u % 2 == 0 and u < 16:
                            xn(nl, nk, nh, u // 2)
                        if ahead and u % 2 and 3 < u < 20:
                            h_low(nl, nk, nh, (u - 5) // 2)
                    v.wait_ge(unit_used, base + FB + 2)
                    for m in range(1, KB, 2):
                        v.tensor_copy(y3[:, m, :], bank(m)).then_inc(dn_ev1, 1)
            sum_squares(1, 3, 1)
            inverse(1, 3, 1)
            scaled(y3)
            update(1, 3, 1, y3)


def kernel(x, c, ada_w, ada_b, norm_g, ev_w_in, ev_lambda, ev_subln_g, ev_w_out, od_w_in, od_w_g2, od_b_g2,
           od_head_g, od_w_out, ffn_w_gate, ffn_w_up, ffn_w_down):
    import concourse.bacc as bacc
    from concourse.bass_utils import run_bass_kernel_spmd

    f = np.float32
    x, c, ada_w, ada_b, norm_g = (np.asarray(t) for t in (x, c, ada_w, ada_b, norm_g))
    ffn = [np.asarray(t) for t in (ffn_w_gate, ffn_w_up, ffn_w_down)]

    def columns_units(w):
        w = np.asarray(w)
        n = w.shape[1] // P
        return w.reshape(KB, P, n, P).transpose(2, 1, 0, 3).reshape(n, P, KB * P)

    pack = np.zeros((PACK_UNITS, P, 1024), f)
    for layer, (w_in, w_out) in enumerate(((ev_w_in, ev_w_out), (od_w_in, od_w_out))):
        w_in = np.asarray(w_in)[0]
        pack[PACK_IN[layer]:PACK_IN[layer] + 24] = columns_units(w_in[:, :3072])
        if layer == 1:
            last = w_in[:, 3072:].reshape(KB, P, C_RANK).transpose(1, 0, 2)
            pack[PACK_IN[1] + 24].reshape(P, KB, P)[:, :, :C_RANK] = last
        pack[PACK_OUT[layer]:PACK_OUT[layer] + KB] = columns_units(np.asarray(w_out)[0])
        at = PACK_FFN[layer]
        pack[at:at + 2 * FB:2] = columns_units(ffn[0][layer])
        pack[at + 1:at + 2 * FB:2] = columns_units(ffn[1][layer])
        pack[at + 2 * FB:at + 3 * FB] = ffn[2][layer].reshape(FB, P, D)

    d = 896.0 + np.arange(P)[:, None] - np.arange(S)[None, :]
    copies = (d <= 128).astype(int) + ((d % 4 == 0) & (d <= 512)) + (d % 16 == 0)
    reach = (d >= 0) & (copies > 0)
    dilated = np.where(reach, np.log(np.maximum(copies, 1)) / SCORE_SCALE, MASKED)
    levels = np.zeros((P, 8, P), f)
    j, i = np.arange(P)[:, None], np.arange(P)[None, :]
    for lv in range(LEVELS):
        m = 64 >> lv
        levels[:, lv] = (j // (2 * m) == i // (2 * m)) & (j % (2 * m) < m) & (i % (2 * m) >= m)
    levels[:, LEVELS] = i == j

    arrays = {
        "xT": x[0].T, "cT": c[0].reshape(KB, P).T, "weights": pack,
        "ada_w": ada_w.reshape(2, KB, P, 6, D).transpose(0, 3, 1, 2, 4).reshape(96, P, D),
        "ada_bT": ada_b.reshape(96, P).T, "norm_gT": norm_g.reshape(64, P).T,
        "lam_p": np.broadcast_to(np.asarray(ev_lambda).reshape(1, 4 * HEAD_DIM), (P, 4 * HEAD_DIM)),
        "subln_g": np.asarray(ev_subln_g).reshape(P, 1),
        "w_g2": np.asarray(od_w_g2)[0].reshape(C_RANK, C_HEADS, P).transpose(1, 0, 2),
        "b_g2": np.asarray(od_b_g2)[0].reshape(C_HEADS, P, 1),
        "head_g": np.asarray(od_head_g)[0].reshape(2, P).T,
        "identity": np.eye(P, dtype=f), "distance": (-d / SCORE_SCALE).astype(f),
        "causal_bias": np.where(d >= 0, 0.0, MASKED).astype(f), "dilated_bias": dilated.astype(f),
        "level_masks": levels,
    }
    arrays = {k: np.ascontiguousarray(a) for k, a in arrays.items()}
    nc = bacc.Bacc("TRN2", target_bir_lowering=False, num_devices=1)
    args = [nc.dram_tensor(k, a.shape, mybir.dt.from_np(a.dtype), kind="ExternalInput").ap() for k, a in arrays.items()]
    args.append(nc.dram_tensor("outT", (D, S), mybir.dt.float32, kind="ExternalOutput").ap())
    trunk_kernel(nc, *args)
    r = run_bass_kernel_spmd(nc, [arrays], core_ids=[0])
    return np.ascontiguousarray(r.results[0]["outT"].T)[None]
```
